# Optimizing a Trainium2 kernel written in Bass

```python
import math
import jax
import jax.numpy as jnp
from jax import lax
import numpy as np
import jax, jax.numpy as jnp

D_MODEL = 2048
BATCH = 1
SEQ = 256
DEPTH = 2

CHUNK = 64
N_META = 16
ROPE_THETA = 500000.0
NORM_EPS = 1e-5
N_A_LAYERS = DEPTH // 2
N_B_LAYERS = DEPTH - N_A_LAYERS

A_HEADS = 8
A_HEAD_DIM = D_MODEL // (2 * A_HEADS)
A_ROT = A_HEAD_DIM // 4
A_QBLOCK = 128

B_HEAD_DIM = 64
B_Q_HEADS = D_MODEL // B_HEAD_DIM
B_KV_HEADS = 4
B_GROUP = B_Q_HEADS // B_KV_HEADS
B_ROT = B_HEAD_DIM // 4
WINDOW = 128
WINDOW_CHUNKS = WINDOW // CHUNK


def rms_norm(x, g):
    xf = x.astype(jnp.float32)
    y = xf * lax.rsqrt(jnp.mean(xf * xf, axis=-1, keepdims=True) + NORM_EPS)
    return (y * g.astype(jnp.float32)).astype(x.dtype)

def chunk_ids(pos):
    return jnp.where(pos < N_META, 0, (pos - N_META) // CHUNK + 1)

def rope_tables(pos, rot):
    inv = ROPE_THETA ** (-jnp.arange(0, rot, 2, dtype=jnp.float32) / rot)
    ang = pos.astype(jnp.float32)[:, None] * inv[None, :]
    return jnp.cos(ang), jnp.sin(ang)

def partial_rope(x, cos, sin):
    half = cos.shape[-1]
    c = cos[None, :, None, :].astype(x.dtype)
    s = sin[None, :, None, :].astype(x.dtype)
    x1 = x[..., :half]
    x2 = x[..., half:2 * half]
    return jnp.concatenate([x1 * c - x2 * s, x2 * c + x1 * s, x[..., 2 * half:]], axis=-1)

def diff_attention(q, k, v, lam, cid):
    L = q.shape[1]
    scale = A_HEAD_DIM ** -0.5
    outs = []
    for s in range(0, L, A_QBLOCK):
        e = min(L, s + A_QBLOCK)
        kend = min(L, e + CHUNK)
        sc = jnp.einsum('bqhd,bkhd->bhqk', q[:, s:e], k[:, :kend]).astype(jnp.float32) * scale
        mask = cid[None, :kend] <= cid[s:e, None]
        sc = jnp.where(mask[None, None], sc, -jnp.inf)
        p = jax.nn.softmax(sc, axis=-1)
        p = p.reshape(p.shape[0], A_HEADS, 2, e - s, kend)
        w = p[:, :, 0] - lam * p[:, :, 1]
        outs.append(jnp.einsum('bhqk,bkhd->bqhd', w.astype(v.dtype), v[:, :kend]))
    return jnp.concatenate(outs, axis=1)

def diff_attn_layer(x, norm_g, w_in, w_out, lq1, lk1, lq2, lk2, subln_g, lambda_init, cos, sin, cid):
    B, L, _ = x.shape
    h = rms_norm(x, norm_g)
    q, k, v, gate = jnp.split(h @ w_in, 4, axis=-1)
    q = partial_rope(q.reshape(B, L, 2 * A_HEADS, A_HEAD_DIM), cos, sin)
    k = partial_rope(k.reshape(B, L, 2 * A_HEADS, A_HEAD_DIM), cos, sin)
    v = v.reshape(B, L, A_HEADS, 2 * A_HEAD_DIM)
    f32 = jnp.float32
    lam = (jnp.exp(jnp.sum(lq1.astype(f32) * lk1.astype(f32)))
           - jnp.exp(jnp.sum(lq2.astype(f32) * lk2.astype(f32))) + lambda_init)
    o = diff_attention(q, k, v, lam, cid)
    o = rms_norm(o, subln_g) * (1.0 - lambda_init)
    o = o.reshape(B, L, D_MODEL) * jax.nn.silu(gate)
    return x + o @ w_out

def shared_kv(x, kv_norm, w_kv, cos, sin):
    B, L, _ = x.shape
    k, v = jnp.split(rms_norm(x, kv_norm) @ w_kv, 2, axis=-1)
    k = partial_rope(k.reshape(B, L, B_KV_HEADS, B_HEAD_DIM), cos, sin)
    v = v.reshape(B, L, B_KV_HEADS, B_HEAD_DIM)
    return k, v

def sink_softmax(sc, sink):
    m = jnp.maximum(jnp.max(sc, axis=-1, keepdims=True), sink)
    e = jnp.exp(sc - m)
    return e / (jnp.sum(e, axis=-1, keepdims=True) + jnp.exp(sink - m))

def swa_sink_attention(q, k, v, sinks):
    B, L = q.shape[:2]
    S = L - N_META
    NC = S // CHUNK
    scale = B_HEAD_DIM ** -0.5
    sink = sinks.astype(jnp.float32).reshape(B_KV_HEADS, B_GROUP)
    qm = q[:, :N_META].reshape(B, N_META, B_KV_HEADS, B_GROUP, B_HEAD_DIM)
    km, vm = k[:, :N_META], v[:, :N_META]
    sm = jnp.einsum('bqkgd,bskd->bkgqs', qm, km).astype(jnp.float32) * scale
    pm = sink_softmax(sm, sink[None, :, :, None, None])
    om = jnp.einsum('bkgqs,bskd->bqkgd', pm.astype(v.dtype), vm).reshape(B, N_META, D_MODEL)
    qr = q[:, N_META:].reshape(B, NC, CHUNK, B_KV_HEADS, B_GROUP, B_HEAD_DIM)
    kr = k[:, N_META:].reshape(B, NC, CHUNK, B_KV_HEADS, B_HEAD_DIM)
    vr = v[:, N_META:].reshape(B, NC, CHUNK, B_KV_HEADS, B_HEAD_DIM)
    pad = ((0, 0), (WINDOW_CHUNKS, 0), (0, 0), (0, 0), (0, 0))
    kp, vp = jnp.pad(kr, pad), jnp.pad(vr, pad)
    kb = jnp.concatenate([kp[:, j:j + NC] for j in range(WINDOW_CHUNKS + 1)], axis=2)
    vb = jnp.concatenate([vp[:, j:j + NC] for j in range(WINDOW_CHUNKS + 1)], axis=2)
    meta_shape = (B, NC, N_META, B_KV_HEADS, B_HEAD_DIM)
    kb = jnp.concatenate([jnp.broadcast_to(km[:, None], meta_shape), kb], axis=2)
    vb = jnp.concatenate([jnp.broadcast_to(vm[:, None], meta_shape), vb], axis=2)
    band_chunk = jnp.arange(NC)[:, None] - WINDOW_CHUNKS + jnp.arange(WINDOW_CHUNKS + 1)[None, :]
    valid = jnp.concatenate([jnp.ones((NC, N_META), dtype=bool),
                             jnp.repeat(band_chunk >= 0, CHUNK, axis=1)], axis=1)
    sr = jnp.einsum('bnqkgd,bnskd->bnkgqs', qr, kb).astype(jnp.float32) * scale
    sr = jnp.where(valid[None, :, None, None, None, :], sr, -jnp.inf)
    pr = sink_softmax(sr, sink[None, None, :, :, None, None])
    orr = jnp.einsum('bnkgqs,bnskd->bnqkgd', pr.astype(v.dtype), vb).reshape(B, S, D_MODEL)
    return jnp.concatenate([om, orr], axis=1)

def swa_layer(x, norm_g, w_in, w_out, sinks, k_sh, v_sh, cos, sin):
    B, L, _ = x.shape
    q, gate = jnp.split(rms_norm(x, norm_g) @ w_in, 2, axis=-1)
    q = partial_rope(q.reshape(B, L, B_Q_HEADS, B_HEAD_DIM), cos, sin)
    o = swa_sink_attention(q, k_sh, v_sh, sinks)
    return x + (o * jax.nn.silu(gate)) @ w_out

def first_inputs(seed: int = 0) -> dict:
    key = jax.random.key(seed)
    ks = jax.random.split(key, 17)
    D = D_MODEL

    def nrm(k, shape, s):
        return jax.random.normal(k, shape, jnp.float32) * s

    return {
        'x': nrm(ks[0], (BATCH, SEQ, D), 1.0),
        'meta_tokens': nrm(ks[1], (N_META, D), 1.0),
        'a_norm': 1.0 + nrm(ks[2], (N_A_LAYERS, D), 0.02),
        'a_w_in': nrm(ks[3], (N_A_LAYERS, D, 4 * D), D ** -0.5),
        'a_w_out': nrm(ks[4], (N_A_LAYERS, D, D), D ** -0.5),
        'a_lambda_q1': nrm(ks[5], (N_A_LAYERS, A_HEAD_DIM), 0.1),
        'a_lambda_k1': nrm(ks[6], (N_A_LAYERS, A_HEAD_DIM), 0.1),
        'a_lambda_q2': nrm(ks[7], (N_A_LAYERS, A_HEAD_DIM), 0.1),
        'a_lambda_k2': nrm(ks[8], (N_A_LAYERS, A_HEAD_DIM), 0.1),
        'a_subln': 1.0 + nrm(ks[9], (N_A_LAYERS, 2 * A_HEAD_DIM), 0.02),
        'kv_norm': 1.0 + nrm(ks[10], (D,), 0.02),
        'w_kv': nrm(ks[11], (D, 2 * B_KV_HEADS * B_HEAD_DIM), D ** -0.5),
        'b_norm': 1.0 + nrm(ks[12], (N_B_LAYERS, D), 0.02),
        'b_w_in': nrm(ks[13], (N_B_LAYERS, D, 2 * D), D ** -0.5),
        'b_w_out': nrm(ks[14], (N_B_LAYERS, D, D), D ** -0.5),
        'b_sinks': nrm(ks[15], (N_B_LAYERS, B_Q_HEADS), 0.5),
        'final_norm': 1.0 + nrm(ks[16], (D,), 0.02),
    }

def first_block(x, meta_tokens, a_norm, a_w_in, a_w_out, a_lambda_q1, a_lambda_k1, a_lambda_q2,
              a_lambda_k2, a_subln, kv_norm, w_kv, b_norm, b_w_in, b_w_out, b_sinks, final_norm):
    B = x.shape[0]
    meta = jnp.broadcast_to(meta_tokens.astype(x.dtype)[None], (B, N_META, D_MODEL))
    h = jnp.concatenate([meta, x], axis=1)
    L = h.shape[1]
    pos = jnp.arange(L, dtype=jnp.int32)
    cid = chunk_ids(pos)
    cos_a, sin_a = rope_tables(pos, A_ROT)
    cos_b, sin_b = rope_tables(pos, B_ROT)
    k_sh = v_sh = None
    for i in range(DEPTH):
        if i < N_A_LAYERS:
            lambda_init = 0.8 - 0.6 * math.exp(-0.3 * i)
            h = diff_attn_layer(h, a_norm[i], a_w_in[i], a_w_out[i], a_lambda_q1[i], a_lambda_k1[i],
                                a_lambda_q2[i], a_lambda_k2[i], a_subln[i], lambda_init,
                                cos_a, sin_a, cid)
        else:
            if i == N_A_LAYERS:
                k_sh, v_sh = shared_kv(h, kv_norm, w_kv, cos_b, sin_b)
            j = i - N_A_LAYERS
            h = swa_layer(h, b_norm[j], b_w_in[j], b_w_out[j], b_sinks[j], k_sh, v_sh, cos_b, sin_b)
    return rms_norm(h, final_norm)[:, N_META:]


DEPTH_2 = 1

Q_BLOCK = 128
SB_HEAD_DIM = 128
SB_WIDTH = D_MODEL // 4
SB_HEADS = SB_WIDTH // SB_HEAD_DIM
FOX_HEAD_DIM = 128
FOX_WIDTH = D_MODEL // 4
FOX_HEADS = FOX_WIDTH // FOX_HEAD_DIM
RWKV_HEAD_DIM = 64
RWKV_WIDTH = D_MODEL // 2
RWKV_HEADS = RWKV_WIDTH // RWKV_HEAD_DIM
DECAY_LORA = 64
AAA_LORA = 64
GATE_LORA = 160
RWKV_IN = 3 * RWKV_WIDTH + DECAY_LORA + AAA_LORA + GATE_LORA
N_BRANCHES = 3
N_IN = 3 * SB_WIDTH + 3 * FOX_WIDTH + FOX_HEADS + RWKV_IN + N_BRANCHES * D_MODEL
D_FF = 4 * D_MODEL
RMS_EPS = 1e-6
RWKV_GN_EPS = 64e-5


def _split(x, sizes):
    points = np.cumsum(sizes)[:-1].tolist()
    return jnp.split(x, points, axis=-1)

def _rms_norm(x, gain):
    xf = x.astype(jnp.float32)
    y = xf * lax.rsqrt(jnp.mean(xf * xf, axis=-1, keepdims=True) + RMS_EPS)
    return (y * gain.astype(jnp.float32)).astype(x.dtype)

def _heads(x, n_heads):
    b, s, _ = x.shape
    return x.reshape(b, s, n_heads, -1).transpose(0, 2, 1, 3)

def _merge_heads(x):
    b, h, s, d = x.shape
    return x.transpose(0, 2, 1, 3).reshape(b, s, h * d)

def _query_blocks(x):
    b, h, s = x.shape[:3]
    x = x.reshape((b, h, s // Q_BLOCK, Q_BLOCK) + x.shape[3:])
    return jnp.moveaxis(x, 2, 0)

def _unblock(o):
    nb, b, h, qb, d = o.shape
    return o.transpose(1, 2, 0, 3, 4).reshape(b, h, nb * qb, d)

def stick_breaking_attention(q, k, v):
    s, d = q.shape[2], q.shape[3]
    scale = d ** -0.5
    kpos = jnp.arange(s)

    def block(args):
        qb, start = args
        z = jnp.einsum('bhqd,bhkd->bhqk', qb, k).astype(jnp.float32) * scale
        qpos = start + jnp.arange(Q_BLOCK)
        strict = kpos[None, :] < qpos[:, None]
        log_beta = jax.nn.log_sigmoid(z)
        log_rest = jnp.where(strict, jax.nn.log_sigmoid(-z), 0.0)
        between = lax.cumsum(log_rest, axis=3, reverse=True) - log_rest
        a = jnp.where(strict, jnp.exp(log_beta + between), 0.0)
        return jnp.einsum('bhqk,bhkd->bhqd', a.astype(v.dtype), v)

    starts = jnp.arange(s // Q_BLOCK, dtype=jnp.int32) * Q_BLOCK
    return _unblock(lax.map(block, (_query_blocks(q), starts)))

def forgetting_attention(q, k, v, log_f):
    s, d = q.shape[2], q.shape[3]
    scale = d ** -0.5
    kpos = jnp.arange(s)
    c = lax.cumsum(log_f.astype(jnp.float32), axis=2)

    def block(args):
        qb, cb, start = args
        z = jnp.einsum('bhqd,bhkd->bhqk', qb, k).astype(jnp.float32) * scale
        z = z + (cb[..., :, None] - c[..., None, :])
        qpos = start + jnp.arange(Q_BLOCK)
        causal = kpos[None, :] <= qpos[:, None]
        p = jax.nn.softmax(jnp.where(causal, z, -jnp.inf), axis=-1)
        return jnp.einsum('bhqk,bhkd->bhqd', p.astype(v.dtype), v)

    starts = jnp.arange(s // Q_BLOCK, dtype=jnp.int32) * Q_BLOCK
    return _unblock(lax.map(block, (_query_blocks(q), _query_blocks(c), starts)))

def rwkv7_time_mix(z, mu, w0, w_up, a0, a_up, g_up, k_k, k_a, r_k, ln_w, ln_b):
    b, s, _ = z.shape
    h, n = RWKV_HEADS, RWKV_HEAD_DIM
    z_prev = jnp.pad(z[:, :-1], ((0, 0), (1, 0), (0, 0)))
    z = z + (z_prev - z) * mu
    r, k, v, wd, ad, gd = _split(z, (RWKV_WIDTH,) * 3 + (DECAY_LORA, AAA_LORA, GATE_LORA))
    w_log = -jax.nn.softplus(-(w0 + jnp.tanh(wd) @ w_up)) - 0.5
    a = jax.nn.sigmoid(a0 + ad @ a_up)
    g = jax.nn.sigmoid(gd) @ g_up
    kk_raw = k * k_k
    k = k * (1 + (a - 1) * k_a)

    def per_head(t):
        return t.reshape(b, s, h, n).astype(jnp.float32)

    r_h, k_h, v_h, a_h, kk = map(per_head, (r, k, v, a, kk_raw))
    kk = kk / jnp.maximum(jnp.sqrt(jnp.sum(kk * kk, axis=-1, keepdims=True)), 1e-12)
    decay = jnp.exp(-jnp.exp(per_head(w_log)))

    def time_major(t):
        return t.transpose(1, 0, 2, 3).reshape(s // CHUNK, CHUNK, b, h, n)

    inputs = tuple(time_major(t) for t in (r_h, decay, k_h, v_h, kk, kk * a_h))

    def frame(state, inp):
        r_t, w_t, k_t, v_t, kk_t, kka_t = inp
        sa = jnp.einsum('bhvk,bhk->bhv', state, kk_t)
        state = (state * w_t[:, :, None, :] - sa[..., None] * kka_t[:, :, None, :]
                 + v_t[..., None] * k_t[:, :, None, :])
        return state, jnp.einsum('bhvk,bhk->bhv', state, r_t)

    def chunk(state, inp):
        return lax.scan(frame, state, inp)

    _, y = lax.scan(chunk, jnp.zeros((b, h, n, n), jnp.float32), inputs)
    y = y.reshape(s, b, h, n).transpose(1, 0, 2, 3)
    mean = jnp.mean(y, axis=-1, keepdims=True)
    var = jnp.mean(jnp.square(y - mean), axis=-1, keepdims=True)
    y = ((y - mean) * lax.rsqrt(var + RWKV_GN_EPS) * ln_w.astype(jnp.float32).reshape(h, n)
         + ln_b.astype(jnp.float32).reshape(h, n))
    y = y + jnp.sum(r_h * k_h * r_k.astype(jnp.float32), axis=-1, keepdims=True) * v_h
    return y.reshape(b, s, RWKV_WIDTH).astype(z.dtype) * g

def hybrid_mixer(u, w_in, b_forget, rwkv_mu, rwkv_w0, rwkv_w_up, rwkv_a0, rwkv_a_up, rwkv_g_up,
                 rwkv_k_k, rwkv_k_a, rwkv_r_k, rwkv_ln_w, rwkv_ln_b,
                 w_branch_a, w_branch_b, w_branch_c, w_out):
    proj = u @ w_in
    sb, fox, rw, gates = _split(proj, (3 * SB_WIDTH, 3 * FOX_WIDTH + FOX_HEADS, RWKV_IN,
                                       N_BRANCHES * D_MODEL))
    q_a, k_a, v_a = _split(sb, (SB_WIDTH,) * 3)
    y_a = _merge_heads(stick_breaking_attention(_heads(q_a, SB_HEADS), _heads(k_a, SB_HEADS),
                                                _heads(v_a, SB_HEADS)))
    q_b, k_b, v_b, f_b = _split(fox, (FOX_WIDTH,) * 3 + (FOX_HEADS,))
    log_f = jax.nn.log_sigmoid((f_b + b_forget).astype(jnp.float32)).transpose(0, 2, 1)
    y_b = _merge_heads(forgetting_attention(_heads(q_b, FOX_HEADS), _heads(k_b, FOX_HEADS),
                                            _heads(v_b, FOX_HEADS), log_f))
    y_c = rwkv7_time_mix(rw, rwkv_mu, rwkv_w0, rwkv_w_up, rwkv_a0, rwkv_a_up, rwkv_g_up,
                         rwkv_k_k, rwkv_k_a, rwkv_r_k, rwkv_ln_w, rwkv_ln_b)
    g_a, g_b, g_c = _split(jax.nn.sigmoid(gates), (D_MODEL,) * 3)
    m = g_a * (y_a @ w_branch_a) + g_b * (y_b @ w_branch_b) + g_c * (y_c @ w_branch_c)
    return m @ w_out

def second_inputs(seed: int = 0) -> dict:
    key = jax.random.key(seed)
    ks = jax.random.split(key, 24)
    L, D = DEPTH_2, D_MODEL

    def nrm(k, shape, scale):
        return jax.random.normal(k, shape, jnp.float32) * scale

    return {
        'x': nrm(ks[0], (BATCH, SEQ, D), 1.0),
        'norm_mix_pre': 1.0 + nrm(ks[1], (L, D), 0.05),
        'norm_mix_post': 1.0 + nrm(ks[2], (L, D), 0.05),
        'norm_mlp_pre': 1.0 + nrm(ks[3], (L, D), 0.05),
        'norm_mlp_post': 1.0 + nrm(ks[4], (L, D), 0.05),
        'w_in': nrm(ks[5], (L, D, N_IN), D ** -0.5),
        'b_forget': 1.0 + nrm(ks[6], (L, FOX_HEADS), 0.5),
        'rwkv_mu': jax.random.uniform(ks[7], (L, RWKV_IN), jnp.float32),
        'rwkv_w0': nrm(ks[8], (L, RWKV_WIDTH), 0.5),
        'rwkv_w_up': nrm(ks[9], (L, DECAY_LORA, RWKV_WIDTH), 0.5 * DECAY_LORA ** -0.5),
        'rwkv_a0': nrm(ks[10], (L, RWKV_WIDTH), 0.1),
        'rwkv_a_up': nrm(ks[11], (L, AAA_LORA, RWKV_WIDTH), 0.5 * AAA_LORA ** -0.5),
        'rwkv_g_up': nrm(ks[12], (L, GATE_LORA, RWKV_WIDTH), GATE_LORA ** -0.5),
        'rwkv_k_k': 0.85 + nrm(ks[13], (L, RWKV_WIDTH), 0.05),
        'rwkv_k_a': 1.0 + nrm(ks[14], (L, RWKV_WIDTH), 0.05),
        'rwkv_r_k': nrm(ks[15], (L, RWKV_HEADS, RWKV_HEAD_DIM), 0.1),
        'rwkv_ln_w': 1.0 + nrm(ks[16], (L, RWKV_WIDTH), 0.05),
        'rwkv_ln_b': nrm(ks[17], (L, RWKV_WIDTH), 0.01),
        'w_branch_a': nrm(ks[18], (L, SB_WIDTH, D), SB_WIDTH ** -0.5),
        'w_branch_b': nrm(ks[19], (L, FOX_WIDTH, D), FOX_WIDTH ** -0.5),
        'w_branch_c': nrm(ks[20], (L, RWKV_WIDTH, D), RWKV_WIDTH ** -0.5),
        'w_out': nrm(ks[21], (L, D, D), D ** -0.5),
        'w_mlp_up': nrm(ks[22], (L, D, D_FF), D ** -0.5),
        'w_mlp_down': nrm(ks[23], (L, D_FF, D), D_FF ** -0.5),
    }

def second_block(x, norm_mix_pre, norm_mix_post, norm_mlp_pre, norm_mlp_post, w_in, b_forget,
              rwkv_mu, rwkv_w0, rwkv_w_up, rwkv_a0, rwkv_a_up, rwkv_g_up, rwkv_k_k, rwkv_k_a,
              rwkv_r_k, rwkv_ln_w, rwkv_ln_b, w_branch_a, w_branch_b, w_branch_c, w_out,
              w_mlp_up, w_mlp_down):
    for l in range(DEPTH_2):
        u = _rms_norm(x, norm_mix_pre[l])
        mix = hybrid_mixer(u, w_in[l], b_forget[l], rwkv_mu[l], rwkv_w0[l], rwkv_w_up[l],
                           rwkv_a0[l], rwkv_a_up[l], rwkv_g_up[l], rwkv_k_k[l], rwkv_k_a[l],
                           rwkv_r_k[l], rwkv_ln_w[l], rwkv_ln_b[l], w_branch_a[l], w_branch_b[l],
                           w_branch_c[l], w_out[l])
        x = x + _rms_norm(mix, norm_mix_post[l])
        hdn = jnp.square(jax.nn.relu(_rms_norm(x, norm_mlp_pre[l]) @ w_mlp_up[l]))
        x = x + _rms_norm(hdn @ w_mlp_down[l], norm_mlp_post[l])
    return x


def setup_inputs(seed=0):
    out = dict(first_inputs(seed))
    for name, value in second_inputs(seed + 1).items():
        if name != "x":
            out[name + "_2"] = value
    return out


def reference(
    x, meta_tokens, a_norm, a_w_in, a_w_out, a_lambda_q1, a_lambda_k1, a_lambda_q2, a_lambda_k2,
    a_subln, kv_norm, w_kv, b_norm, b_w_in, b_w_out, b_sinks, final_norm, norm_mix_pre_2,
    norm_mix_post_2, norm_mlp_pre_2, norm_mlp_post_2, w_in_2, b_forget_2, rwkv_mu_2, rwkv_w0_2,
    rwkv_w_up_2, rwkv_a0_2, rwkv_a_up_2, rwkv_g_up_2, rwkv_k_k_2, rwkv_k_a_2, rwkv_r_k_2,
    rwkv_ln_w_2, rwkv_ln_b_2, w_branch_a_2, w_branch_b_2, w_branch_c_2, w_out_2, w_mlp_up_2,
    w_mlp_down_2,
):
    x = first_block(
        x, meta_tokens, a_norm, a_w_in, a_w_out, a_lambda_q1, a_lambda_k1, a_lambda_q2,
        a_lambda_k2, a_subln, kv_norm, w_kv, b_norm, b_w_in, b_w_out, b_sinks, final_norm,
    )
    return second_block(
        x, norm_mix_pre_2, norm_mix_post_2, norm_mlp_pre_2, norm_mlp_post_2, w_in_2, b_forget_2,
        rwkv_mu_2, rwkv_w0_2, rwkv_w_up_2, rwkv_a0_2, rwkv_a_up_2, rwkv_g_up_2, rwkv_k_k_2,
        rwkv_k_a_2, rwkv_r_k_2, rwkv_ln_w_2, rwkv_ln_b_2, w_branch_a_2, w_branch_b_2,
        w_branch_c_2, w_out_2, w_mlp_up_2, w_mlp_down_2,
    )


_drawn_inputs = setup_inputs


def setup_inputs(seed=0):
    import zlib

    import numpy as np

    out = dict(_drawn_inputs(seed))
    spreads = {}
    factors = {'a_lambda_k2': 3.162,
     'a_subln': 4.431,
     'kv_norm': 8.0,
     'b_norm': 8.0,
     'b_sinks': 8.0,
     'rwkv_k_k_2': 51.884,
     'rwkv_ln_w_2': 2.737,
     'rwkv_ln_b_2': 25.241}
    for name, (base, spread) in spreads.items():
        noise = np.random.default_rng([zlib.crc32(name.encode()), seed]).standard_normal(out[name].shape)
        drawn = base * np.exp(spread * noise) if base else spread * noise
        out[name] = jnp.asarray(drawn.astype(out[name].dtype))
    for name, factor in factors.items():
        out[name] = (out[name] * factor).astype(out[name].dtype)
    return out
```

```python
from contextlib import ExitStack

import concourse.bass as bass
import numpy as np
from concourse import mybir

ALU = mybir.AluOpType
ACT = mybir.ActivationFunctionType
F32 = mybir.dt.float32
AX = mybir.AxisListType

D = 2048
SEQ = 256
META = 16
NT = SEQ + META
KT = D // 128
CHUNK = 64
UNIT = 16 * 256
RING = 4
NEG = -1e30
HEADS_A = 8
GROUPS_B = 4
SB_HEADS = 4
RW_TILES = 8
FF_TILES = 64
ROPE_THETA = 500000.0
SCALE_A = 128 ** -0.5
SCALE_B = 64 ** -0.5
SCALE_Z = 128 ** -0.5
LAMBDA_INIT = 0.8 - 0.6
DECAY = float(np.exp(-0.5))
IN_R = 3076

UNITS = [("a", 4 * HEADS_A), ("a_out", 8), ("kv", 2), ("b", 4 * GROUPS_B), ("b_out", 8), ("rw", 12),
         ("small", 3), ("zp", 12), ("mix", 32), ("mix_out", 8), ("up", 32), ("down", 32)]
FIRST_UNIT = {}
for _name, _n in UNITS:
    FIRST_UNIT[_name] = sum(n for _, n in UNITS[:len(FIRST_UNIT)])
N_UNITS = sum(n for _, n in UNITS)


def columns(sizes):
    at, n = {}, 0
    for name, size in sizes:
        at[name] = (n, n + size)
        n += size
    return at, n


P_AT, P_N = columns([(g, KT) for g in ("a", "kv", "b", "fin", "mix_pre", "mix_post", "mlp_pre", "mlp_post")]
                    + [("lam", 4), ("subln", 2), ("sinks", 32), ("mu_wa", 1), ("mu_g", 2), ("bf", 1),
                       ("rw", 10 * RW_TILES)])
MU_R, MU_K, MU_V, W0, A0, K_K, K_A, R_K, LN_W, LN_B = range(10)
LEVELS = (1, 2, 4, 8, 16, 32)
C_AT, C_N = columns([("ident", 128), ("ones", 128), ("hones", 128), ("tri", 128), ("after", 128),
                     ("not_after", 128), ("future", 128), ("strict", 128), ("incl", 128), ("lev1t", 128)]
                    + [(f"lev{b}", 128) for b in LEVELS]
                    + [("reset", 256), ("cos_a", NT), ("sin_a", NT), ("cos_b", NT), ("sin_b", NT),
                       ("low", 128), ("high", 128), ("neg", 64), ("sel", 4 * 128)])


class Steps:

    def __init__(self, sem, names):
        self.sem, self.per = sem, len(names)
        self.at_ = {n: k + 1 for k, n in enumerate(names)}
        assert len(self.at_) == self.per
        self.now = 0

    def step(self, name):
        self.now += 1
        if self.at_[name] != self.now:
            raise ValueError(f"step {name} out of order, at {self.now}")
        self.now %= self.per
        return 1

    def at(self, name, i=0):
        return self.at_[name] + self.per * i


def ran(i):
    return not isinstance(i, int) or i >= 0


def repeat(eng, n, body):
    body(0)
    if n > 1:
        with eng.Fori(1, n) as i:
            body(i)


def build(nc, w, x, params, consts, out):
    with ExitStack() as ctx:
        def sb(name, shape):
            return ctx.enter_context(nc.sbuf_tensor(name, shape, F32))

        def sem(name):
            return ctx.enter_context(nc.semaphore(name))

        ring = sb("ring", [128, RING, 16, 256])
        C = sb("C", [128, C_N])
        P = sb("P", [128, P_N])
        xT = sb("xT", [128, KT, NT])
        hT = sb("hT", [128, KT, NT])
        og = sb("og", [128, KT, NT])
        st = sb("st", [128, 64])
        eps = sb("eps", [128, 4])
        ARENA = nc.sbuf_bytes_remaining // 4 - 8
        arena = sb("arena", [128, ARENA])
        ps = ctx.enter_context(nc.psum_tensor("ps", [128, 8, 512], F32))

        def c(name, rows=128):
            a, b = C_AT[name]
            return C[0:rows, a:b]

        def p(name, k=0, rows=128):
            return P[0:rows, P_AT[name][0] + k:P_AT[name][0] + k + 1]

        def carve(sizes):
            got, at = {}, 0
            for name, *shape in sizes:
                n = int(np.prod(shape))
                v = arena[:, at:at + n]
                if len(shape) == 2:
                    v = v.rearrange("p (a b) -> p a b", a=shape[0])
                got[name] = v
                at += n
            if at > ARENA:
                raise ValueError(f"arena: {at} of {ARENA}")
            return got

        unit_in = [sem(f"unit_in{s}") for s in range(RING)]
        half_done = sem("half_done")
        x_in, cp_in, out_in = sem("x_in"), sem("cp_in"), sem("out_in")
        eps_set = sem("eps_set")

        def phase(name, **steps):
            return {e: Steps(sem(f"{name}_{e}"), s.split()) for e, s in steps.items()}

        def loaded(phase_name, u, i=0, per=0):
            return 16 * ((FIRST_UNIT[phase_name] + u) // RING + 1) + 16 * (per // RING) * i

        def halves(phase_name, u, half, i=0, per=0):
            return 2 * (FIRST_UNIT[phase_name] + u) + half + 1 + 2 * per * i

        def half(slot, h, acc, rhs, n, k0=0, kts=range(16), first=True, last=True, m=128):
            for kt in kts:
                ins = nc.tensor.matmul(acc[0:m, 0:n], ring[:, slot, kt, 128 * h:128 * h + m],
                                       rhs[:, k0 + kt, 0:n],
                                       start=(first and kt == kts[0]), stop=(last and kt == kts[-1]))
            return ins

        def mm(o, lhsT, rhs, start=True, stop=True):
            return nc.tensor.matmul(o, lhsT, rhs, start=start, stop=stop)

        class Norm:

            def __init__(self, name, src, n, eps_col, outs, residual=None):
                self.src, self.n, self.eps_col, self.outs, self.residual = src, n, eps_col, outs, residual
                s = phase(name, a="sq0 sq1 sq2 sq3 root", t="s0 s1 s2 s3",
                          v="var rstd " + " ".join(f"o{k}_{kt}" for k in range(len(outs)) for kt in range(KT))
                          + (" " + " ".join(f"r{kt}" for kt in range(KT)) if residual is not None else ""))
                self.A, self.T, self.V = s["a"], s["t"], s["v"]
                a = carve([("low", ARENA - 9 * NT), ("sq", 2, 4 * NT), ("rstd", NT)])
                self.rstd = a["rstd"][:, 0:n]
                self.sq = [a["sq"][:, k, :].rearrange("p (a b) -> p a b", a=4)[:, :, 0:n] for k in range(2)]
                self.last = f"r{KT - 1}" if residual is not None else f"o{len(outs) - 1}_{KT - 1}"

            def act(self, eng):
                for k in range(4):
                    if k >= 2:
                        eng.wait_ge(self.T.sem, self.T.at(f"s{k - 2}"))
                    nc.scalar.activation(self.sq[k % 2], self.src[:, 4 * k:4 * k + 4, 0:self.n],
                                                     ACT.Square)\
                        .then_inc(self.A.sem, self.A.step(f"sq{k}"))
                eng.wait_ge(self.V.sem, self.V.at("var"))
                nc.scalar.activation(self.rstd, self.rstd, ACT.Sqrt)\
                    .then_inc(self.A.sem, self.A.step("root"))

            def pe(self, eng):
                for k in range(4):
                    eng.wait_ge(self.A.sem, self.A.at(f"sq{k}"))
                    for j in range(4):
                        ins = mm(ps[:, 7, 0:self.n], c("ones"), self.sq[k % 2][:, j, :],
                                 start=(k == 0 and j == 0), stop=(k == 3 and j == 3))
                    ins\
                        .then_inc(self.T.sem, self.T.step(f"s{k}"))

            def dve(self, eng):
                n, V = self.n, self.V
                eng.wait_ge(self.T.sem, self.T.at("s3"))
                nc.vector.tensor_scalar(self.rstd, ps[:, 7, 0:n], 1.0 / D,
                                               eps[:, self.eps_col:self.eps_col + 1], ALU.mult, ALU.add)\
                    .then_inc(V.sem, V.step("var"))
                eng.wait_ge(self.A.sem, self.A.at("root"))
                nc.vector.reciprocal(self.rstd, self.rstd)\
                    .then_inc(V.sem, V.step("rstd"))
                eng.wait_ge(V.sem, V.at("rstd"))
                for k, (gain, dst) in enumerate(self.outs):
                    for kt in range(KT):
                        nc.vector.scalar_tensor_tensor(
                            out=dst[:, kt, 0:n], in0=self.src[:, kt, 0:n], scalar=p(gain, kt), in1=self.rstd,
                            op0=ALU.mult, op1=ALU.mult)\
                            .then_inc(V.sem, V.step(f"o{k}_{kt}"))
                if self.residual is not None:
                    for kt in range(KT):
                        eng.wait_ge(V.sem, V.at(f"o0_{kt}"))
                        x = self.residual[:, kt, 0:n]
                        nc.vector.tensor_tensor(x, x, self.outs[0][1][:, kt, 0:n], ALU.add)\
                            .then_inc(V.sem, V.step(f"r{kt}"))

        class Product:
            def __init__(self, name, units, rhs, n, dst, add):
                self.units, self.rhs, self.n, self.dst, self.add = units, rhs, n, dst, add
                self.V = phase(name, v=" ".join(f"t{t}" for t in range(8)))["v"]

            def pe(self, eng):
                def body(i):
                    for u in range(4):
                        slot = (FIRST_UNIT[self.units] + u) % RING
                        eng.wait_ge(unit_in[slot], loaded(self.units, u, i, 4))
                        for h in range(2):
                            t = 2 * u + h
                            if ran(i if t >= 4 else i - 1):
                                eng.wait_ge(self.V.sem, self.V.at(f"t{(t - 4) % 8}", i if t >= 4 else i - 1))
                            half(slot, h, ps[:, t % 4, :], self.rhs, self.n).then_inc(half_done, 1)
                repeat(eng, 2, body)

            def dve(self, eng):
                def body(i):
                    for t in range(8):
                        eng.wait_ge(half_done, halves(self.units, t // 2, t % 2, i, 4))
                        o = self.dst[:, bass.ds(8 * i + t, 1), 0:self.n]
                        acc = ps[:, t % 4:t % 4 + 1, 0:self.n]
                        if self.add:
                            nc.vector.tensor_tensor(o, acc, o, ALU.add)\
                                .then_inc(self.V.sem, self.V.step(f"t{t}"))
                        else:
                            nc.vector.tensor_copy(o, acc)\
                                .then_inc(self.V.sem, self.V.step(f"t{t}"))
                repeat(eng, 2, body)

        norm_a = Norm("norm_a", xT, NT, 0, [("a", hT)])
        SA = phase("attn_a",
                   a="qk0 qk1 qk2 qk3 v0 v1 e0 e1 e2 e3 e4 e5 g0 g1 wT sqo root",
                   t="scores vt wt pv osum",
                   v="rcos shuf rsin radd mx0 mx1 mxm nb v vm rr rl n0 w0 n1 w1 nm wm wTm var rstd o0 o1 og0 og1")
        fa = carve([("qk", 4, NT), ("sh", 4, NT), ("xc", 4, NT), ("vT", 2, NT), ("v", 3, 256), ("ga", 2, NT), ("p0", 2, 144),
                    ("p1", 2, NT), ("pm", 2, META), ("wT", 384), ("wTm", NT), ("sqo", 2, NT), ("rstd", NT),
                    ("o", 2, NT)])
        A_MX, A_NB, A_RS, A_RR = 0, 6, 12, 18
        LAM = 24
        lam_steps = phase("lam", v="prod1 prod2 diff neg", t="sum", a="exp")

        def lam_pe(pe):
            pe.wait_ge(lam_steps["v"].sem, lam_steps["v"].at("prod2"))
            mm(ps[:, 6, 0:2], c("ones"), st[:, LAM + 1:LAM + 3])\
                .then_inc(lam_steps["t"].sem, lam_steps["t"].step("sum"))

        def lam_act(act):
            act.wait_ge(lam_steps["t"].sem, lam_steps["t"].at("sum"))
            nc.scalar.activation(st[:, LAM + 3:LAM + 5], ps[:, 6, 0:2], ACT.Exp)\
                .then_inc(lam_steps["a"].sem, lam_steps["a"].step("exp"))

        def lam_dve(dve):
            V = lam_steps["v"]
            for k in range(2):
                nc.vector.tensor_tensor(st[:, LAM + 1 + k:LAM + 2 + k], p("lam", 2 * k), p("lam", 2 * k + 1),
                                               ALU.mult)\
                    .then_inc(V.sem, V.step(f"prod{k + 1}"))
            dve.wait_ge(lam_steps["a"].sem, lam_steps["a"].at("exp"))
            nc.vector.tensor_tensor(st[:, LAM:LAM + 1], st[:, LAM + 4:LAM + 5], st[:, LAM + 3:LAM + 4],
                                           ALU.subtract)\
                .then_inc(V.sem, V.step("diff"))
            dve.wait_ge(V.sem, V.at("diff"))
            nc.vector.tensor_scalar(st[:, LAM:LAM + 1], st[:, LAM:LAM + 1], -LAMBDA_INIT, None, ALU.add)\
                .then_inc(V.sem, V.step("neg"))

        def attn_a_pe(pe):
            A, T, V = SA["a"], SA["t"], SA["v"]
            qk, v, p0, p1, pm = fa["qk"], fa["v"], fa["p0"], fa["p1"], fa["pm"]
            pe.wait_ge(norm_a.V.sem, norm_a.V.at(norm_a.last))

            def body(i):
                for t in range(6):
                    if t % 2 == 0:
                        slot = (FIRST_UNIT["a"] + t // 2) % RING
                        pe.wait_ge(unit_in[slot], loaded("a", t // 2, i, 4))
                    if t == 0:
                        if ran(i - 1):
                            pe.wait_ge(V.sem, V.at("vm", i - 1))
                    elif t == 1:
                        if ran(i - 1):
                            pe.wait_ge(A.sem, A.at("v1", i - 1))
                    elif t < 4:
                        if ran(i - 1):
                            pe.wait_ge(A.sem, A.at(f"g{t - 2}", i - 1))
                    else:
                        pe.wait_ge(A.sem, A.at(f"qk{t - 4}", i))
                    half(slot, t % 2, ps[:, t % 4, :], hT, NT).then_inc(half_done, 1)
                pe.wait_ge(V.sem, V.at("radd", i))
                if ran(i - 1):
                    pe.wait_ge(A.sem, A.at("wT", i - 1))
                if ran(i - 1):
                    pe.wait_ge(V.sem, V.at("var", i - 1))
                if ran(i - 1):
                    pe.wait_ge(V.sem, V.at("o1", i - 1))
                for a in range(2):
                    k = qk[:, 2 + a, :]
                    q = qk[:, a, :]
                    o = ps[:, 4, 144 * a:144 * a + 144]
                    mm(o[:, 128:144], q[:, 0:128], k[:, 256:NT])
                    mm(o[:, 0:128], q[:, 0:128], k[:, 0:128], stop=False)
                    mm(o[:, 64:128], c("low", 1), c("neg", 1), start=False)
                    o = ps[:, 5 + a, :]
                    mm(o[:, 0:NT], q[:, 128:256], k, stop=False)
                    mm(o[:, 192:256], c("low", 1), c("neg", 1), start=False)
                    ins = mm(ps[0:META, 4, 288 + META * a:288 + META * (a + 1)], q[:, 256:NT], k[:, 256:NT])
                ins\
                    .then_inc(T.sem, T.step("scores"))
                pe.wait_ge(A.sem, A.at("v1", i))
                if ran(i - 1):
                    pe.wait_ge(V.sem, V.at("o1", i - 1))
                for tok in range(2):
                    for d in range(2):
                        nc.tensor.transpose(ps[:, 7, 256 * tok + 128 * d:256 * tok + 128 * d + 128],
                                            fa["vT"][:, d, 128 * tok:128 * tok + 128], c("ident"))
                for d in range(2):
                    ins = nc.tensor.transpose(ps[0:META, 0, 128 * d:128 * d + 128], fa["vT"][:, d, 256:NT], c("ident"))
                ins\
                    .then_inc(T.sem, T.step("vt"))
                slot = (FIRST_UNIT["a"] + 3) % RING
                pe.wait_ge(unit_in[slot], loaded("a", 3, i, 4))
                for t in (6, 7):
                    pe.wait_ge(A.sem, A.at(f"qk{t - 4}", i))
                    half(slot, t % 2, ps[:, t % 4, :], hT, NT).then_inc(half_done, 1)
                pe.wait_ge(V.sem, V.at("wm", i))
                pe.wait_ge(A.sem, A.at("e5", i))
                nc.tensor.transpose(ps[:, 4, 0:128], p0[:, 0, 0:128], c("ident"))
                nc.tensor.transpose(ps[:, 4, 128:256], p1[:, 0, 0:128], c("ident"))
                nc.tensor.transpose(ps[:, 4, 256:384], p1[:, 0, 128:256], c("ident"))
                nc.tensor.transpose(ps[0:META, 5, 0:128], p0[:, 0, 128:144], c("ident"))
                nc.tensor.transpose(ps[0:META, 5, 128:256], p1[:, 0, 256:NT], c("ident"))
                nc.tensor.transpose(ps[0:META, 5, 256:NT], pm[0:META, 0, :], c("ident", META)[:, 0:META])\
                    .then_inc(T.sem, T.step("wt"))
                pe.wait_ge(A.sem, A.at("wT", i))
                pe.wait_ge(V.sem, V.at("wTm", i))
                for d in range(2):
                    o = ps[:, 6 + d, :]
                    f = slice(128 * d, 128 * d + 128)
                    mm(o[:, 0:NT], v[0:META, 2, f], fa["wTm"][0:META, :], stop=False)
                    mm(o[:, 0:256], v[:, 0, f], fa["wT"][:, 0:256], start=False, stop=False)
                    ins = mm(o[:, 128:256], v[:, 1, f], fa["wT"][:, 256:384], start=False)
                ins\
                    .then_inc(T.sem, T.step("pv"))
                pe.wait_ge(A.sem, A.at("sqo", i))
                for d in range(2):
                    ins = mm(ps[:, 5, 0:NT], c("ones"), fa["sqo"][:, d, :], start=(d == 0), stop=(d == 1))
                ins\
                    .then_inc(T.sem, T.step("osum"))
            repeat(pe, HEADS_A, body)

        def attn_a_act(act):
            A, T, V = SA["a"], SA["t"], SA["v"]

            def body(i):
                for t in range(4):
                    act.wait_ge(half_done, halves("a", t // 2, t % 2, i, 4))
                    if ran(i - 1):
                        act.wait_ge(T.sem, T.at("scores", i - 1))
                    nc.scalar.activation(fa["qk"][:, t, :], ps[:, t, 0:NT], ACT.Copy)\
                        .then_inc(A.sem, A.step(f"qk{t}"))
                for d in range(2):
                    act.wait_ge(half_done, halves("a", 2, d, i, 4))
                    if ran(i - 1):
                        act.wait_ge(T.sem, T.at("vt", i - 1))
                    nc.scalar.activation(fa["vT"][:, d, :], ps[:, d, 0:NT], ACT.Copy)\
                        .then_inc(A.sem, A.step(f"v{d}"))
                act.wait_ge(V.sem, V.at("nb", i))
                if ran(i - 1):
                    act.wait_ge(T.sem, T.at("wt", i - 1))

                def e(k, rows, o, s):
                    nc.scalar.activation(o, s, ACT.Exp, bias=st[0:rows, A_NB + k:A_NB + k + 1], scale=SCALE_A,
                                                accum_out=st[0:rows, A_RS + k:A_RS + k + 1])\
                        .then_inc(A.sem, A.step(f"e{k}"))
                for a in range(2):
                    e(a, 128, fa["p0"][:, a, :], ps[:, 4, 144 * a:144 * a + 144])
                for a in range(2):
                    e(2 + a, 128, fa["p1"][:, a, :], ps[:, 5 + a, 0:NT])
                for a in range(2):
                    e(4 + a, META, fa["pm"][0:META, a, :], ps[0:META, 4, 288 + META * a:288 + META * (a + 1)])
                for d in range(2):
                    act.wait_ge(half_done, halves("a", 3, d, i, 4))
                    if ran(i - 1):
                        act.wait_ge(V.sem, V.at("og1", i - 1))
                    nc.scalar.activation(fa["ga"][:, d, :], ps[:, 2 + d, 0:NT], ACT.Silu)\
                        .then_inc(A.sem, A.step(f"g{d}"))
                act.wait_ge(T.sem, T.at("wt", i))
                nc.scalar.activation(fa["wT"], ps[:, 4, 0:384], ACT.Copy)\
                    .then_inc(A.sem, A.step("wT"))
                act.wait_ge(T.sem, T.at("pv", i))
                nc.scalar.activation(fa["sqo"], ps[:, 6:8, 0:NT], ACT.Square)\
                    .then_inc(A.sem, A.step("sqo"))
                act.wait_ge(V.sem, V.at("var", i))
                nc.scalar.activation(fa["rstd"], fa["rstd"], ACT.Sqrt)\
                    .then_inc(A.sem, A.step("root"))
            repeat(act, HEADS_A, body)

        def attn_a_dve(dve):
            A, T, V = SA["a"], SA["t"], SA["v"]
            swap = [(r + 16) % 32 for r in range(32)]
            x, xc, sh = fa["qk"][0:32], fa["xc"][0:32], fa["sh"][0:32]
            cos = c("cos_a", 32).unsqueeze(1).to_broadcast([32, 4, NT])
            sin = c("sin_a", 32).unsqueeze(1).to_broadcast([32, 4, NT])
            p0, p1, pm = fa["p0"], fa["p1"], fa["pm"]

            def body(i):
                dve.wait_ge(A.sem, A.at("qk3", i))
                nc.vector.tensor_tensor(xc, x, cos, ALU.mult)\
                    .then_inc(V.sem, V.step("rcos"))
                nc.vector.stream_shuffle(sh, x, swap)\
                    .then_inc(V.sem, V.step("shuf"))
                dve.wait_ge(V.sem, V.at("shuf", i))
                nc.vector.tensor_tensor(sh, sh, sin, ALU.mult)\
                    .then_inc(V.sem, V.step("rsin"))
                dve.wait_ge(V.sem, V.at("rsin", i))
                nc.vector.tensor_tensor(x, xc, sh, ALU.add)\
                    .then_inc(V.sem, V.step("radd"))
                dve.wait_ge(T.sem, T.at("scores", i))
                nc.vector.tensor_reduce(st[:, 0:2], ps[:, 4, 0:288].rearrange("p (a b) -> p a b", a=2),
                                               AX.X, ALU.max)\
                    .then_inc(V.sem, V.step("mx0"))
                nc.vector.tensor_reduce(st[:, 2:4], ps[:, 5:7, 0:NT], AX.X, ALU.max)\
                    .then_inc(V.sem, V.step("mx1"))
                nc.vector.tensor_reduce(st[0:META, 4:6],
                                               ps[0:META, 4, 288:320].rearrange("p (a b) -> p a b", a=2),
                                               AX.X, ALU.max)\
                    .then_inc(V.sem, V.step("mxm"))
                dve.wait_ge(V.sem, V.at("mxm", i))
                nc.vector.tensor_scalar(st[:, A_NB:A_NB + 6], st[:, A_MX:A_MX + 6], -SCALE_A, None, ALU.mult)\
                    .then_inc(V.sem, V.step("nb"))
                dve.wait_ge(T.sem, T.at("vt", i))
                if ran(i - 1):
                    dve.wait_ge(T.sem, T.at("pv", i - 1))
                nc.vector.tensor_copy(fa["v"][:, 0:2, :], ps[:, 7, :].rearrange("p (a b) -> p a b", a=2))\
                    .then_inc(V.sem, V.step("v"))
                nc.vector.tensor_copy(fa["v"][0:META, 2, :], ps[0:META, 0, 0:256])\
                    .then_inc(V.sem, V.step("vm"))
                dve.wait_ge(A.sem, A.at("e5", i))
                nc.vector.reciprocal(st[:, A_RR:A_RR + 6], st[:, A_RS:A_RS + 6])\
                    .then_inc(V.sem, V.step("rr"))
                dve.wait_ge(V.sem, V.at("rr", i))
                odd = st[:, A_RR:A_RR + 6].rearrange("p (a b) -> p a b", b=2)[:, :, 1]
                nc.vector.tensor_scalar(odd, odd, st[:, LAM:LAM + 1], None, ALU.mult)\
                    .then_inc(V.sem, V.step("rl"))
                dve.wait_ge(V.sem, V.at("rl", i))
                for k, (w_, rows) in enumerate(((p0, 128), (p1, 128), (pm, META))):
                    r = A_RR + 2 * k
                    s = "01m"[k]
                    nc.vector.tensor_scalar(w_[0:rows, 0, :], w_[0:rows, 0, :], st[0:rows, r:r + 1], None,
                                                   ALU.mult)\
                        .then_inc(V.sem, V.step(f"n{s}"))
                    dve.wait_ge(V.sem, V.at(f"n{s}", i))
                    nc.vector.scalar_tensor_tensor(
                        out=w_[0:rows, 0, :], in0=w_[0:rows, 1, :], scalar=st[0:rows, r + 1:r + 2],
                        in1=w_[0:rows, 0, :], op0=ALU.mult, op1=ALU.add)\
                        .then_inc(V.sem, V.step(f"w{s}"))
                dve.wait_ge(T.sem, T.at("wt", i))
                nc.vector.tensor_copy(fa["wTm"][0:META, :], ps[0:META, 5, 0:NT])\
                    .then_inc(V.sem, V.step("wTm"))
                dve.wait_ge(T.sem, T.at("osum", i))
                nc.vector.tensor_scalar(fa["rstd"], ps[:, 5, 0:NT], 1.0 / 256, eps[:, 0:1], ALU.mult, ALU.add)\
                    .then_inc(V.sem, V.step("var"))
                dve.wait_ge(A.sem, A.at("root", i))
                nc.vector.reciprocal(fa["rstd"], fa["rstd"])\
                    .then_inc(V.sem, V.step("rstd"))
                dve.wait_ge(V.sem, V.at("rstd", i))
                for d in range(2):
                    nc.vector.scalar_tensor_tensor(
                        out=fa["o"][:, d, :], in0=ps[:, 6 + d, 0:NT], scalar=p("subln", d), in1=fa["rstd"],
                        op0=ALU.mult, op1=ALU.mult)\
                        .then_inc(V.sem, V.step(f"o{d}"))
                dve.wait_ge(A.sem, A.at("g1", i))
                for d in range(2):
                    dve.wait_ge(V.sem, V.at(f"o{d}", i))
                    nc.vector.scalar_tensor_tensor(
                        out=og[:, bass.ds(2 * i + d, 1), :], in0=fa["o"][:, d:d + 1, :], scalar=1.0 - LAMBDA_INIT,
                        in1=fa["ga"][:, d:d + 1, :], op0=ALU.mult, op1=ALU.mult)\
                        .then_inc(V.sem, V.step(f"og{d}"))
            repeat(dve, HEADS_A, body)

        a_out = Product("a_out", "a_out", og, NT, xT, add=True)

        norm_b = Norm("norm_b", xT, NT, 0, [("kv", hT), ("b", og)])
        SK = phase("kv", a="c0 c1 c2 c3", t="vt",
                   v="shuf rsin rcos radd zero " + " ".join(f"k{g}_{h}" for g in range(4) for h in range(2)) + " v vm")
        fb = carve([("kd", 4, 2 * NT), ("vB", 3, 256), ("kv", 4, NT), ("sh", 2, NT)])

        def kv_pe(pe):
            pe.wait_ge(norm_b.V.sem, norm_b.V.at(norm_b.last))
            for u in range(2):
                slot = (FIRST_UNIT["kv"] + u) % RING
                pe.wait_ge(unit_in[slot], loaded("kv", u))
                for h in range(2):
                    half(slot, h, ps[:, 2 * u + h, :], hT, NT).then_inc(half_done, 1)
            pe.wait_ge(SK["a"].sem, SK["a"].at("c3"))
            for tok in range(2):
                for k in range(2):
                    nc.tensor.transpose(ps[:, 4, 256 * tok + 128 * k:256 * tok + 128 * k + 128],
                                        fb["kv"][:, 2 + k, 128 * tok:128 * tok + 128], c("ident"))
            for k in range(2):
                ins = nc.tensor.transpose(ps[0:META, 5, 128 * k:128 * k + 128], fb["kv"][:, 2 + k, 256:NT], c("ident"))
            ins\
                .then_inc(SK["t"].sem, SK["t"].step("vt"))

        def kv_act(act):
            for t in range(4):
                act.wait_ge(half_done, halves("kv", t // 2, t % 2))
                nc.scalar.activation(fb["kv"][:, t, :], ps[:, t, 0:NT], ACT.Copy)\
                    .then_inc(SK["a"].sem, SK["a"].step(f"c{t}"))

        def kv_dve(dve):
            V = SK["v"]
            swap = [r ^ 8 if r < 16 else r for r in range(32)]
            x, sh = fb["kv"][:, 0:2, :], fb["sh"]
            dve.wait_ge(SK["a"].sem, SK["a"].at("c1"))
            nc.vector.stream_shuffle(sh, x, swap)\
                .then_inc(V.sem, V.step("shuf"))
            dve.wait_ge(V.sem, V.at("shuf"))
            nc.vector.tensor_tensor(sh, sh, c("sin_b").unsqueeze(1).to_broadcast([128, 2, NT]), ALU.mult)\
                .then_inc(V.sem, V.step("rsin"))
            nc.vector.tensor_tensor(x, x, c("cos_b").unsqueeze(1).to_broadcast([128, 2, NT]), ALU.mult)\
                .then_inc(V.sem, V.step("rcos"))
            dve.wait_ge(V.sem, V.at("rcos"))
            nc.vector.tensor_tensor(x, x, sh, ALU.add)\
                .then_inc(V.sem, V.step("radd"))
            nc.vector.memset(fb["kd"], 0.0)\
                .then_inc(V.sem, V.step("zero"))
            dve.wait_ge(V.sem, V.at("zero"))
            for g in range(4):
                for h in range(2):
                    nc.vector.tensor_copy(fb["kd"][64 * h:64 * h + 64, g, NT * h:NT * h + NT],
                                                 fb["kv"][64 * (g % 2):64 * (g % 2) + 64, g // 2, :])\
                        .then_inc(V.sem, V.step(f"k{g}_{h}"))
            dve.wait_ge(SK["t"].sem, SK["t"].at("vt"))
            nc.vector.tensor_copy(fb["vB"][:, 0:2, :], ps[:, 4, :].rearrange("p (a b) -> p a b", a=2))\
                .then_inc(V.sem, V.step("v"))
            nc.vector.tensor_copy(fb["vB"][0:META, 2, :], ps[0:META, 5, 0:256])\
                .then_inc(V.sem, V.step("vm"))

        rounds = " ".join(f"R{j}" for j in range(4))
        SB = phase("attn_b",
                   a="q0 q1 q2 q3 " + " ".join(f"e{j}_0 e{j}_1 e{j}_2 e{j}_3 es{j} g{j} wk{j}" for j in range(4)),
                   t=" ".join(f"sc{j} wt{j} pv{j}" for j in range(4)),
                   v="kg vg vgm sk rcos shuf rsin radd " + " ".join(
                       f"ma{j} mb{j} sm{j} nb{j} sn{j} den{j} rr{j} p{j}_0 p{j}_1 p{j}_2 p{j}_3 w1{j} wm{j} o{j}"
                       for j in range(4)))
        f2 = carve([("kd", 4, 2 * NT), ("vB", 3, 256), ("q", 4, 256), ("sh", 4, 256), ("xc", 4, 256), ("kg", 2 * NT), ("vg", 3, 64),
                    ("sk", 8), ("p0", 2, 144), ("p1", 2, NT), ("wk0", 512), ("wk1", 256), ("wkm", 512),
                    ("gb", 4, 256), ("stb", 32)])
        B_MX, B_SM, B_NB, B_SN, B_RS, B_RR = 0, 4, 8, 12, 16, 20

        def attn_b_pe(pe):
            A, T, V = SB["a"], SB["t"], SB["v"]
            q, kg, vg, p0, p1 = f2["q"], f2["kg"], f2["vg"], f2["p0"], f2["p1"]
            pe.wait_ge(norm_b.V.sem, norm_b.V.at(norm_b.last))
            pe.wait_ge(SK["v"].sem, SK["v"].at("vm"))

            def body(i):
                for t in range(4):
                    if t % 2 == 0:
                        slot = (FIRST_UNIT["b"] + t // 2) % RING
                        pe.wait_ge(unit_in[slot], loaded("b", t // 2, i, 4))
                    if ran(i - 1):
                        pe.wait_ge(A.sem, A.at(f"g{t}", i - 1))
                    half(slot, t % 2, ps[:, t, :], og, 256).then_inc(half_done, 1)
                pe.wait_ge(V.sem, V.at("radd", i))
                for j in range(4):
                    if j:
                        pe.wait_ge(V.sem, V.at(f"o{j - 1}", i))
                    else:
                        if ran(i - 1):
                            pe.wait_ge(V.sem, V.at("o3", i - 1))
                    for a in range(2):
                        ka = kg[:, NT * a:NT * a + NT]
                        o = ps[:, 4, 144 * a:144 * a + 144]
                        mm(o[:, 128:144], q[:, j, 0:128], ka[:, 256:NT])
                        mm(o[:, 0:128], q[:, j, 0:128], ka[:, 0:128], stop=False)
                        mm(o[:, 64:128], c("low", 1), c("neg", 1), start=False)
                        o = ps[:, 5 + a, :]
                        mm(o[:, 0:NT], q[:, j, 128:256], ka, stop=False)
                        mm(o[:, 192:256], c("low", 1), c("neg", 1), start=False, stop=False)
                        ins = mm(o[:, 0:64], c("high", 1), c("neg", 1), start=False)
                    ins\
                        .then_inc(T.sem, T.step(f"sc{j}"))
                    if j % 2 == 0:
                        slot = (FIRST_UNIT["b"] + 2 + j // 2) % RING
                        pe.wait_ge(unit_in[slot], loaded("b", 2 + j // 2, i, 4))
                    pe.wait_ge(A.sem, A.at(f"q{j}", i))
                    half(slot, j % 2, ps[:, j, :], og, 256).then_inc(half_done, 1)
                    pe.wait_ge(V.sem, V.at(f"p{j}_3", i))
                    if ran(i if j else i - 1):
                        pe.wait_ge(A.sem, A.at(f"wk{j - 1}" if j else "wk3", i if j else i - 1))
                    for a in range(2):
                        nc.tensor.transpose(ps[:, 7, 256 * a:256 * a + 128], p0[:, a, 0:128], c("ident"))
                        nc.tensor.transpose(ps[:, 7, 256 * a + 128:256 * a + 256], p1[:, a, 0:128], c("ident"))
                        nc.tensor.transpose(ps[:, 4, 128 * a:128 * a + 128], p1[:, a, 128:256], c("ident"))
                        nc.tensor.transpose(ps[0:META, 5, 256 * a:256 * a + 128], p0[:, a, 128:144], c("ident"))
                        ins = nc.tensor.transpose(ps[0:META, 5, 256 * a + 128:256 * a + 256], p1[:, a, 256:NT],
                                                  c("ident"))
                    ins\
                        .then_inc(T.sem, T.step(f"wt{j}"))
                    pe.wait_ge(A.sem, A.at(f"wk{j}", i))
                    pe.wait_ge(V.sem, V.at(f"wm{j}", i))
                    for a in range(2):
                        o = ps[64 * a:64 * a + 64, 6, :]
                        mm(o[:, 0:256], vg[0:META, 2, :], f2["wkm"][0:META, 256 * a:256 * a + 256], stop=False)
                        mm(o[:, 0:256], vg[:, 0, :], f2["wk0"][:, 256 * a:256 * a + 256], start=False, stop=False)
                        ins = mm(o[:, 128:256], vg[:, 1, :], f2["wk1"][:, 128 * a:128 * a + 128], start=False)
                    ins\
                        .then_inc(T.sem, T.step(f"pv{j}"))
            repeat(pe, GROUPS_B, body)

        def attn_b_act(act):
            A, T, V = SB["a"], SB["t"], SB["v"]
            stb = f2["stb"]

            def body(i):
                for t in range(4):
                    act.wait_ge(half_done, halves("b", t // 2, t % 2, i, 4))
                    if ran(i - 1):
                        act.wait_ge(T.sem, T.at("sc3", i - 1))
                    nc.scalar.activation(f2["q"][:, t, :], ps[:, t, 0:256], ACT.Copy)\
                        .then_inc(A.sem, A.step(f"q{t}"))
                for j in range(4):
                    act.wait_ge(V.sem, V.at(f"sn{j}", i))
                    if ran(i if j else i - 1):
                        act.wait_ge(T.sem, T.at(f"wt{j - 1}" if j else "wt3", i if j else i - 1))
                    for k in range(4):
                        o, s = ((f2["p0"][:, k, :], ps[:, 4, 144 * k:144 * k + 144]) if k < 2 else
                                (f2["p1"][:, k - 2, :], ps[:, 3 + k, 0:NT]))
                        nc.scalar.activation(o, s, ACT.Exp, bias=stb[:, B_NB + k:B_NB + k + 1], scale=SCALE_B,
                                                    accum_out=stb[:, B_RS + k:B_RS + k + 1])\
                            .then_inc(A.sem, A.step(f"e{j}_{k}"))
                    nc.scalar.activation(stb[:, B_SN:B_SN + 4], stb[:, B_SN:B_SN + 4], ACT.Exp)\
                        .then_inc(A.sem, A.step(f"es{j}"))
                    act.wait_ge(half_done, halves("b", 2 + j // 2, j % 2, i, 4))
                    if ran(i - 1):
                        act.wait_ge(V.sem, V.at(f"o{j}", i - 1))
                    nc.scalar.activation(f2["gb"][:, j, :], ps[:, j, 0:256], ACT.Silu)\
                        .then_inc(A.sem, A.step(f"g{j}"))
                    act.wait_ge(T.sem, T.at(f"wt{j}", i))
                    nc.scalar.activation(f2["wk0"], ps[:, 7, :], ACT.Copy)\
                        .then_inc(A.sem, A.step(f"wk{j}"))
            repeat(act, GROUPS_B, body)

        def attn_b_dve(dve):
            A, T, V = SB["a"], SB["t"], SB["v"]
            stb, p0, p1 = f2["stb"], f2["p0"], f2["p1"]
            swap = [r ^ 8 if r < 16 else r for r in range(32)]
            cos = c("cos_b")[:, 0:256].unsqueeze(1).to_broadcast([128, 4, 256])
            sin = c("sin_b")[:, 0:256].unsqueeze(1).to_broadcast([128, 4, 256])
            dve.wait_ge(SK["v"].sem, SK["v"].at("vm"))

            def body(i):
                if ran(i - 1):
                    dve.wait_ge(T.sem, T.at("pv3", i - 1))
                nc.vector.tensor_copy(f2["kg"].unsqueeze(1), f2["kd"][:, bass.ds(i, 1), :])\
                    .then_inc(V.sem, V.step("kg"))
                nc.vector.tensor_copy(f2["vg"][:, 0:2, :], f2["vB"][:, 0:2, bass.ds(64 * i, 64)])\
                    .then_inc(V.sem, V.step("vg"))
                nc.vector.tensor_copy(f2["vg"][0:META, 2:3, :], f2["vB"][0:META, 2:3, bass.ds(64 * i, 64)])\
                    .then_inc(V.sem, V.step("vgm"))
                nc.vector.tensor_copy(f2["sk"], P[:, bass.ds(8 * i + P_AT["sinks"][0], 8)])\
                    .then_inc(V.sem, V.step("sk"))
                dve.wait_ge(A.sem, A.at("q3", i))
                nc.vector.tensor_tensor(f2["xc"], f2["q"], cos, ALU.mult)\
                    .then_inc(V.sem, V.step("rcos"))
                nc.vector.stream_shuffle(f2["sh"], f2["q"], swap)\
                    .then_inc(V.sem, V.step("shuf"))
                dve.wait_ge(V.sem, V.at("shuf", i))
                nc.vector.tensor_tensor(f2["sh"], f2["sh"], sin, ALU.mult)\
                    .then_inc(V.sem, V.step("rsin"))
                dve.wait_ge(V.sem, V.at("rsin", i))
                nc.vector.tensor_tensor(f2["q"], f2["xc"], f2["sh"], ALU.add)\
                    .then_inc(V.sem, V.step("radd"))
                for j in range(4):
                    sink = f2["sk"][:, 2 * j:2 * j + 2].unsqueeze(1).to_broadcast([128, 2, 2])

                    def s4(k):
                        return stb[:, k:k + 4].rearrange("p (a b) -> p a b", a=2)
                    dve.wait_ge(T.sem, T.at(f"sc{j}", i))
                    nc.vector.tensor_reduce(stb[:, 0:2], ps[:, 4, 0:288].rearrange("p (a b) -> p a b", a=2),
                                                   AX.X, ALU.max)\
                        .then_inc(V.sem, V.step(f"ma{j}"))
                    nc.vector.tensor_reduce(stb[:, 2:4], ps[:, 5:7, 0:NT], AX.X, ALU.max)\
                        .then_inc(V.sem, V.step(f"mb{j}"))
                    dve.wait_ge(V.sem, V.at(f"mb{j}", i))
                    nc.vector.scalar_tensor_tensor(out=s4(B_SM), in0=s4(B_MX), scalar=SCALE_B, in1=sink,
                                                          op0=ALU.mult, op1=ALU.max)\
                        .then_inc(V.sem, V.step(f"sm{j}"))
                    dve.wait_ge(V.sem, V.at(f"sm{j}", i))
                    nc.vector.tensor_scalar(stb[:, B_NB:B_NB + 4], stb[:, B_SM:B_SM + 4], -1.0, None,
                                                   ALU.mult)\
                        .then_inc(V.sem, V.step(f"nb{j}"))
                    nc.vector.tensor_tensor(s4(B_SN), sink, s4(B_SM), ALU.subtract)\
                        .then_inc(V.sem, V.step(f"sn{j}"))
                    dve.wait_ge(A.sem, A.at(f"es{j}", i))
                    nc.vector.tensor_tensor(stb[:, B_RR:B_RR + 4], stb[:, B_RS:B_RS + 4],
                                                   stb[:, B_SN:B_SN + 4], ALU.add)\
                        .then_inc(V.sem, V.step(f"den{j}"))
                    dve.wait_ge(V.sem, V.at(f"den{j}", i))
                    nc.vector.reciprocal(stb[:, B_RR:B_RR + 4], stb[:, B_RR:B_RR + 4])\
                        .then_inc(V.sem, V.step(f"rr{j}"))
                    dve.wait_ge(V.sem, V.at(f"rr{j}", i))
                    for k in range(4):
                        w_ = p0[:, k, :] if k < 2 else p1[:, k - 2, :]
                        nc.vector.tensor_scalar(w_, w_, stb[:, B_RR + k:B_RR + k + 1], None, ALU.mult)\
                            .then_inc(V.sem, V.step(f"p{j}_{k}"))
                    dve.wait_ge(T.sem, T.at(f"wt{j}", i))
                    nc.vector.tensor_copy(f2["wk1"], ps[:, 4, 0:256])\
                        .then_inc(V.sem, V.step(f"w1{j}"))
                    nc.vector.tensor_copy(f2["wkm"][0:META, :], ps[0:META, 5, :])\
                        .then_inc(V.sem, V.step(f"wm{j}"))
                    dve.wait_ge(T.sem, T.at(f"pv{j}", i))
                    dve.wait_ge(A.sem, A.at(f"g{j}", i))
                    nc.vector.tensor_tensor(hT[:, bass.ds(4 * i + j, 1), 0:256], ps[:, 6:7, 0:256],
                                                   f2["gb"][:, j:j + 1, :], ALU.mult)\
                        .then_inc(V.sem, V.step(f"o{j}"))
            repeat(dve, GROUPS_B, body)

        b_out = Product("b_out", "b_out", hT, SEQ, xT, add=True)
        norm_fin = Norm("norm_fin", xT, SEQ, 0, [("fin", xT)])
        norm_mix = Norm("norm_mix", xT, SEQ, 1, [("mix_pre", hT)])

        SR = phase("rw_in", v=" ".join(f"t{t}" for t in range(8)))
        SS = phase("rw_small", a="wa g0 g1 tanh sig0 sig1 f lora", v=" ".join(
            f"d{k} n{k} m{k}" for k in range(3)) + " zeroa zerob zeroc zerov", t="lora")
        fr = carve([("zr", 24, 256), ("zs", 4, 256), ("lora", 3, 1024), ("aq", 4, 256), ("bx", 4, 128),
                    ("cx", 4, 128), ("vx", 4, 128), ("LT", 4, 128), ("BQ", 4, 128), ("CA", 4, 128),
                    ("CQ", 4, 128), ("X", 4, 128), ("Y", 4, 128), ("bT", 4, 128), ("cT", 4, 128),
                    ("vT", 4, 128), ("lw", 3, 128), ("pj", 10), ("S", 128), ("R", 128), ("U", 128),
                    ("g", 256), ("bon", 256)])
        zs = fr["zs"]

        def rw_in_pe(pe):
            pe.wait_ge(norm_mix.V.sem, norm_mix.V.at(norm_mix.last))

            def body(i):
                for t in range(8):
                    if t % 2 == 0:
                        slot = (FIRST_UNIT["rw"] + t // 2) % RING
                        pe.wait_ge(unit_in[slot], loaded("rw", t // 2, i, 4))
                    if ran(i if t >= 4 else i - 1):
                        pe.wait_ge(SR["v"].sem, SR["v"].at(f"t{(t - 4) % 8}", i if t >= 4 else i - 1))
                    half(slot, t % 2, ps[:, t % 4, :], hT, SEQ).then_inc(half_done, 1)
            repeat(pe, 3, body)
            slot = (FIRST_UNIT["small"] + 0) % RING
            pe.wait_ge(unit_in[slot], loaded("small", 0))
            pe.wait_ge(SR["v"].sem, SR["v"].at("t7", 2))
            half(slot, 0, ps[:, 0, :], hT, SEQ).then_inc(half_done, 1)
            half(slot, 1, ps[:, 1, :], hT, SEQ, m=SB_HEADS).then_inc(half_done, 1)
            slot = (FIRST_UNIT["small"] + 1) % RING
            pe.wait_ge(unit_in[slot], loaded("small", 1))
            half(slot, 0, ps[:, 2, :], hT, SEQ).then_inc(half_done, 1)
            half(slot, 1, ps[:, 3, :], hT, SEQ, m=32).then_inc(half_done, 1)
            pe.wait_ge(SS["a"].sem, SS["a"].at("lora"))
            slot = (FIRST_UNIT["small"] + 2) % RING
            for k in range(2):
                nc.tensor.matmul(ps[0:32, 4, 0:32], C[0:32, 0:32], C[0:32, 0:32], start=True, stop=True)\
                    .then_inc(half_done, 1)

        def rw_in_act(act):
            A = SS["a"]
            act.wait_ge(half_done, halves("small", 0, 0))
            nc.scalar.activation(zs[:, 0, :], ps[:, 0, 0:256], ACT.Copy)\
                .then_inc(A.sem, A.step("wa"))
            act.wait_ge(half_done, halves("small", 1, 1))
            nc.scalar.activation(zs[:, 1, :], ps[:, 2, 0:256], ACT.Copy)\
                .then_inc(A.sem, A.step("g0"))
            nc.scalar.activation(zs[0:32, 2, :], ps[0:32, 3, 0:256], ACT.Copy)\
                .then_inc(A.sem, A.step("g1"))
            act.wait_ge(SS["v"].sem, SS["v"].at("m0"))
            nc.scalar.activation(zs[0:64, 0, :], zs[0:64, 0, :], ACT.Tanh)\
                .then_inc(A.sem, A.step("tanh"))
            act.wait_ge(SS["v"].sem, SS["v"].at("m2"))
            nc.scalar.activation(zs[:, 1, :], zs[:, 1, :], ACT.Sigmoid)\
                .then_inc(A.sem, A.step("sig0"))
            nc.scalar.activation(zs[0:32, 2, :], zs[0:32, 2, :], ACT.Sigmoid)\
                .then_inc(A.sem, A.step("sig1"))
            nc.scalar.activation(zs[0:SB_HEADS, 3, :], ps[0:SB_HEADS, 1, 0:256], ACT.Copy)\
                .then_inc(A.sem, A.step("f"))
            slot = (FIRST_UNIT["small"] + 2) % RING
            act.wait_ge(unit_in[slot], loaded("small", 2))
            src = ring[:, slot, 0:12, :].rearrange("p a b -> p (a b)").rearrange("p (a b) -> p a b", a=3)
            nc.scalar.activation(fr["lora"], src, ACT.Copy)\
                .then_inc(A.sem, A.step("lora"))

        def rw_in_dve(dve):
            def body(i):
                for t in range(8):
                    dve.wait_ge(half_done, halves("rw", t // 2, t % 2, i, 4))
                    nc.vector.tensor_copy(fr["zr"][:, bass.ds(8 * i + t, 1), :],
                                                       ps[:, t % 4:t % 4 + 1, 0:256])\
                        .then_inc(SR["v"].sem, SR["v"].step(f"t{t}"))
            repeat(dve, 3, body)
            V = SS["v"]
            tmp = og[:, 0, 0:256]
            for k, (name, j, rows, ready) in enumerate((("mu_wa", 0, 128, "wa"), ("mu_g", 0, 128, "g0"),
                                                        ("mu_g", 1, 32, "g1"))):
                z = zs[0:rows, k, :]
                dve.wait_ge(SS["a"].sem, SS["a"].at(ready))
                if k:
                    dve.wait_ge(V.sem, V.at(f"m{k - 1}"))
                nc.vector.tensor_tensor(tmp[0:rows, 1:256], z[:, 0:255], z[:, 1:256], ALU.subtract)\
                    .then_inc(V.sem, V.step(f"d{k}"))
                nc.vector.tensor_scalar(tmp[0:rows, 0:1], z[:, 0:1], -1.0, None, ALU.mult)\
                    .then_inc(V.sem, V.step(f"n{k}"))
                dve.wait_ge(V.sem, V.at(f"n{k}"))
                nc.vector.scalar_tensor_tensor(out=z, in0=tmp[0:rows, :], scalar=p(name, j, rows), in1=z,
                                                      op0=ALU.mult, op1=ALU.add)\
                    .then_inc(V.sem, V.step(f"m{k}"))
            nc.vector.memset(fr["aq"], 0.0)\
                .then_inc(V.sem, V.step("zeroa"))
            nc.vector.memset(fr["bx"], 0.0)\
                .then_inc(V.sem, V.step("zerob"))
            nc.vector.memset(fr["cx"], 0.0)\
                .then_inc(V.sem, V.step("zeroc"))
            nc.vector.memset(fr["vx"], 0.0)\
                .then_inc(V.sem, V.step("zerov"))

        NCH = SEQ // CHUNK
        lv = LEVELS[1:]
        SW = phase("rwkv",
                   a="w a g sqk nrm ea enc ec bT cT vT " + " ".join(f"t1_{b}" for b in lv)
                     + " " + " ".join(f"U{n}" for n in range(NCH)) + " sqy root",
                   t="lora kk bon grams tr " + " ".join(f"T{b} dY{b}" for b in lv)
                     + " " + " ".join(f"R{n} U{n} y{n}" for n in range(NCH)) + " mean var",
                   v="pj lw " + " ".join(f"d{z} n{z} m{z}" for z in "rkv") + " kk max rec kkn am1 k2 rk rkk bonus ld "
                     "cum cb a0 a1 q0 q1 ka b0 b1 c0 c1 v0 v1 LT BQ CA CQ x0 x1 y0 y1 "
                     "M2 M4 X2 Y2 M8 X4 Y4 M16 X8 Y8 M32 X16 Y16 Y32 "
                     + " ".join(f"R{n} S{n} P{n}" if 0 < n < NCH - 1 else (f"R{n} P{n}" if n == 0 else f"R{n}")
                                for n in range(NCH))
                     + " ys0 ys1 yc gvar grec gn gl gb gy")
        tmp = {n: og[:, k, 0:256] for k, n in enumerate("r k v kk a ec enc t1".split())}
        tmp["g"] = fr["g"]
        Xv = {"M": (fr["bx"], fr["cx"])}

        def rwkv_pe(pe):
            A, T, V = SW["a"], SW["t"], SW["v"]
            aq, bx, cx, vx, S = fr["aq"], fr["bx"], fr["cx"], fr["vx"], fr["S"]
            pe.wait_ge(SS["a"].sem, SS["a"].at("lora"))

            def body(i):
                pe.wait_ge(V.sem, V.at("lw", i))
                if ran(i - 1):
                    pe.wait_ge(V.sem, V.at("grec", i - 1))
                lw = fr["lw"]
                mm(ps[:, 0, 0:256], lw[0:64, 0, :], zs[0:64, 0, :])
                mm(ps[:, 1, 0:256], lw[64:128, 0, :], zs[64:128, 0, :])
                mm(ps[:, 2, 0:256], lw[:, 1, :], zs[:, 1, :], stop=False)
                mm(ps[:, 2, 0:256], lw[0:32, 2, :], zs[0:32, 2, :], start=False)\
                    .then_inc(T.sem, T.step("lora"))
                pe.wait_ge(A.sem, A.at("sqk", i))
                mm(ps[:, 3, 0:256], c("hones"), tmp["t1"])\
                    .then_inc(T.sem, T.step("kk"))
                pe.wait_ge(V.sem, V.at("rkk", i))
                mm(ps[:, 4, 0:256], c("hones"), tmp["enc"])\
                    .then_inc(T.sem, T.step("bon"))
                pe.wait_ge(V.sem, V.at("v1", i))
                for n in range(NCH):
                    mm(ps[:, n, 0:256], bx[:, n, :], aq[:, n, :])
                    mm(ps[:, n, 256:512], cx[:, n, :], aq[:, n, :])
                for n in range(NCH):
                    ins = mm(ps[:, 4, 128 * n:128 * n + 128], aq[:, n, 0:128], bx[:, n, :])
                ins\
                    .then_inc(T.sem, T.step("grams"))
                if ran(i - 1):
                    pe.wait_ge(V.sem, V.at("ys1", i - 1))
                for bank, src in ((5, bx), (6, cx), (7, vx)):
                    for n in range(NCH):
                        ins = nc.tensor.transpose(ps[:, bank, 128 * n:128 * n + 128], src[:, n, :], c("ident"))
                ins\
                    .then_inc(T.sem, T.step("tr"))
                X, Y, T1 = fr["X"], fr["Y"], fr["vx"]
                for k, b in enumerate(lv):
                    pe.wait_ge(V.sem, V.at(f"M{b}", i))
                    pe.wait_ge(V.sem, V.at(f"X{lv[k - 1]}" if k else "y1", i))
                    for n in range(NCH):
                        ins = mm(ps[:, 0, 128 * n:128 * n + 128], Xv["M"][k % 2][:, n, :], X[:, n, :])
                    ins\
                        .then_inc(T.sem, T.step(f"T{b}"))
                    pe.wait_ge(A.sem, A.at(f"t1_{b}", i))
                    if k:
                        pe.wait_ge(V.sem, V.at(f"Y{lv[k - 1]}", i))
                    for n in range(NCH):
                        if b != lv[-1]:
                            mm(ps[:, 1, 128 * n:128 * n + 128], Y[:, n, :], T1[:, n, :])
                        ins = mm(ps[:, 2, 128 * n:128 * n + 128], T1[:, n, :], Y[:, n, :])
                    ins\
                        .then_inc(T.sem, T.step(f"dY{b}"))
                pe.wait_ge(V.sem, V.at(f"Y{lv[-1]}", i))
                for n in range(NCH):
                    if n:
                        pe.wait_ge(V.sem, V.at(f"P{n - 1}", i))
                        mm(ps[:, 3, 0:128], aq[:, n, 0:128], S, stop=False)
                    mm(ps[:, 3, 0:128], fr["CA"][:, n, :], fr["vT"][:, n, :], start=(n == 0))\
                        .then_inc(T.sem, T.step(f"R{n}"))
                    pe.wait_ge(V.sem, V.at(f"R{n}", i))
                    mm(ps[:, 4, 0:128], Y[:, n, :], fr["R"])\
                        .then_inc(T.sem, T.step(f"U{n}"))
                    pe.wait_ge(A.sem, A.at(f"U{n}", i))
                    y = ps[:, 5, 128 * n:128 * n + 128]
                    if n:
                        mm(y, S, aq[:, n, 128:256], stop=False)
                    mm(y, fr["U"], fr["BQ"][:, n, :], start=(n == 0), stop=False)
                    ins = mm(y, fr["vT"][:, n, :], fr["CQ"][:, n, :], start=False)
                    if n < NCH - 1:
                        mm(ps[:, 6, 0:128], fr["cT"][:, n, :], fr["vT"][:, n, :], stop=False)
                        ins = mm(ps[:, 6, 0:128], fr["bT"][:, n, :], fr["U"], start=False)
                    ins\
                        .then_inc(T.sem, T.step(f"y{n}"))
                pe.wait_ge(V.sem, V.at("ys1", i))
                mm(ps[:, 0, 0:256], c("hones"), tmp["t1"])\
                    .then_inc(T.sem, T.step("mean"))
                pe.wait_ge(A.sem, A.at("sqy", i))
                mm(ps[:, 1, 0:256], c("hones"), tmp["enc"])\
                    .then_inc(T.sem, T.step("var"))
            repeat(pe, RW_TILES, body)

        def rwkv_act(act):
            A, T, V = SW["a"], SW["t"], SW["v"]
            pj = fr["pj"]
            flat = "p a b -> p (a b)"

            def body(i):
                act.wait_ge(T.sem, T.at("lora", i))
                if ran(i - 1):
                    act.wait_ge(V.sem, V.at("gy", i - 1))
                nc.scalar.activation(tmp["ec"], ps[:, 0, 0:256], ACT.Sigmoid, bias=pj[:, W0:W0 + 1])\
                    .then_inc(A.sem, A.step("w"))
                nc.scalar.activation(tmp["a"], ps[:, 1, 0:256], ACT.Sigmoid, bias=pj[:, A0:A0 + 1])\
                    .then_inc(A.sem, A.step("a"))
                nc.scalar.activation(tmp["g"], ps[:, 2, 0:256], ACT.Copy)\
                    .then_inc(A.sem, A.step("g"))
                act.wait_ge(V.sem, V.at("kk", i))
                nc.scalar.activation(tmp["t1"], tmp["kk"], ACT.Square)\
                    .then_inc(A.sem, A.step("sqk"))
                act.wait_ge(T.sem, T.at("kk", i))
                nc.scalar.activation(tmp["t1"], ps[:, 3, 0:256], ACT.Sqrt)\
                    .then_inc(A.sem, A.step("nrm"))
                act.wait_ge(V.sem, V.at("cb", i))
                nc.scalar.activation(tmp["t1"], tmp["t1"], ACT.Exp)\
                    .then_inc(A.sem, A.step("ea"))
                nc.scalar.activation(tmp["enc"], tmp["ec"], ACT.Exp, scale=-1.0)\
                    .then_inc(A.sem, A.step("enc"))
                act.wait_ge(A.sem, A.at("enc", i))
                nc.scalar.activation(tmp["ec"], tmp["ec"], ACT.Exp)\
                    .then_inc(A.sem, A.step("ec"))
                act.wait_ge(T.sem, T.at("tr", i))
                nc.scalar.activation(fr["bT"].rearrange(flat), ps[:, 5, :], ACT.Copy, scale=-1.0)\
                    .then_inc(A.sem, A.step("bT"))
                nc.scalar.activation(fr["cT"].rearrange(flat), ps[:, 6, :], ACT.Copy)\
                    .then_inc(A.sem, A.step("cT"))
                nc.scalar.activation(fr["vT"].rearrange(flat), ps[:, 7, :], ACT.Copy)\
                    .then_inc(A.sem, A.step("vT"))
                for b in lv:
                    act.wait_ge(T.sem, T.at(f"T{b}", i))
                    nc.scalar.activation(fr["vx"].rearrange(flat), ps[:, 0, :], ACT.Copy)\
                        .then_inc(A.sem, A.step(f"t1_{b}"))
                for n in range(NCH):
                    act.wait_ge(T.sem, T.at(f"U{n}", i))
                    nc.scalar.activation(fr["U"], ps[:, 4, 0:128], ACT.Copy)\
                        .then_inc(A.sem, A.step(f"U{n}"))
                act.wait_ge(V.sem, V.at("yc", i))
                nc.scalar.activation(tmp["enc"], tmp["ec"], ACT.Square)\
                    .then_inc(A.sem, A.step("sqy"))
                act.wait_ge(V.sem, V.at("gvar", i))
                nc.scalar.activation(tmp["t1"], tmp["t1"], ACT.Sqrt)\
                    .then_inc(A.sem, A.step("root"))
            repeat(act, RW_TILES, body)

        def rwkv_dve(dve):
            A, T, V = SW["a"], SW["t"], SW["v"]
            pj = fr["pj"]
            aq, bx, cx, vx = fr["aq"], fr["bx"], fr["cx"], fr["vx"]
            flat = "p a b -> p (a b)"
            r, k, v, kk, a, ec, enc, t1 = (tmp[n] for n in "r k v kk a ec enc t1".split())

            def col(k_):
                return pj[:, k_:k_ + 1]

            def mask(name):
                return c(name).unsqueeze(1).to_broadcast([128, NCH, 128])

            def spread(o, off, x, y, names, op=ALU.mult):
                for h in range(2):
                    r_ = slice(64 * h, 64 * h + 64)
                    dst = o[r_, :, off + 64 * h:off + 64 * h + 64]
                    xv = x[r_].rearrange("p (a b) -> p a b", a=NCH)
                    if y is None:
                        nc.vector.tensor_copy(dst, xv)\
                            .then_inc(V.sem, V.step(names[h]))
                    else:
                        nc.vector.tensor_tensor(dst, xv, y[r_].rearrange("p (a b) -> p a b", a=NCH), op)\
                            .then_inc(V.sem, V.step(names[h]))

            def body(i):
                if ran(i - 1):
                    dve.wait_ge(V.sem, V.at("gy", i - 1))
                dve.wait_ge(SS["a"].sem, SS["a"].at("lora"))
                nc.vector.tensor_copy(pj, P[:, bass.ds(10 * i + P_AT["rw"][0], 10)])\
                    .then_inc(V.sem, V.step("pj"))
                nc.vector.tensor_copy(fr["lw"], fr["lora"][:, :, bass.ds(128 * i, 128)])\
                    .then_inc(V.sem, V.step("lw"))
                dve.wait_ge(V.sem, V.at("pj", i))
                for q, (z, o) in enumerate(zip("rkv", (r, k, v))):
                    src = fr["zr"][:, bass.ds(i + 8 * q, 1), :]
                    nc.vector.tensor_tensor(o[:, 1:256].unsqueeze(1), src[:, :, 0:255], src[:, :, 1:256], ALU.subtract)\
                        .then_inc(V.sem, V.step(f"d{z}"))
                    nc.vector.tensor_scalar(o[:, 0:1].unsqueeze(1), src[:, :, 0:1], -1.0, None, ALU.mult)\
                        .then_inc(V.sem, V.step(f"n{z}"))
                    dve.wait_ge(V.sem, V.at(f"n{z}", i))
                    nc.vector.scalar_tensor_tensor(out=o.unsqueeze(1), in0=o.unsqueeze(1), scalar=col(MU_R + q), in1=src,
                                                   op0=ALU.mult, op1=ALU.add)\
                        .then_inc(V.sem, V.step(f"m{z}"))
                dve.wait_ge(V.sem, V.at("mv", i))
                nc.vector.tensor_scalar(kk, k, col(K_K), None, ALU.mult)\
                    .then_inc(V.sem, V.step("kk"))
                dve.wait_ge(A.sem, A.at("nrm", i))
                nc.vector.tensor_scalar(t1, t1, 1e-12, None, ALU.max)\
                    .then_inc(V.sem, V.step("max"))
                dve.wait_ge(V.sem, V.at("max", i))
                nc.vector.reciprocal(t1, t1)\
                    .then_inc(V.sem, V.step("rec"))
                dve.wait_ge(V.sem, V.at("rec", i))
                nc.vector.tensor_tensor(kk, kk, t1, ALU.mult)\
                    .then_inc(V.sem, V.step("kkn"))
                dve.wait_ge(V.sem, V.at("kkn", i))
                nc.vector.tensor_scalar(t1, a, -1.0, col(K_A), ALU.add, ALU.mult)\
                    .then_inc(V.sem, V.step("am1"))
                dve.wait_ge(V.sem, V.at("am1", i))
                nc.vector.scalar_tensor_tensor(out=k, in0=t1, scalar=1.0, in1=k,
                                               op0=ALU.add, op1=ALU.mult)\
                    .then_inc(V.sem, V.step("k2"))
                dve.wait_ge(V.sem, V.at("k2", i))
                nc.vector.tensor_scalar(enc, r, col(R_K), None, ALU.mult)\
                    .then_inc(V.sem, V.step("rk"))
                dve.wait_ge(V.sem, V.at("rk", i))
                nc.vector.tensor_tensor(enc, enc, k, ALU.mult)\
                    .then_inc(V.sem, V.step("rkk"))
                dve.wait_ge(T.sem, T.at("bon", i))
                nc.vector.tensor_tensor(fr["bon"], ps[:, 4, 0:256], v, ALU.mult)\
                    .then_inc(V.sem, V.step("bonus"))
                nc.vector.tensor_scalar(t1, ec, -DECAY, None, ALU.mult)\
                    .then_inc(V.sem, V.step("ld"))
                dve.wait_ge(V.sem, V.at("ld", i))
                nc.vector.tensor_tensor_scan(ec, c("reset"), t1, 0.0, ALU.mult, ALU.add)\
                    .then_inc(V.sem, V.step("cum"))
                dve.wait_ge(V.sem, V.at("cum", i))
                nc.vector.tensor_tensor(t1, ec, t1, ALU.subtract)\
                    .then_inc(V.sem, V.step("cb"))
                dve.wait_ge(A.sem, A.at("ec", i))
                spread(aq, 0, kk, t1, ("a0", "a1"))
                spread(aq, 128, r, ec, ("q0", "q1"))
                dve.wait_ge(V.sem, V.at("a1", i))
                nc.vector.tensor_tensor(kk, kk, a, ALU.mult)\
                    .then_inc(V.sem, V.step("ka"))
                dve.wait_ge(V.sem, V.at("ka", i))
                spread(bx, 0, kk, enc, ("b0", "b1"))
                spread(cx, 0, k, enc, ("c0", "c1"))
                spread(vx, 0, v, None, ("v0", "v1"))
                dve.wait_ge(T.sem, T.at("grams", i))
                nc.vector.tensor_tensor(fr["LT"], ps[:, 0:4, 0:128], mask("strict"), ALU.mult)\
                    .then_inc(V.sem, V.step("LT"))
                nc.vector.scalar_tensor_tensor(out=fr["BQ"], in0=ps[:, 0:4, 128:256], scalar=-1.0, in1=mask("incl"),
                                               op0=ALU.mult, op1=ALU.mult)\
                    .then_inc(V.sem, V.step("BQ"))
                nc.vector.tensor_tensor(fr["CA"], ps[:, 0:4, 256:384], mask("strict"), ALU.mult)\
                    .then_inc(V.sem, V.step("CA"))
                nc.vector.tensor_tensor(fr["CQ"], ps[:, 0:4, 384:512], mask("incl"), ALU.mult)\
                    .then_inc(V.sem, V.step("CQ"))
                nc.vector.tensor_tensor(fr["X"], ps[:, 4, :].rearrange("p (a b) -> p a b", a=NCH), mask("lev1t"), ALU.mult)\
                    .then_inc(V.sem, V.step("x0"))
                dve.wait_ge(V.sem, V.at("x0", i))
                nc.vector.tensor_tensor(fr["X"], mask("ident"), fr["X"], ALU.subtract)\
                    .then_inc(V.sem, V.step("x1"))
                nc.vector.tensor_tensor(fr["Y"], fr["LT"], mask("lev1"), ALU.mult)\
                    .then_inc(V.sem, V.step("y0"))
                dve.wait_ge(V.sem, V.at("y0", i))
                nc.vector.tensor_tensor(fr["Y"], mask("ident"), fr["Y"], ALU.subtract)\
                    .then_inc(V.sem, V.step("y1"))
                dve.wait_ge(T.sem, T.at("tr", i))
                nc.vector.tensor_tensor(bx, fr["LT"], mask(f"lev{lv[0]}"), ALU.mult)\
                    .then_inc(V.sem, V.step(f"M{lv[0]}"))
                nc.vector.tensor_tensor(cx, fr["LT"], mask(f"lev{lv[1]}"), ALU.mult)\
                    .then_inc(V.sem, V.step(f"M{lv[1]}"))
                for step, b in enumerate(lv):
                    dve.wait_ge(T.sem, T.at(f"dY{b}", i))
                    if b != lv[-1]:
                        nc.vector.tensor_tensor(fr["X"].rearrange(flat), fr["X"].rearrange(flat), ps[:, 1, :], ALU.subtract)\
                            .then_inc(V.sem, V.step(f"X{b}"))
                    nc.vector.tensor_tensor(fr["Y"].rearrange(flat), fr["Y"].rearrange(flat), ps[:, 2, :], ALU.subtract)\
                        .then_inc(V.sem, V.step(f"Y{b}"))
                    if step + 2 < len(lv):
                        nc.vector.tensor_tensor(Xv["M"][step % 2], fr["LT"], mask(f"lev{lv[step + 2]}"), ALU.mult)\
                            .then_inc(V.sem, V.step(f"M{lv[step + 2]}"))
                S = fr["S"]
                for n in range(NCH):
                    dve.wait_ge(T.sem, T.at(f"R{n}", i))
                    nc.vector.tensor_copy(fr["R"], ps[:, 3, 0:128])\
                        .then_inc(V.sem, V.step(f"R{n}"))
                    if n == NCH - 1:
                        break
                    dve.wait_ge(T.sem, T.at(f"y{n}", i))
                    end = ec[:, CHUNK * (n + 1) - 1:CHUNK * (n + 1)]
                    if n == 0:
                        nc.vector.tensor_scalar(S, ps[:, 6, 0:128], end, None, ALU.mult)\
                            .then_inc(V.sem, V.step("P0"))
                    else:
                        nc.vector.tensor_tensor(S, S, ps[:, 6, 0:128], ALU.add)\
                            .then_inc(V.sem, V.step(f"S{n}"))
                        dve.wait_ge(V.sem, V.at(f"S{n}", i))
                        nc.vector.tensor_scalar(S, S, end, None, ALU.mult)\
                            .then_inc(V.sem, V.step(f"P{n}"))
                dve.wait_ge(T.sem, T.at(f"y{NCH - 1}", i))
                y = ps[:, 5, :].rearrange("p (a b) -> p a b", a=NCH)
                for h in range(2):
                    r_ = slice(64 * h, 64 * h + 64)
                    nc.vector.tensor_copy(t1[r_].rearrange("p (a b) -> p a b", a=NCH), y[r_, :, r_])\
                        .then_inc(V.sem, V.step(f"ys{h}"))
                dve.wait_ge(T.sem, T.at("mean", i))
                nc.vector.scalar_tensor_tensor(out=ec, in0=ps[:, 0, 0:256], scalar=-1.0 / 64, in1=t1,
                                               op0=ALU.mult, op1=ALU.add)\
                    .then_inc(V.sem, V.step("yc"))
                dve.wait_ge(T.sem, T.at("var", i))
                nc.vector.tensor_scalar(t1, ps[:, 1, 0:256], 1.0 / 64, eps[:, 2:3], ALU.mult, ALU.add)\
                    .then_inc(V.sem, V.step("gvar"))
                dve.wait_ge(A.sem, A.at("root", i))
                nc.vector.reciprocal(t1, t1)\
                    .then_inc(V.sem, V.step("grec"))
                dve.wait_ge(V.sem, V.at("grec", i))
                nc.vector.tensor_tensor(ec, ec, t1, ALU.mult)\
                    .then_inc(V.sem, V.step("gn"))
                dve.wait_ge(V.sem, V.at("gn", i))
                nc.vector.tensor_scalar(ec, ec, col(LN_W), col(LN_B), ALU.mult, ALU.add)\
                    .then_inc(V.sem, V.step("gl"))
                dve.wait_ge(V.sem, V.at("gl", i))
                nc.vector.tensor_tensor(ec, ec, fr["bon"], ALU.add)\
                    .then_inc(V.sem, V.step("gb"))
                dve.wait_ge(V.sem, V.at("gb", i))
                nc.vector.tensor_tensor(og[:, bass.ds(8 + i, 1), 0:256], ec.unsqueeze(1), fr["g"].unsqueeze(1), ALU.mult)\
                    .then_inc(V.sem, V.step("gy"))
            repeat(dve, RW_TILES, body)

        SZ = phase("zp", v=" ".join(f"t{t}" for t in range(8)))
        fz = carve([("z", 24, 256), ("zs", 4, 256), ("vv", 8, 256), ("p", 4, 384), ("q", 4, 384), ("u", 4, 384),
                    ("fs", 4, 256)])

        def zp_pe(pe):
            pe.wait_ge(SW["v"].sem, SW["v"].at("gy", RW_TILES - 1))

            def body(i):
                for t in range(8):
                    if t % 2 == 0:
                        slot = (FIRST_UNIT["zp"] + t // 2) % RING
                        pe.wait_ge(unit_in[slot], loaded("zp", t // 2, i, 4))
                    if ran(i if t >= 4 else i - 1):
                        pe.wait_ge(SZ["v"].sem, SZ["v"].at(f"t{(t - 4) % 8}", i if t >= 4 else i - 1))
                    half(slot, t % 2, ps[:, t % 4, :], hT, SEQ).then_inc(half_done, 1)
            repeat(pe, 3, body)

        def zp_dve(dve):
            def body(i):
                for t in range(8):
                    dve.wait_ge(half_done, halves("zp", t // 2, t % 2, i, 4))
                    nc.vector.tensor_copy(fz["z"][:, bass.ds(8 * i + t, 1), :],
                                                       ps[:, t % 4:t % 4 + 1, 0:256])\
                        .then_inc(SZ["v"].sem, SZ["v"].step(f"t{t}"))
            repeat(dve, 3, body)

        H4 = range(4)
        ST = phase("attn_z",
                   a="va vb abs exp ln relu ew ya fabs fexp fln frelu " + " ".join(f"x{k}" for k in range(8)),
                   t="v0 v1 z logw ya f wt yb",
                   v="sq_a sq_b l m0 m1 fb fl cum ncum mx0 mx1 nb rr " + " ".join(f"n{k}" for k in range(8)) + " wt yb")
        z, u = fz["z"], fz["u"]
        zq_a, zk_a, zv_a, zq_b, zk_b, zv_b = (z[:, 4 * k:4 * k + 4, :] for k in range(6))
        fsm = zs[0:SB_HEADS, 3, :]
        F_MX, F_NB, F_RS, F_RR = 32, 40, 48, 56

        def attn_z_pe(pe):
            A, T, V = ST["a"], ST["t"], ST["v"]
            pe.wait_ge(SZ["v"].sem, SZ["v"].at("t7", 2))
            for k, zv in enumerate((zv_a, zv_b)):
                for h in H4:
                    for tok in range(2):
                        bank, at = 4 * k + h // 2, 256 * (h % 2) + 128 * tok
                        ins = nc.tensor.transpose(ps[:, bank, at:at + 128], zv[:, h, 128 * tok:128 * tok + 128],
                                                  c("ident"))
                ins\
                    .then_inc(T.sem, T.step(f"v{k}"))
            pe.wait_ge(V.sem, V.at("sq_b"))
            pe.wait_ge(A.sem, A.at("va"))
            for h in H4:
                mm(ps[:, h, 0:256], zk_a[:, h, 0:128], zq_a[:, h, :])
                ins = mm(ps[:, h, 256:384], zk_a[:, h, 128:256], zq_a[:, h, 128:256])
            ins\
                .then_inc(T.sem, T.step("z"))
            pe.wait_ge(A.sem, A.at("vb"))
            pe.wait_ge(V.sem, V.at("m1"))
            L = fz["p"]
            for h in H4:
                o = ps[:, 4 + h, :]
                mm(o[:, 0:256], zk_a[:, h, 0:128], zq_a[:, h, :], stop=False)
                mm(o[:, 0:256], c("tri"), L[:, h, 0:256], start=False, stop=False)
                mm(o[:, 128:256], c("ones"), L[:, h, 256:384], start=False, stop=False)
                mm(o[:, 0:128], c("ident"), c("not_after"), start=False)
                mm(o[:, 256:384], zk_a[:, h, 128:256], zq_a[:, h, 128:256], stop=False)
                mm(o[:, 256:384], c("tri"), L[:, h, 256:384], start=False, stop=False)
                ins = mm(o[:, 256:384], c("ident"), c("not_after"), start=False)
            ins\
                .then_inc(T.sem, T.step("logw"))
            pe.wait_ge(A.sem, A.at("ew"))
            W = fz["q"]
            for h in H4:
                o = ps[:, h, 0:256]
                mm(o, fz["vv"][:, h, 0:128], W[:, h, 0:256], stop=False)
                ins = mm(o[:, 128:256], fz["vv"][:, h, 128:256], W[:, h, 256:384], start=False)
            ins\
                .then_inc(T.sem, T.step("ya"))
            pe.wait_ge(V.sem, V.at("ncum"))
            cum, ncum = fz["fs"][0:4, 0, :], fz["fs"][0:4, 1, :]
            for h in H4:
                o = ps[:, 4 + h, :]
                sel = c("sel", 4)[:, 128 * h:128 * h + 128]
                mm(o[:, 0:128], zq_b[:, h, 0:128], zk_b[:, h, 0:128], stop=False)
                mm(o[:, 0:128], sel, ncum[:, 0:128], start=False, stop=False)
                mm(o[:, 0:128], cum[:, 0:128], sel, start=False, stop=False)
                mm(o[:, 0:128], c("ident"), c("future"), start=False)
                mm(o[:, 128:384], zq_b[:, h, 128:256], zk_b[:, h, :], stop=False)
                mm(o[:, 128:384], sel, ncum, start=False, stop=False)
                for k in range(2):
                    mm(o[:, 128 + 128 * k:256 + 128 * k], cum[:, 128:256], sel, start=False, stop=False)
                ins = mm(o[:, 256:384], c("ident"), c("future"), start=False)
            ins\
                .then_inc(T.sem, T.step("f"))
            pe.wait_ge(V.sem, V.at("n7"))
            pe.wait_ge(A.sem, A.at("ya"))
            pr = fz["p"]
            for h in H4:
                nc.tensor.transpose(ps[:, h, 0:128], pr[:, h, 0:128], c("ident"))
                nc.tensor.transpose(ps[:, h, 128:256], pr[:, h, 128:256], c("ident"))
                ins = nc.tensor.transpose(ps[:, h, 256:384], pr[:, h, 256:384], c("ident"))
            ins\
                .then_inc(T.sem, T.step("wt"))
            pe.wait_ge(V.sem, V.at("wt"))
            W = fz["q"]
            for h in H4:
                o = ps[:, 4 + h, 0:256]
                mm(o, fz["vv"][:, 4 + h, 0:128], W[:, h, 0:256], stop=False)
                ins = mm(o[:, 128:256], fz["vv"][:, 4 + h, 128:256], W[:, h, 256:384], start=False)
            ins\
                .then_inc(T.sem, T.step("yb"))

        def attn_z_act(act):
            A, T, V = ST["a"], ST["t"], ST["v"]
            act.wait_ge(T.sem, T.at("v0"))
            vv = fz["vv"]
            nc.scalar.activation(vv[:, 0:4, :], ps[:, 0:2, :].rearrange("p a (b c) -> p (a b) c", b=2),
                                        ACT.Copy)\
                .then_inc(A.sem, A.step("va"))
            act.wait_ge(T.sem, T.at("v1"))
            nc.scalar.activation(vv[:, 4:8, :], ps[:, 4:6, :].rearrange("p a (b c) -> p (a b) c", b=2),
                                        ACT.Copy)\
                .then_inc(A.sem, A.step("vb"))
            zz = ps[:, 0:4, 0:384]
            act.wait_ge(T.sem, T.at("z"))
            nc.scalar.activation(fz["q"], zz, ACT.Abs)\
                .then_inc(A.sem, A.step("abs"))
            act.wait_ge(A.sem, A.at("abs"))
            nc.scalar.activation(fz["q"], fz["q"], ACT.Exp, scale=-1.0)\
                .then_inc(A.sem, A.step("exp"))
            act.wait_ge(A.sem, A.at("exp"))
            nc.scalar.activation(fz["q"], fz["q"], ACT.Ln, bias=eps[:, 3:4])\
                .then_inc(A.sem, A.step("ln"))
            nc.scalar.activation(u, zz, ACT.Relu)\
                .then_inc(A.sem, A.step("relu"))
            act.wait_ge(T.sem, T.at("logw"))
            act.wait_ge(V.sem, V.at("l"))
            nc.scalar.activation(fz["q"], ps[:, 4:8, 0:384], ACT.Exp)\
                .then_inc(A.sem, A.step("ew"))
            act.wait_ge(T.sem, T.at("ya"))
            nc.scalar.activation(og[:, 0:4, 0:256], ps[:, 0:4, 0:256], ACT.Copy)\
                .then_inc(A.sem, A.step("ya"))
            f = fz["fs"]
            act.wait_ge(V.sem, V.at("fb"))
            nc.scalar.activation(f[0:4, 2, :], f[0:4, 0, :], ACT.Abs)\
                .then_inc(A.sem, A.step("fabs"))
            act.wait_ge(A.sem, A.at("fabs"))
            nc.scalar.activation(f[0:4, 2, :], f[0:4, 2, :], ACT.Exp, scale=-1.0)\
                .then_inc(A.sem, A.step("fexp"))
            act.wait_ge(A.sem, A.at("fexp"))
            nc.scalar.activation(f[0:4, 2, :], f[0:4, 2, :], ACT.Ln, bias=eps[0:4, 3:4])\
                .then_inc(A.sem, A.step("fln"))
            nc.scalar.activation(f[0:4, 3, :], f[0:4, 0, :], ACT.Relu, scale=-1.0)\
                .then_inc(A.sem, A.step("frelu"))
            act.wait_ge(V.sem, V.at("nb"))
            for h in H4:
                for k, s_ in enumerate((slice(0, 128), slice(128, 384))):
                    q = 4 * k + h
                    nc.scalar.activation(fz["p"][:, h, s_], ps[:, 4 + h, s_], ACT.Exp,
                                                bias=st[:, F_NB + q:F_NB + q + 1],
                                                accum_out=st[:, F_RS + q:F_RS + q + 1])\
                        .then_inc(A.sem, A.step(f"x{2 * h + k}"))

        def attn_z_dve(dve):
            A, T, V = ST["a"], ST["t"], ST["v"]
            flat = "p a b -> p (a b)"
            L, f = fz["p"], fz["fs"]
            dve.wait_ge(SZ["v"].sem, SZ["v"].at("t7", 2))
            nc.vector.tensor_scalar(zq_a, zq_a, SCALE_Z, None, ALU.mult)\
                .then_inc(V.sem, V.step("sq_a"))
            nc.vector.tensor_scalar(zq_b, zq_b, SCALE_Z, None, ALU.mult)\
                .then_inc(V.sem, V.step("sq_b"))
            dve.wait_ge(A.sem, A.at("relu"))
            nc.vector.scalar_tensor_tensor(out=L.rearrange(flat), in0=fz["q"].rearrange(flat), scalar=-1.0,
                                                  in1=u.rearrange(flat), op0=ALU.mult, op1=ALU.subtract)\
                .then_inc(V.sem, V.step("l"))
            dve.wait_ge(V.sem, V.at("l"))
            after = c("after").unsqueeze(1).to_broadcast([128, 4, 128])
            nc.vector.tensor_tensor(L[:, :, 0:128], L[:, :, 0:128], after, ALU.mult)\
                .then_inc(V.sem, V.step("m0"))
            nc.vector.tensor_tensor(L[:, :, 256:384], L[:, :, 256:384], after, ALU.mult)\
                .then_inc(V.sem, V.step("m1"))
            nc.vector.tensor_scalar(f[0:4, 0, :], fsm, p("bf", 0, 4), None, ALU.add)\
                .then_inc(V.sem, V.step("fb"))
            dve.wait_ge(A.sem, A.at("frelu"))
            nc.vector.scalar_tensor_tensor(out=f[0:4, 1, :], in0=f[0:4, 2, :], scalar=-1.0, in1=f[0:4, 3, :],
                                                  op0=ALU.mult, op1=ALU.subtract)\
                .then_inc(V.sem, V.step("fl"))
            dve.wait_ge(V.sem, V.at("fl"))
            nc.vector.tensor_tensor_scan(f[0:4, 0, :], c("ones", 4)[:, 0:1].to_broadcast([4, 256]),
                                                f[0:4, 1, :], 0.0, ALU.mult, ALU.add)\
                .then_inc(V.sem, V.step("cum"))
            dve.wait_ge(V.sem, V.at("cum"))
            nc.vector.tensor_scalar(f[0:4, 1, :], f[0:4, 0, :], -1.0, None, ALU.mult)\
                .then_inc(V.sem, V.step("ncum"))
            dve.wait_ge(T.sem, T.at("f"))
            nc.vector.tensor_reduce(st[:, F_MX:F_MX + 4], ps[:, 4:8, 0:128], AX.X, ALU.max)\
                .then_inc(V.sem, V.step("mx0"))
            nc.vector.tensor_reduce(st[:, F_MX + 4:F_MX + 8], ps[:, 4:8, 128:384], AX.X, ALU.max)\
                .then_inc(V.sem, V.step("mx1"))
            dve.wait_ge(V.sem, V.at("mx1"))
            nc.vector.tensor_scalar(st[:, F_NB:F_NB + 8], st[:, F_MX:F_MX + 8], -1.0, None, ALU.mult)\
                .then_inc(V.sem, V.step("nb"))
            dve.wait_ge(A.sem, A.at("x7"))
            nc.vector.reciprocal(st[:, F_RR:F_RR + 8], st[:, F_RS:F_RS + 8])\
                .then_inc(V.sem, V.step("rr"))
            dve.wait_ge(V.sem, V.at("rr"))
            for h in H4:
                for k, s_ in enumerate((slice(0, 128), slice(128, 384))):
                    q = 4 * k + h
                    w_ = fz["p"][:, h, s_]
                    nc.vector.tensor_scalar(w_, w_, st[:, F_RR + q:F_RR + q + 1], None, ALU.mult)\
                        .then_inc(V.sem, V.step(f"n{2 * h + k}"))
            dve.wait_ge(T.sem, T.at("wt"))
            nc.vector.tensor_copy(fz["q"], ps[:, 0:4, 0:384])\
                .then_inc(V.sem, V.step("wt"))
            dve.wait_ge(T.sem, T.at("yb"))
            nc.vector.tensor_copy(og[:, 4:8, 0:256], ps[:, 4:8, 0:256])\
                .then_inc(V.sem, V.step("yb"))

        SM = phase("mix", a="sg0 sg1 sg2 sg3 sg4 sg5", v="ma0 mb0 mc0 s0 o0 ma1 mb1 mc1 s1 o1")
        fm = carve([("m", KT, 256), ("sg", 6, 256), ("ta", 2, 256), ("tb", 2, 256), ("tc", 2, 256)])
        BANK = ((2, 3, 0), (1, 2, 3))

        def mix_pe(pe):
            A, V = SM["a"], SM["v"]
            pe.wait_ge(ST["v"].sem, ST["v"].at("yb"))
            pe.wait_ge(ST["a"].sem, ST["a"].at("x7"))

            def body(i):
                for t in range(6):
                    if t % 2 == 0:
                        slot = (FIRST_UNIT["mix"] + t // 2) % RING
                        pe.wait_ge(unit_in[slot], loaded("mix", t // 2, i, 4))
                    if t < 4:
                        if ran(i - 1):
                            pe.wait_ge(V.sem, V.at(("mc0", "ma1", "mb1", "mc1")[t], i - 1))
                    else:
                        pe.wait_ge(A.sem, A.at(f"sg{t - 4}", i))
                    half(slot, t % 2, ps[:, t % 4, :], hT, SEQ).then_inc(half_done, 1)
                slot = (FIRST_UNIT["mix"] + 3) % RING
                pe.wait_ge(unit_in[slot], loaded("mix", 3, i, 4))
                for jj in range(2):
                    for k, kts in enumerate((range(0, 4), range(4, 8), range(8, 16))):
                        if jj == 1 and k:
                            pe.wait_ge(V.sem, V.at(("", "ma0", "mb0")[k], i))
                        else:
                            pe.wait_ge(A.sem, A.at(f"sg{2 + k + 3 * jj}", i))
                        ins = half(slot, jj, ps[:, BANK[jj][k], :], og, SEQ, kts=kts)
                        if k == 2:
                            ins.then_inc(half_done, 1)
            repeat(pe, 8, body)

        def mix_act(act):
            def body(i):
                for t in range(6):
                    act.wait_ge(half_done, halves("mix", t // 2, t % 2, i, 4))
                    if ran(i - 1):
                        act.wait_ge(SM["v"].sem, SM["v"].at("mc1", i - 1))
                    nc.scalar.activation(fm["sg"][:, t, :], ps[:, t % 4, 0:256], ACT.Sigmoid)\
                        .then_inc(SM["a"].sem, SM["a"].step(f"sg{t}"))
            repeat(act, 8, body)

        def mix_dve(dve):
            V = SM["v"]

            def body(i):
                for jj in range(2):
                    dve.wait_ge(half_done, halves("mix", 3, jj, i, 4))
                    dve.wait_ge(SM["a"].sem, SM["a"].at("sg5", i))
                    for k, n in enumerate("abc"):
                        nc.vector.tensor_tensor(fm["t" + n][:, jj, :], ps[:, BANK[jj][k], 0:256],
                                                       fm["sg"][:, 2 * k + jj, :], ALU.mult)\
                            .then_inc(V.sem, V.step(f"m{n}{jj}"))
                    dve.wait_ge(V.sem, V.at(f"mc{jj}", i))
                    ta = fm["ta"][:, jj:jj + 1, :]
                    nc.vector.tensor_tensor(ta, ta, fm["tb"][:, jj:jj + 1, :], ALU.add)\
                        .then_inc(V.sem, V.step(f"s{jj}"))
                    dve.wait_ge(V.sem, V.at(f"s{jj}", i))
                    nc.vector.tensor_tensor(fm["m"][:, bass.ds(2 * i + jj, 1), :], ta,
                                                   fm["tc"][:, jj:jj + 1, :], ALU.add)\
                        .then_inc(V.sem, V.step(f"o{jj}"))
            repeat(dve, 8, body)

        mix_out = Product("mix_out", "mix_out", fm["m"], SEQ, og, add=False)
        norm_post = Norm("norm_post", og, SEQ, 1, [("mix_post", og)], residual=xT)
        norm_mlp = Norm("norm_mlp", xT, SEQ, 1, [("mlp_pre", hT)])

        SU = phase("up", a=" ".join(f"t{t}" for t in range(8)), v=" ".join(f"t{t}" for t in range(8)))
        SD = phase("down", v="t0 t1 t2 t3")
        fu = carve([("h", FF_TILES, 256), ("r", 4, 256)])

        def up_pe(pe):
            pe.wait_ge(norm_mlp.V.sem, norm_mlp.V.at(norm_mlp.last))

            def body(i):
                for t in range(8):
                    if t % 2 == 0:
                        slot = (FIRST_UNIT["up"] + t // 2) % RING
                        pe.wait_ge(unit_in[slot], loaded("up", t // 2, i, 4))
                    if ran(i if t >= 4 else i - 1):
                        pe.wait_ge(SU["a"].sem, SU["a"].at(f"t{(t - 4) % 8}", i if t >= 4 else i - 1))
                    half(slot, t % 2, ps[:, t % 4, :], hT, SEQ).then_inc(half_done, 1)
            repeat(pe, 8, body)

        def up_act(act):
            def body(i):
                for t in range(8):
                    act.wait_ge(half_done, halves("up", t // 2, t % 2, i, 4))
                    if ran(i if t >= 4 else i - 1):
                        act.wait_ge(SU["v"].sem, SU["v"].at(f"t{(t - 4) % 8}", i if t >= 4 else i - 1))
                    nc.scalar.activation(fu["r"][:, t % 4, :], ps[:, t % 4, 0:256], ACT.Relu)\
                        .then_inc(SU["a"].sem, SU["a"].step(f"t{t}"))
            repeat(act, 8, body)

        def up_dve(dve):
            def body(i):
                for t in range(8):
                    dve.wait_ge(SU["a"].sem, SU["a"].at(f"t{t}", i))
                    r_ = fu["r"][:, t % 4:t % 4 + 1, :]
                    nc.vector.tensor_tensor(fu["h"][:, bass.ds(8 * i + t, 1), :], r_, r_, ALU.mult)\
                        .then_inc(SU["v"].sem, SU["v"].step(f"t{t}"))
            repeat(dve, 8, body)

        def down_pe(pe):
            pe.wait_ge(SU["v"].sem, SU["v"].at("t7", 7))
            pe.wait_ge(SU["a"].sem, SU["a"].at("t7", 7))

            def body(i):
                for g in range(2):
                    for kb in range(4):
                        slot = (FIRST_UNIT["down"] + 4 * g + kb) % RING
                        pe.wait_ge(unit_in[slot], loaded("down", 4 * g + kb, i, 8))
                        for h in range(2):
                            if kb == 0:
                                if ran(i - 1):
                                    pe.wait_ge(SD["v"].sem, SD["v"].at(f"t{2 * g + h}", i - 1))
                            half(slot, h, ps[:, 2 * g + h, :], fu["h"], SEQ, k0=16 * kb, first=(kb == 0),
                                 last=(kb == 3)).then_inc(half_done, 1)
            repeat(pe, 4, body)

        def down_dve(dve):
            def body(i):
                for t in range(4):
                    dve.wait_ge(half_done, halves("down", 4 * (t // 2) + 3, t % 2, i, 8))
                    nc.vector.tensor_copy(og[:, bass.ds(4 * i + t, 1), 0:256], ps[:, t:t + 1, 0:256])\
                        .then_inc(SD["v"].sem, SD["v"].step(f"t{t}"))
            repeat(dve, 4, body)

        norm_out = Norm("norm_out", og, SEQ, 1, [("mlp_post", og)], residual=xT)

        block = ctx.enter_context(nc.Block())

        @block.sync
        def _(sp):
            sp.dma_start(xT[:, :, :], x).then_inc(x_in, 16)
            sp.dma_start(C[:, :], consts).then_inc(cp_in, 16)
            sp.dma_start(P[:, :], params).then_inc(cp_in, 16)

            def load(m, slot):
                sp.dma_start(ring[:, slot, :, :].rearrange("p a b -> p (a b)").unsqueeze(1),
                             w[:, bass.ds(m, 1), :]).then_inc(unit_in[slot], 16)
            for m in range(RING):
                load(m, m)
            turns = (N_UNITS - RING) // RING
            with sp.Fori(0, turns) as i:
                for s in range(RING):
                    sp.wait_ge(half_done, 2 * RING * i + 2 * s + 2)
                    load(RING * i + RING + s, s)
            for m in range(RING * (turns + 1), N_UNITS):
                sp.wait_ge(half_done, 2 * (m - RING) + 2)
                load(m, m % RING)
            sp.wait_ge(norm_out.V.sem, norm_out.V.at(norm_out.last))
            sp.dma_start(out, xT[:, :, 0:SEQ]).then_inc(out_in, 16)
            sp.wait_ge(out_in, 16)

        @block.scalar
        def _(act):
            act.wait_ge(x_in, 16)
            norm_a.act(act)
            lam_act(act)
            attn_a_act(act)
            act.wait_ge(a_out.V.sem, a_out.V.at("t7", 1))
            norm_b.act(act)
            kv_act(act)
            attn_b_act(act)
            act.wait_ge(b_out.V.sem, b_out.V.at("t7", 1))
            norm_fin.act(act)
            act.wait_ge(norm_fin.V.sem, norm_fin.V.at(norm_fin.last))
            norm_mix.act(act)
            rw_in_act(act)
            rwkv_act(act)
            attn_z_act(act)
            mix_act(act)
            act.wait_ge(mix_out.V.sem, mix_out.V.at("t7", 1))
            norm_post.act(act)
            act.wait_ge(norm_post.V.sem, norm_post.V.at(norm_post.last))
            norm_mlp.act(act)
            up_act(act)
            act.wait_ge(SD["v"].sem, SD["v"].at("t3", 3))
            norm_out.act(act)

        @block.vector
        def _(dve):
            for k, value in enumerate((1e-5, 1e-6, 64e-5, 1.0)):
                nc.vector.memset(eps[:, k:k + 1], value).then_inc(eps_set, 1)
            nc.vector.memset(st[:, :], 1.0).then_inc(eps_set, 1)
            dve.wait_ge(eps_set, 5)
            dve.wait_ge(cp_in, 32)
            norm_a.dve(dve)
            lam_dve(dve)
            attn_a_dve(dve)
            a_out.dve(dve)
            dve.wait_ge(a_out.V.sem, a_out.V.at("t7", 1))
            norm_b.dve(dve)
            kv_dve(dve)
            attn_b_dve(dve)
            b_out.dve(dve)
            dve.wait_ge(b_out.V.sem, b_out.V.at("t7", 1))
            norm_fin.dve(dve)
            dve.wait_ge(norm_fin.V.sem, norm_fin.V.at(norm_fin.last))
            norm_mix.dve(dve)
            rw_in_dve(dve)
            rwkv_dve(dve)
            zp_dve(dve)
            attn_z_dve(dve)
            mix_dve(dve)
            mix_out.dve(dve)
            dve.wait_ge(mix_out.V.sem, mix_out.V.at("t7", 1))
            norm_post.dve(dve)
            dve.wait_ge(norm_post.V.sem, norm_post.V.at(norm_post.last))
            norm_mlp.dve(dve)
            up_dve(dve)
            down_dve(dve)
            dve.wait_ge(SD["v"].sem, SD["v"].at("t3", 3))
            norm_out.dve(dve)

        @block.tensor
        def _(pe):
            pe.wait_ge(cp_in, 32)
            norm_a.pe(pe)
            lam_pe(pe)
            attn_a_pe(pe)
            pe.wait_ge(SA["v"].sem, SA["v"].at("og1", HEADS_A - 1))
            a_out.pe(pe)
            norm_b.pe(pe)
            kv_pe(pe)
            attn_b_pe(pe)
            pe.wait_ge(SB["v"].sem, SB["v"].at("o3", GROUPS_B - 1))
            b_out.pe(pe)
            norm_fin.pe(pe)
            norm_mix.pe(pe)
            rw_in_pe(pe)
            rwkv_pe(pe)
            zp_pe(pe)
            attn_z_pe(pe)
            mix_pe(pe)
            pe.wait_ge(SM["v"].sem, SM["v"].at("o1", 7))
            mix_out.pe(pe)
            norm_post.pe(pe)
            norm_mlp.pe(pe)
            up_pe(pe)
            down_pe(pe)
            norm_out.pe(pe)


def constants():
    q = np.arange(128)
    same = (q[:, None] // 64) == (q[None, :] // 64)
    col, row = q[None, :], q[:, None]
    t = {
        "ident": np.eye(128), "ones": np.ones((128, 128)), "hones": same, "tri": row >= col,
        "after": col > row, "not_after": np.where(col <= row, NEG, 0), "future": np.where(col > row, NEG, 0),
        "strict": same & (row < col), "incl": same & (row <= col),
    }
    for b in LEVELS:
        t[f"lev{b}"] = (row // (2 * b) == col // (2 * b)) & ((row // b) % 2 == 0) & ((col // b) % 2 == 1)
    t["lev1t"] = t["lev1"].T
    t["reset"] = np.broadcast_to(np.arange(256) % 64 != 0, (128, 256))
    pos = np.concatenate([np.arange(SEQ) + META, np.arange(META)]).astype(np.float32)
    for name, dim in (("a", 32), ("b", 16)):
        inv = np.float32(ROPE_THETA) ** (-np.arange(0, dim, 2, dtype=np.float32) / np.float32(dim))
        ang = (pos[None, :] * inv[:, None]).astype(np.float32)
        cos, sin = np.ones((128, NT)), np.zeros((128, NT))
        for r in range(0, 128, 64 if name == "b" else 128):
            half = dim // 2
            cos[r:r + half] = cos[r + half:r + dim] = np.cos(ang)
            sin[r:r + half], sin[r + half:r + dim] = -np.sin(ang), np.sin(ang)
        t[f"cos_{name}"], t[f"sin_{name}"] = cos, sin
    t["low"] = np.broadcast_to(q < 64, (128, 128))
    t["high"] = np.broadcast_to(q >= 64, (128, 128))
    t["neg"] = np.full((128, 64), NEG)
    t["sel"] = np.repeat(np.eye(128)[:, 0:4], 128, axis=1)
    c = np.zeros((128, C_N), np.float32)
    for name, (a, b) in C_AT.items():
        c[:, a:b] = t[name]
    return c


def lay_out(w):
    units = np.empty((128, N_UNITS, UNIT), np.float32)
    n = 0

    def put(m):
        nonlocal n
        u = units[:, n].reshape(128, 16, 256)
        c = m.shape[1]
        u[:, :, 0:c] = m.reshape(16, 128, c).transpose(1, 0, 2)
        u[:, :, c:] = 0
        n += 1

    a, b, z = w["a_w_in"][0], w["b_w_in"][0], w["w_in_2"][0]
    for h in range(HEADS_A):
        for part in range(4):
            put(a[:, D * part + 256 * h:D * part + 256 * h + 256])
    for g in range(8):
        put(w["a_w_out"][0][:, 256 * g:256 * g + 256])
    for g in range(2):
        put(w["w_kv"][:, 256 * g:256 * g + 256])
    for g in range(GROUPS_B):
        for part in range(2):
            for k in range(2):
                c = D * part + 512 * g + 256 * k
                put(b[:, c:c + 256])
    for g in range(8):
        put(w["b_w_out"][0][:, 256 * g:256 * g + 256])
    for g in range(12):
        put(z[:, IN_R + 256 * g:IN_R + 256 * g + 256])
    wa, gates = IN_R + 3072, IN_R + 3072 + 288
    put(np.concatenate([z[:, wa:wa + 128], z[:, 3072:3076]], axis=1))
    put(z[:, wa + 128:wa + 288])
    lora = np.zeros((128, UNIT), np.float32)
    lora[0:64, 0:1024] = w["rwkv_w_up_2"][0]
    lora[64:128, 0:1024] = w["rwkv_a_up_2"][0]
    lora[:, 1024:2048] = w["rwkv_g_up_2"][0][0:128]
    lora[0:32, 2048:3072] = w["rwkv_g_up_2"][0][128:160]
    units[:, n] = lora
    n += 1
    for g in range(12):
        put(z[:, 256 * g:256 * g + 256])
    for g in range(8):
        for part in range(3):
            c = gates + D * part + 256 * g
            put(z[:, c:c + 256])
        put(np.concatenate([w[f"w_branch_{k}_2"][0][:, 256 * g:256 * g + 256] for k in "abc"]))
    for g in range(8):
        put(w["w_out_2"][0][:, 256 * g:256 * g + 256])
    for g in range(32):
        put(w["w_mlp_up_2"][0][:, 256 * g:256 * g + 256])
    for g in range(8):
        for kb in range(4):
            put(w["w_mlp_down_2"][0][2048 * kb:2048 * kb + 2048, 256 * g:256 * g + 256])
    assert n == N_UNITS

    p = np.zeros((128, P_N), np.float32)

    def cols(name, v, k=0):
        v = np.asarray(v).reshape(-1)
        rows = min(128, len(v))
        v = v.reshape(-1, rows).T
        p[0:rows, P_AT[name][0] + k:P_AT[name][0] + k + v.shape[1]] = v

    for name, key in (("a", "a_norm"), ("kv", "kv_norm"), ("b", "b_norm"), ("fin", "final_norm"),
                      ("mix_pre", "norm_mix_pre_2"), ("mix_post", "norm_mix_post_2"),
                      ("mlp_pre", "norm_mlp_pre_2"), ("mlp_post", "norm_mlp_post_2")):
        cols(name, w[key])
    for k, key in enumerate(("q1", "k1", "q2", "k2")):
        cols("lam", w["a_lambda_" + key], k)
    cols("subln", w["a_subln"])
    p[:, P_AT["sinks"][0]:P_AT["sinks"][1]] = w["b_sinks"].reshape(1, -1)
    mu = w["rwkv_mu_2"][0]
    cols("mu_wa", mu[3072:3200])
    cols("mu_g", mu[3200:3328])
    cols("mu_g", mu[3328:3360], 1)
    cols("bf", w["b_forget_2"])
    for j in range(RW_TILES):
        f = slice(128 * j, 128 * j + 128)
        parts = [mu[0:1024], mu[1024:2048], mu[2048:3072]] + [
            w[f"rwkv_{k}_2"].reshape(-1) for k in ("w0", "a0", "k_k", "k_a", "r_k", "ln_w", "ln_b")]
        for k, v in enumerate(parts):
            cols("rw", v[f], 10 * j + k)
    return units, p


def kernel(**inputs):
    import concourse.bacc as _bacc
    from concourse.bass_utils import run_bass_kernel_spmd as _run

    w = {k: np.asarray(v) for k, v in inputs.items()}
    units, p = lay_out(w)
    x = np.concatenate([w["x"][0], w["meta_tokens"]]).T.reshape(KT, 128, NT).transpose(1, 0, 2)
    arrays = {"weights": units, "tokens": np.ascontiguousarray(x), "params": p, "consts": constants()}
    nc = _bacc.Bacc("TRN2", target_bir_lowering=False, num_devices=1)
    args = [nc.dram_tensor(n, a.shape, F32, kind="ExternalInput").ap() for n, a in arrays.items()]
    out = nc.dram_tensor("out", [128, KT, SEQ], F32, kind="ExternalOutput").ap()
    build(nc, *args, out)
    r = _run(nc, [arrays], core_ids=[0]).results[0]["out"]
    return np.ascontiguousarray(r.transpose(2, 1, 0)).reshape(1, SEQ, D)
```

```python
from contextlib import ExitStack

import concourse.bass as bass
import numpy as np
from concourse import mybir

ALU = mybir.AluOpType
ACT = mybir.ActivationFunctionType
F32 = mybir.dt.float32
F32R = mybir.dt.float32r
AX = mybir.AxisListType

D = 2048
SEQ = 256
META = 16
NT = SEQ + META
KT = D // 128
CHUNK = 64
TILE = 16 * 128
NEG = -1e30
HEADS_A = 8
GROUPS_B = 4
SB_HEADS = 4
RW_TILES = 8
FF_TILES = 64
ROPE_THETA = 500000.0
SCALE_A = 128 ** -0.5
SCALE_B = 64 ** -0.5
SCALE_Z = 128 ** -0.5
LAMBDA_INIT = 0.8 - 0.6
DECAY = float(np.exp(-0.5))
IN_R = 3076

TILES = [("a", 8 * HEADS_A), ("a_out", 16), ("kv", 4), ("b", 8 * GROUPS_B), ("b_out", 16), ("rw", 24),
         ("small", 4), ("zp", 24), ("mix", 64), ("mix_out", 16), ("mlp", 2 * FF_TILES)]
FIRST = {}
for _name, _n in TILES:
    FIRST[_name] = sum(n for _, n in TILES[:len(FIRST)])
N_TILES = sum(n for _, n in TILES)


def columns(sizes):
    at, n = {}, 0
    for name, size in sizes:
        at[name] = (n, n + size)
        n += size
    return at, n


P_AT, P_N = columns([(g, KT) for g in ("a", "kv", "b", "fin", "mix_pre", "mix_post", "mlp_pre", "mlp_post")]
                    + [("lam", 4), ("subln", 2), ("sinks", 32), ("mu_wa", 1), ("mu_g", 2), ("bf", 1),
                       ("rw", 10 * RW_TILES)])
MU_R, MU_K, MU_V, W0, A0, K_K, K_A, R_K, LN_W, LN_B = range(10)
LEVELS = (1, 2, 4, 8, 16, 32)
C_AT, C_N = columns([("ident", 128), ("ones", 128), ("hones", 128), ("tri", 128), ("after", 128),
                     ("not_after", 128), ("future", 128), ("strict", 128), ("incl", 128), ("lev1t", 128)]
                    + [(f"lev{b}", 128) for b in LEVELS]
                    + [("reset", 256), ("cos_a", NT), ("sin_a", NT), ("cos_b", NT), ("sin_b", NT),
                       ("low", 128), ("high", 128), ("neg", 64), ("sel", 4 * 128)])


class Steps:

    def __init__(self, sem, names):
        self.sem, self.per = sem, len(names)
        self.at_ = {n: k + 1 for k, n in enumerate(names)}
        assert len(self.at_) == self.per
        self.now = 0

    def step(self, name):
        self.now += 1
        if self.at_[name] != self.now:
            raise ValueError(f"step {name} out of order, at {self.now}")
        self.now %= self.per
        return 1

    def at(self, name, i=0):
        return self.at_[name] + self.per * i


def ran(i):
    return not isinstance(i, int) or i >= 0


def repeat(eng, n, body):
    body(0)
    if n > 1:
        with eng.Fori(1, n) as i:
            body(i)


def build(nc, w, x, params, consts, lora, out):
    with ExitStack() as ctx:
        def sb(name, shape, dtype=F32):
            return ctx.enter_context(nc.sbuf_tensor(name, shape, dtype))

        def sem(name):
            return ctx.enter_context(nc.semaphore(name))

        raw = sb("raw", [128, 4, 8, 128])
        wh, wl = sb("wh", [128, 2, 16, 128], F32R), sb("wl", [128, 2, 16, 128], F32R)
        C = sb("C", [128, C_N])
        P = sb("P", [128, P_N])
        xT = sb("xT", [128, KT, NT])
        hh, hl = sb("hh", [128, KT, NT], F32R), sb("hl", [128, KT, NT], F32R)
        og = sb("og", [128, KT, NT])
        st = sb("st", [128, 64])
        eps = sb("eps", [128, 4])
        ARENA = nc.sbuf_bytes_remaining // 4 - 8
        with nc.sbuf_tensor("arena", [128, ARENA], F32) as arena:
            pass
        gh, gl = sb("gh", [128, KT, SEQ], F32R), sb("gl", [128, KT, SEQ], F32R)
        PAIR = 2 * KT * SEQ
        ps = ctx.enter_context(nc.psum_tensor("ps", [128, 8, 512], F32))

        def c(name, rows=128):
            a, b = C_AT[name]
            return C[0:rows, a:b]

        def p(name, k=0, rows=128):
            return P[0:rows, P_AT[name][0] + k:P_AT[name][0] + k + 1]

        def carve(sizes):
            got, at = {}, 0
            for name, *shape in sizes:
                n = int(np.prod(shape))
                v = arena[:, at:at + n]
                if len(shape) == 2:
                    v = v.rearrange("p (a b) -> p a b", a=shape[0])
                got[name] = v
                at += n
            if at > ARENA:
                raise ValueError(f"arena: {at} of {ARENA}")
            return got

        raw_in = [sem(f"raw_in{s}") for s in range(2)]
        hi_done, lo_done, tile_done = sem("hi_done"), sem("lo_done"), sem("tile_done")
        lora_in = sem("lora_in")
        x_in, cp_in, out_in = sem("x_in"), sem("cp_in"), sem("out_in")
        eps_set = sem("eps_set")

        def phase(name, **steps):
            return {e: Steps(sem(f"{name}_{e}"), s.split()) for e, s in steps.items()}

        def done(phase_name, t, i=0, per=0):
            return FIRST[phase_name] + t + 1 + per * i

        def round_weights(act, phase_name, t, i=0, per=0):
            m = FIRST[phase_name] + t
            if m >= N_TILES:
                return
            act.wait_ge(raw_in[m % 2], 32 * (m // 2 + 1) + 16 * per * i)
            if m >= 2:
                act.wait_ge(tile_done, m - 1 + per * i)
            nc.scalar.activation(wh[:, m % 2, :, :].rearrange("p a b -> p (a b)"),
                                 raw[:, 2 * (m % 2):2 * (m % 2) + 2, :, :].rearrange("p a b c -> p (a b c)"),
                                 ACT.Copy)\
                .then_inc(hi_done, 1)

        def tile(pe, phase_name, t, i, per, parts, n, m=128):
            q = FIRST[phase_name] + t
            slot = q % 2
            pe.wait_ge(hi_done, q + 1 + per * i)
            for acc, rh, rl, kts in parts:
                for kt in kts:
                    nc.tensor.matmul(acc[0:m, 0:n], wh[:, slot, kt, 0:m], rh[:, kt, 0:n],
                                     start=(kt == kts[0]), stop=False)
                    nc.tensor.matmul(acc[0:m, 0:n], wh[:, slot, kt, 0:m], rl[:, kt, 0:n],
                                     start=False, stop=False)
            for acc, rh, rl, kts in parts:
                for kt in kts:
                    if kt % 8 == 0:
                        pe.wait_ge(lo_done, 2 * q + kt // 8 + 1 + 2 * per * i)
                    ins = nc.tensor.matmul(acc[0:m, 0:n], wl[:, slot, kt, 0:m], rh[:, kt, 0:n],
                                           start=False, stop=(kt == kts[-1]))
            return ins

        ALL = range(KT)

        def mm(o, lhsT, rhs, start=True, stop=True):
            return nc.tensor.matmul(o, lhsT, rhs, start=start, stop=stop)

        class Split:
            def __init__(self, name, src, pair, n, gate=None):
                self.src, self.pair, self.n = src, pair, n
                s = phase(name, a="h0 h1 h2 h3", v="l0 l1 l2 l3")
                self.A, self.V = s["a"], s["v"]

            def act(self, eng, V, written):
                for k in range(4):
                    f = slice(4 * k, 4 * k + 4)
                    eng.wait_ge(V.sem, V.at(written[k]) if isinstance(written[k], str) else written[k])
                    nc.scalar.activation(self.pair[0][:, f, 0:self.n], self.src[:, f, 0:self.n], ACT.Copy)\
                        .then_inc(self.A.sem, self.A.step(f"h{k}"))

            def dve(self, eng):
                for k in range(4):
                    f = slice(4 * k, 4 * k + 4)
                    eng.wait_ge(self.A.sem, self.A.at(f"h{k}"))
                    nc.vector.tensor_tensor(self.pair[1][:, f, 0:self.n], self.src[:, f, 0:self.n],
                                            self.pair[0][:, f, 0:self.n].bitcast(F32), ALU.subtract)\
                        .then_inc(self.V.sem, self.V.step(f"l{k}"))

            def pe(self, eng):
                eng.wait_ge(self.V.sem, self.V.at("l3"))

        class Norm:

            def __init__(self, name, src, n, eps_col, outs, residual=None):
                self.src, self.n, self.eps_col, self.outs, self.residual = src, n, eps_col, outs, residual
                s = phase(name, a="sq0 sq1 sq2 sq3 root", t="s0 s1 s2 s3",
                          v="var rstd " + " ".join(f"o{k}_{kt}" for k in range(len(outs)) for kt in range(KT))
                          + (" " + " ".join(f"r{kt}" for kt in range(KT)) if residual is not None else ""))
                self.A, self.T, self.V = s["a"], s["t"], s["v"]
                a = carve([("low", ARENA - 9 * NT), ("sq", 2, 4 * NT), ("rstd", NT)])
                self.rstd = a["rstd"][:, 0:n]
                self.sq = [a["sq"][:, k, :].rearrange("p (a b) -> p a b", a=4)[:, :, 0:n] for k in range(2)]
                self.last = f"r{KT - 1}" if residual is not None else f"o{len(outs) - 1}_{KT - 1}"

            def act(self, eng):
                for k in range(4):
                    if k >= 2:
                        eng.wait_ge(self.T.sem, self.T.at(f"s{k - 2}"))
                    nc.scalar.activation(self.sq[k % 2], self.src[:, 4 * k:4 * k + 4, 0:self.n],
                                                     ACT.Square)\
                        .then_inc(self.A.sem, self.A.step(f"sq{k}"))
                eng.wait_ge(self.V.sem, self.V.at("var"))
                nc.scalar.activation(self.rstd, self.rstd, ACT.Sqrt)\
                    .then_inc(self.A.sem, self.A.step("root"))
                for k, (gain, dst, split) in enumerate(self.outs):
                    if split is not None:
                        split.act(eng, self.V, [f"o{k}_{4 * j + 3}" for j in range(4)])

            def pe(self, eng):
                for k in range(4):
                    eng.wait_ge(self.A.sem, self.A.at(f"sq{k}"))
                    for j in range(4):
                        ins = mm(ps[:, 7, 0:self.n], c("ones"), self.sq[k % 2][:, j, :],
                                 start=(k == 0 and j == 0), stop=(k == 3 and j == 3))
                    ins\
                        .then_inc(self.T.sem, self.T.step(f"s{k}"))

            def dve(self, eng):
                n, V = self.n, self.V
                eng.wait_ge(self.T.sem, self.T.at("s3"))
                nc.vector.tensor_scalar(self.rstd, ps[:, 7, 0:n], 1.0 / D,
                                               eps[:, self.eps_col:self.eps_col + 1], ALU.mult, ALU.add)\
                    .then_inc(V.sem, V.step("var"))
                eng.wait_ge(self.A.sem, self.A.at("root"))
                nc.vector.reciprocal(self.rstd, self.rstd)\
                    .then_inc(V.sem, V.step("rstd"))
                eng.wait_ge(V.sem, V.at("rstd"))
                for k, (gain, dst, split) in enumerate(self.outs):
                    if k:
                        eng.wait_ge(self.outs[k - 1][2].V.sem, self.outs[k - 1][2].V.at("l3"))
                    for kt in range(KT):
                        nc.vector.scalar_tensor_tensor(
                            out=dst[:, kt, 0:n], in0=self.src[:, kt, 0:n], scalar=p(gain, kt), in1=self.rstd,
                            op0=ALU.mult, op1=ALU.mult)\
                            .then_inc(V.sem, V.step(f"o{k}_{kt}"))
                    if split is not None:
                        for j in range(4):
                            eng.wait_ge(V.sem, V.at(f"o{k}_{4 * j + 3}"))
                        split.dve(eng)
                if self.residual is not None:
                    for kt in range(KT):
                        eng.wait_ge(V.sem, V.at(f"o0_{kt}"))
                        x = self.residual[:, kt, 0:n]
                        nc.vector.tensor_tensor(x, x, self.outs[0][1][:, kt, 0:n], ALU.add)\
                            .then_inc(V.sem, V.step(f"r{kt}"))

        class Product:
            def __init__(self, name, units, rhs, n, dst, add):
                self.units, self.rhs, self.n, self.dst, self.add = units, rhs, n, dst, add
                self.V = phase(name, v=" ".join(f"t{t}" for t in range(8)))["v"]

            def pe(self, eng):
                def body(i):
                    for t in range(8):
                        if ran(i if t >= 4 else i - 1):
                            eng.wait_ge(self.V.sem, self.V.at(f"t{(t - 4) % 8}", i if t >= 4 else i - 1))
                        tile(eng, self.units, t, i, 8, [(ps[:, t % 4, :], *self.rhs, ALL)], self.n)\
                            .then_inc(tile_done, 1)
                repeat(eng, 2, body)

            def act(self, eng):
                def body(i):
                    for t in range(8):
                        round_weights(eng, self.units, t + 2, i, 8)
                repeat(eng, 2, body)

            def dve(self, eng):
                def body(i):
                    for t in range(8):
                        eng.wait_ge(tile_done, done(self.units, t, i, 8))
                        o = self.dst[:, bass.ds(8 * i + t, 1), 0:self.n]
                        acc = ps[:, t % 4:t % 4 + 1, 0:self.n]
                        if self.add:
                            nc.vector.tensor_tensor(o, acc, o, ALU.add)\
                                .then_inc(self.V.sem, self.V.step(f"t{t}"))
                        else:
                            nc.vector.tensor_copy(o, acc)\
                                .then_inc(self.V.sem, self.V.step(f"t{t}"))
                repeat(eng, 2, body)

        split_a = Split("split_a", og, (hh, hl), NT)
        norm_a = Norm("norm_a", xT, NT, 0, [("a", og, split_a)])
        SA = phase("attn_a",
                   a="qk0 qk1 qk2 qk3 v0 v1 e0 e1 e2 e3 e4 e5 g0 g1 wT sqo root",
                   t="scores vt wt pv osum",
                   v="rcos shuf rsin radd mx0 mx1 mxm nb v vm rr rl n0 w0 n1 w1 nm wm wTm var rstd o0 o1 og0 og1")
        fa = carve([("qk", 4, NT), ("sh", 4, NT), ("xc", 4, NT), ("vT", 2, NT), ("v", 3, 256), ("ga", 2, NT), ("p0", 2, 144),
                    ("p1", 2, NT), ("pm", 2, META), ("wT", 384), ("wTm", NT), ("sqo", 2, NT), ("rstd", NT),
                    ("o", 2, NT)])
        A_MX, A_NB, A_RS, A_RR = 0, 6, 12, 18
        LAM = 24
        lam_steps = phase("lam", v="prod1 prod2 diff neg", t="sum", a="exp")

        def lam_pe(pe):
            pe.wait_ge(lam_steps["v"].sem, lam_steps["v"].at("prod2"))
            mm(ps[:, 6, 0:2], c("ones"), st[:, LAM + 1:LAM + 3])\
                .then_inc(lam_steps["t"].sem, lam_steps["t"].step("sum"))

        def lam_act(act):
            act.wait_ge(lam_steps["t"].sem, lam_steps["t"].at("sum"))
            nc.scalar.activation(st[:, LAM + 3:LAM + 5], ps[:, 6, 0:2], ACT.Exp)\
                .then_inc(lam_steps["a"].sem, lam_steps["a"].step("exp"))

        def lam_dve(dve):
            V = lam_steps["v"]
            for k in range(2):
                nc.vector.tensor_tensor(st[:, LAM + 1 + k:LAM + 2 + k], p("lam", 2 * k), p("lam", 2 * k + 1),
                                               ALU.mult)\
                    .then_inc(V.sem, V.step(f"prod{k + 1}"))
            dve.wait_ge(lam_steps["a"].sem, lam_steps["a"].at("exp"))
            nc.vector.tensor_tensor(st[:, LAM:LAM + 1], st[:, LAM + 4:LAM + 5], st[:, LAM + 3:LAM + 4],
                                           ALU.subtract)\
                .then_inc(V.sem, V.step("diff"))
            dve.wait_ge(V.sem, V.at("diff"))
            nc.vector.tensor_scalar(st[:, LAM:LAM + 1], st[:, LAM:LAM + 1], -LAMBDA_INIT, None, ALU.add)\
                .then_inc(V.sem, V.step("neg"))

        def attn_a_pe(pe):
            A, T, V = SA["a"], SA["t"], SA["v"]
            qk, v, p0, p1, pm = fa["qk"], fa["v"], fa["p0"], fa["p1"], fa["pm"]
            split_a.pe(pe)

            def body(i):
                for t in range(6):
                    if t == 0:
                        if ran(i - 1):
                            pe.wait_ge(V.sem, V.at("vm", i - 1))
                    elif t == 1:
                        if ran(i - 1):
                            pe.wait_ge(A.sem, A.at("v1", i - 1))
                    elif t < 4:
                        if ran(i - 1):
                            pe.wait_ge(A.sem, A.at(f"g{t - 2}", i - 1))
                    else:
                        pe.wait_ge(A.sem, A.at(f"qk{t - 4}", i))
                    tile(pe, "a", t, i, 8, [(ps[:, t % 4, :], hh, hl, ALL)], NT).then_inc(tile_done, 1)
                pe.wait_ge(V.sem, V.at("radd", i))
                if ran(i - 1):
                    pe.wait_ge(A.sem, A.at("wT", i - 1))
                if ran(i - 1):
                    pe.wait_ge(V.sem, V.at("var", i - 1))
                if ran(i - 1):
                    pe.wait_ge(V.sem, V.at("o1", i - 1))
                for a in range(2):
                    k = qk[:, 2 + a, :]
                    q = qk[:, a, :]
                    o = ps[:, 4, 144 * a:144 * a + 144]
                    mm(o[:, 128:144], q[:, 0:128], k[:, 256:NT])
                    mm(o[:, 0:128], q[:, 0:128], k[:, 0:128], stop=False)
                    mm(o[:, 64:128], c("low", 1), c("neg", 1), start=False)
                    o = ps[:, 5 + a, :]
                    mm(o[:, 0:NT], q[:, 128:256], k, stop=False)
                    mm(o[:, 192:256], c("low", 1), c("neg", 1), start=False)
                    ins = mm(ps[0:META, 4, 288 + META * a:288 + META * (a + 1)], q[:, 256:NT], k[:, 256:NT])
                ins\
                    .then_inc(T.sem, T.step("scores"))
                pe.wait_ge(A.sem, A.at("v1", i))
                if ran(i - 1):
                    pe.wait_ge(V.sem, V.at("o1", i - 1))
                for tok in range(2):
                    for d in range(2):
                        nc.tensor.transpose(ps[:, 7, 256 * tok + 128 * d:256 * tok + 128 * d + 128],
                                            fa["vT"][:, d, 128 * tok:128 * tok + 128], c("ident"))
                for d in range(2):
                    ins = nc.tensor.transpose(ps[0:META, 0, 128 * d:128 * d + 128], fa["vT"][:, d, 256:NT], c("ident"))
                ins\
                    .then_inc(T.sem, T.step("vt"))
                for t in (6, 7):
                    pe.wait_ge(A.sem, A.at(f"qk{t - 4}", i))
                    tile(pe, "a", t, i, 8, [(ps[:, t % 4, :], hh, hl, ALL)], NT).then_inc(tile_done, 1)
                pe.wait_ge(V.sem, V.at("wm", i))
                pe.wait_ge(A.sem, A.at("e5", i))
                nc.tensor.transpose(ps[:, 4, 0:128], p0[:, 0, 0:128], c("ident"))
                nc.tensor.transpose(ps[:, 4, 128:256], p1[:, 0, 0:128], c("ident"))
                nc.tensor.transpose(ps[:, 4, 256:384], p1[:, 0, 128:256], c("ident"))
                nc.tensor.transpose(ps[0:META, 5, 0:128], p0[:, 0, 128:144], c("ident"))
                nc.tensor.transpose(ps[0:META, 5, 128:256], p1[:, 0, 256:NT], c("ident"))
                nc.tensor.transpose(ps[0:META, 5, 256:NT], pm[0:META, 0, :], c("ident", META)[:, 0:META])\
                    .then_inc(T.sem, T.step("wt"))
                pe.wait_ge(A.sem, A.at("wT", i))
                pe.wait_ge(V.sem, V.at("wTm", i))
                for d in range(2):
                    o = ps[:, 6 + d, :]
                    f = slice(128 * d, 128 * d + 128)
                    mm(o[:, 0:NT], v[0:META, 2, f], fa["wTm"][0:META, :], stop=False)
                    mm(o[:, 0:256], v[:, 0, f], fa["wT"][:, 0:256], start=False, stop=False)
                    ins = mm(o[:, 128:256], v[:, 1, f], fa["wT"][:, 256:384], start=False)
                ins\
                    .then_inc(T.sem, T.step("pv"))
                pe.wait_ge(A.sem, A.at("sqo", i))
                for d in range(2):
                    ins = mm(ps[:, 5, 0:NT], c("ones"), fa["sqo"][:, d, :], start=(d == 0), stop=(d == 1))
                ins\
                    .then_inc(T.sem, T.step("osum"))
            repeat(pe, HEADS_A, body)

        def attn_a_act(act):
            A, T, V = SA["a"], SA["t"], SA["v"]

            def body(i):
                for t in range(4):
                    act.wait_ge(tile_done, done("a", t, i, 8))
                    if ran(i - 1):
                        act.wait_ge(T.sem, T.at("scores", i - 1))
                    nc.scalar.activation(fa["qk"][:, t, :], ps[:, t, 0:NT], ACT.Copy)\
                        .then_inc(A.sem, A.step(f"qk{t}"))
                    round_weights(act, "a", t + 2, i, 8)
                for d in range(2):
                    act.wait_ge(tile_done, done("a", 4 + d, i, 8))
                    if ran(i - 1):
                        act.wait_ge(T.sem, T.at("vt", i - 1))
                    nc.scalar.activation(fa["vT"][:, d, :], ps[:, d, 0:NT], ACT.Copy)\
                        .then_inc(A.sem, A.step(f"v{d}"))
                    round_weights(act, "a", d + 6, i, 8)
                act.wait_ge(V.sem, V.at("nb", i))
                if ran(i - 1):
                    act.wait_ge(T.sem, T.at("wt", i - 1))

                def e(k, rows, o, s):
                    nc.scalar.activation(o, s, ACT.Exp, bias=st[0:rows, A_NB + k:A_NB + k + 1], scale=SCALE_A,
                                                accum_out=st[0:rows, A_RS + k:A_RS + k + 1])\
                        .then_inc(A.sem, A.step(f"e{k}"))
                for a in range(2):
                    e(a, 128, fa["p0"][:, a, :], ps[:, 4, 144 * a:144 * a + 144])
                for a in range(2):
                    e(2 + a, 128, fa["p1"][:, a, :], ps[:, 5 + a, 0:NT])
                for a in range(2):
                    e(4 + a, META, fa["pm"][0:META, a, :], ps[0:META, 4, 288 + META * a:288 + META * (a + 1)])
                for d in range(2):
                    act.wait_ge(tile_done, done("a", 6 + d, i, 8))
                    if ran(i - 1):
                        act.wait_ge(V.sem, V.at("og1", i - 1))
                    nc.scalar.activation(fa["ga"][:, d, :], ps[:, 2 + d, 0:NT], ACT.Silu)\
                        .then_inc(A.sem, A.step(f"g{d}"))
                    round_weights(act, "a", d + 8, i, 8)
                act.wait_ge(T.sem, T.at("wt", i))
                nc.scalar.activation(fa["wT"], ps[:, 4, 0:384], ACT.Copy)\
                    .then_inc(A.sem, A.step("wT"))
                act.wait_ge(T.sem, T.at("pv", i))
                nc.scalar.activation(fa["sqo"], ps[:, 6:8, 0:NT], ACT.Square)\
                    .then_inc(A.sem, A.step("sqo"))
                act.wait_ge(V.sem, V.at("var", i))
                nc.scalar.activation(fa["rstd"], fa["rstd"], ACT.Sqrt)\
                    .then_inc(A.sem, A.step("root"))
            repeat(act, HEADS_A, body)

        def attn_a_dve(dve):
            A, T, V = SA["a"], SA["t"], SA["v"]
            swap = [(r + 16) % 32 for r in range(32)]
            x, xc, sh = fa["qk"][0:32], fa["xc"][0:32], fa["sh"][0:32]
            cos = c("cos_a", 32).unsqueeze(1).to_broadcast([32, 4, NT])
            sin = c("sin_a", 32).unsqueeze(1).to_broadcast([32, 4, NT])
            p0, p1, pm = fa["p0"], fa["p1"], fa["pm"]

            def body(i):
                dve.wait_ge(A.sem, A.at("qk3", i))
                nc.vector.tensor_tensor(xc, x, cos, ALU.mult)\
                    .then_inc(V.sem, V.step("rcos"))
                nc.vector.stream_shuffle(sh, x, swap)\
                    .then_inc(V.sem, V.step("shuf"))
                dve.wait_ge(V.sem, V.at("shuf", i))
                nc.vector.tensor_tensor(sh, sh, sin, ALU.mult)\
                    .then_inc(V.sem, V.step("rsin"))
                dve.wait_ge(V.sem, V.at("rsin", i))
                nc.vector.tensor_tensor(x, xc, sh, ALU.add)\
                    .then_inc(V.sem, V.step("radd"))
                dve.wait_ge(T.sem, T.at("scores", i))
                nc.vector.tensor_reduce(st[:, 0:2], ps[:, 4, 0:288].rearrange("p (a b) -> p a b", a=2),
                                               AX.X, ALU.max)\
                    .then_inc(V.sem, V.step("mx0"))
                nc.vector.tensor_reduce(st[:, 2:4], ps[:, 5:7, 0:NT], AX.X, ALU.max)\
                    .then_inc(V.sem, V.step("mx1"))
                nc.vector.tensor_reduce(st[0:META, 4:6],
                                               ps[0:META, 4, 288:320].rearrange("p (a b) -> p a b", a=2),
                                               AX.X, ALU.max)\
                    .then_inc(V.sem, V.step("mxm"))
                dve.wait_ge(V.sem, V.at("mxm", i))
                nc.vector.tensor_scalar(st[:, A_NB:A_NB + 6], st[:, A_MX:A_MX + 6], -SCALE_A, None, ALU.mult)\
                    .then_inc(V.sem, V.step("nb"))
                dve.wait_ge(T.sem, T.at("vt", i))
                if ran(i - 1):
                    dve.wait_ge(T.sem, T.at("pv", i - 1))
                nc.vector.tensor_copy(fa["v"][:, 0:2, :], ps[:, 7, :].rearrange("p (a b) -> p a b", a=2))\
                    .then_inc(V.sem, V.step("v"))
                nc.vector.tensor_copy(fa["v"][0:META, 2, :], ps[0:META, 0, 0:256])\
                    .then_inc(V.sem, V.step("vm"))
                dve.wait_ge(A.sem, A.at("e5", i))
                nc.vector.reciprocal(st[:, A_RR:A_RR + 6], st[:, A_RS:A_RS + 6])\
                    .then_inc(V.sem, V.step("rr"))
                dve.wait_ge(V.sem, V.at("rr", i))
                odd = st[:, A_RR:A_RR + 6].rearrange("p (a b) -> p a b", b=2)[:, :, 1]
                nc.vector.tensor_scalar(odd, odd, st[:, LAM:LAM + 1], None, ALU.mult)\
                    .then_inc(V.sem, V.step("rl"))
                dve.wait_ge(V.sem, V.at("rl", i))
                for k, (w_, rows) in enumerate(((p0, 128), (p1, 128), (pm, META))):
                    r = A_RR + 2 * k
                    s = "01m"[k]
                    nc.vector.tensor_scalar(w_[0:rows, 0, :], w_[0:rows, 0, :], st[0:rows, r:r + 1], None,
                                                   ALU.mult)\
                        .then_inc(V.sem, V.step(f"n{s}"))
                    dve.wait_ge(V.sem, V.at(f"n{s}", i))
                    nc.vector.scalar_tensor_tensor(
                        out=w_[0:rows, 0, :], in0=w_[0:rows, 1, :], scalar=st[0:rows, r + 1:r + 2],
                        in1=w_[0:rows, 0, :], op0=ALU.mult, op1=ALU.add)\
                        .then_inc(V.sem, V.step(f"w{s}"))
                dve.wait_ge(T.sem, T.at("wt", i))
                nc.vector.tensor_copy(fa["wTm"][0:META, :], ps[0:META, 5, 0:NT])\
                    .then_inc(V.sem, V.step("wTm"))
                dve.wait_ge(T.sem, T.at("osum", i))
                nc.vector.tensor_scalar(fa["rstd"], ps[:, 5, 0:NT], 1.0 / 256, eps[:, 0:1], ALU.mult, ALU.add)\
                    .then_inc(V.sem, V.step("var"))
                dve.wait_ge(A.sem, A.at("root", i))
                nc.vector.reciprocal(fa["rstd"], fa["rstd"])\
                    .then_inc(V.sem, V.step("rstd"))
                dve.wait_ge(V.sem, V.at("rstd", i))
                for d in range(2):
                    nc.vector.scalar_tensor_tensor(
                        out=fa["o"][:, d, :], in0=ps[:, 6 + d, 0:NT], scalar=p("subln", d), in1=fa["rstd"],
                        op0=ALU.mult, op1=ALU.mult)\
                        .then_inc(V.sem, V.step(f"o{d}"))
                dve.wait_ge(A.sem, A.at("g1", i))
                for d in range(2):
                    dve.wait_ge(V.sem, V.at(f"o{d}", i))
                    nc.vector.scalar_tensor_tensor(
                        out=og[:, bass.ds(2 * i + d, 1), :], in0=fa["o"][:, d:d + 1, :], scalar=1.0 - LAMBDA_INIT,
                        in1=fa["ga"][:, d:d + 1, :], op0=ALU.mult, op1=ALU.mult)\
                        .then_inc(V.sem, V.step(f"og{d}"))
            repeat(dve, HEADS_A, body)

        split_ao = Split("split_ao", og, (hh, hl), NT)
        a_out = Product("a_out", "a_out", (hh, hl), NT, xT, add=True)

        split_kv = Split("split_kv", og, (hh, hl), NT)
        split_b = Split("split_b", og, (gh, gl), SEQ)
        norm_b = Norm("norm_b", xT, NT, 0, [("kv", og, split_kv), ("b", og, split_b)])
        SK = phase("kv", a="c0 c1 c2 c3", t="vt",
                   v="shuf rsin rcos radd zero " + " ".join(f"k{g}_{h}" for g in range(4) for h in range(2)) + " v vm")
        fb = carve([("pair", PAIR), ("kd", 4, 2 * NT), ("vB", 3, 256), ("kv", 4, NT), ("sh", 2, NT)])

        def kv_pe(pe):
            split_kv.pe(pe)
            for t in range(4):
                tile(pe, "kv", t, 0, 0, [(ps[:, t, :], hh, hl, ALL)], NT).then_inc(tile_done, 1)
            pe.wait_ge(SK["a"].sem, SK["a"].at("c3"))
            for tok in range(2):
                for k in range(2):
                    nc.tensor.transpose(ps[:, 4, 256 * tok + 128 * k:256 * tok + 128 * k + 128],
                                        fb["kv"][:, 2 + k, 128 * tok:128 * tok + 128], c("ident"))
            for k in range(2):
                ins = nc.tensor.transpose(ps[0:META, 5, 128 * k:128 * k + 128], fb["kv"][:, 2 + k, 256:NT], c("ident"))
            ins\
                .then_inc(SK["t"].sem, SK["t"].step("vt"))

        def kv_act(act):
            for t in range(4):
                act.wait_ge(tile_done, done("kv", t))
                nc.scalar.activation(fb["kv"][:, t, :], ps[:, t, 0:NT], ACT.Copy)\
                    .then_inc(SK["a"].sem, SK["a"].step(f"c{t}"))
                round_weights(act, "kv", t + 2)

        def kv_dve(dve):
            V = SK["v"]
            swap = [r ^ 8 if r < 16 else r for r in range(32)]
            x, sh = fb["kv"][:, 0:2, :], fb["sh"]
            dve.wait_ge(SK["a"].sem, SK["a"].at("c1"))
            nc.vector.stream_shuffle(sh, x, swap)\
                .then_inc(V.sem, V.step("shuf"))
            dve.wait_ge(V.sem, V.at("shuf"))
            nc.vector.tensor_tensor(sh, sh, c("sin_b").unsqueeze(1).to_broadcast([128, 2, NT]), ALU.mult)\
                .then_inc(V.sem, V.step("rsin"))
            nc.vector.tensor_tensor(x, x, c("cos_b").unsqueeze(1).to_broadcast([128, 2, NT]), ALU.mult)\
                .then_inc(V.sem, V.step("rcos"))
            dve.wait_ge(V.sem, V.at("rcos"))
            nc.vector.tensor_tensor(x, x, sh, ALU.add)\
                .then_inc(V.sem, V.step("radd"))
            nc.vector.memset(fb["kd"], 0.0)\
                .then_inc(V.sem, V.step("zero"))
            dve.wait_ge(V.sem, V.at("zero"))
            for g in range(4):
                for h in range(2):
                    nc.vector.tensor_copy(fb["kd"][64 * h:64 * h + 64, g, NT * h:NT * h + NT],
                                                 fb["kv"][64 * (g % 2):64 * (g % 2) + 64, g // 2, :])\
                        .then_inc(V.sem, V.step(f"k{g}_{h}"))
            dve.wait_ge(SK["t"].sem, SK["t"].at("vt"))
            nc.vector.tensor_copy(fb["vB"][:, 0:2, :], ps[:, 4, :].rearrange("p (a b) -> p a b", a=2))\
                .then_inc(V.sem, V.step("v"))
            nc.vector.tensor_copy(fb["vB"][0:META, 2, :], ps[0:META, 5, 0:256])\
                .then_inc(V.sem, V.step("vm"))

        rounds = " ".join(f"R{j}" for j in range(4))
        SB = phase("attn_b",
                   a="q0 q1 q2 q3 " + " ".join(f"e{j}_0 e{j}_1 e{j}_2 e{j}_3 es{j} g{j} wk{j}" for j in range(4)),
                   t=" ".join(f"sc{j} wt{j} pv{j}" for j in range(4)),
                   v="kg vg vgm sk rcos shuf rsin radd " + " ".join(
                       f"ma{j} mb{j} sm{j} nb{j} sn{j} den{j} rr{j} p{j}_0 p{j}_1 p{j}_2 p{j}_3 w1{j} wm{j} o{j}"
                       for j in range(4)))
        f2 = carve([("pair", PAIR), ("kd", 4, 2 * NT), ("vB", 3, 256), ("q", 4, 256), ("sh", 4, 256), ("xc", 4, 256), ("kg", 2 * NT), ("vg", 3, 64),
                    ("sk", 8), ("p0", 2, 144), ("p1", 2, NT), ("wk0", 512), ("wk1", 256), ("wkm", 512),
                    ("gb", 4, 256), ("stb", 32)])
        B_MX, B_SM, B_NB, B_SN, B_RS, B_RR = 0, 4, 8, 12, 16, 20

        def attn_b_pe(pe):
            A, T, V = SB["a"], SB["t"], SB["v"]
            q, kg, vg, p0, p1 = f2["q"], f2["kg"], f2["vg"], f2["p0"], f2["p1"]
            split_b.pe(pe)
            pe.wait_ge(SK["v"].sem, SK["v"].at("vm"))

            def body(i):
                for t in range(4):
                    if ran(i - 1):
                        pe.wait_ge(A.sem, A.at(f"g{t}", i - 1))
                    tile(pe, "b", t, i, 8, [(ps[:, t, :], gh, gl, ALL)], SEQ).then_inc(tile_done, 1)
                pe.wait_ge(V.sem, V.at("radd", i))
                for j in range(4):
                    if j:
                        pe.wait_ge(V.sem, V.at(f"o{j - 1}", i))
                    else:
                        if ran(i - 1):
                            pe.wait_ge(V.sem, V.at("o3", i - 1))
                    for a in range(2):
                        ka = kg[:, NT * a:NT * a + NT]
                        o = ps[:, 4, 144 * a:144 * a + 144]
                        mm(o[:, 128:144], q[:, j, 0:128], ka[:, 256:NT])
                        mm(o[:, 0:128], q[:, j, 0:128], ka[:, 0:128], stop=False)
                        mm(o[:, 64:128], c("low", 1), c("neg", 1), start=False)
                        o = ps[:, 5 + a, :]
                        mm(o[:, 0:NT], q[:, j, 128:256], ka, stop=False)
                        mm(o[:, 192:256], c("low", 1), c("neg", 1), start=False, stop=False)
                        ins = mm(o[:, 0:64], c("high", 1), c("neg", 1), start=False)
                    ins\
                        .then_inc(T.sem, T.step(f"sc{j}"))
                    pe.wait_ge(A.sem, A.at(f"q{j}", i))
                    tile(pe, "b", 4 + j, i, 8, [(ps[:, j, :], gh, gl, ALL)], SEQ).then_inc(tile_done, 1)
                    pe.wait_ge(V.sem, V.at(f"p{j}_3", i))
                    if ran(i if j else i - 1):
                        pe.wait_ge(A.sem, A.at(f"wk{j - 1}" if j else "wk3", i if j else i - 1))
                    for a in range(2):
                        nc.tensor.transpose(ps[:, 7, 256 * a:256 * a + 128], p0[:, a, 0:128], c("ident"))
                        nc.tensor.transpose(ps[:, 7, 256 * a + 128:256 * a + 256], p1[:, a, 0:128], c("ident"))
                        nc.tensor.transpose(ps[:, 4, 128 * a:128 * a + 128], p1[:, a, 128:256], c("ident"))
                        nc.tensor.transpose(ps[0:META, 5, 256 * a:256 * a + 128], p0[:, a, 128:144], c("ident"))
                        ins = nc.tensor.transpose(ps[0:META, 5, 256 * a + 128:256 * a + 256], p1[:, a, 256:NT],
                                                  c("ident"))
                    ins\
                        .then_inc(T.sem, T.step(f"wt{j}"))
                    pe.wait_ge(A.sem, A.at(f"wk{j}", i))
                    pe.wait_ge(V.sem, V.at(f"wm{j}", i))
                    for a in range(2):
                        o = ps[64 * a:64 * a + 64, 6, :]
                        mm(o[:, 0:256], vg[0:META, 2, :], f2["wkm"][0:META, 256 * a:256 * a + 256], stop=False)
                        mm(o[:, 0:256], vg[:, 0, :], f2["wk0"][:, 256 * a:256 * a + 256], start=False, stop=False)
                        ins = mm(o[:, 128:256], vg[:, 1, :], f2["wk1"][:, 128 * a:128 * a + 128], start=False)
                    ins\
                        .then_inc(T.sem, T.step(f"pv{j}"))
            repeat(pe, GROUPS_B, body)

        def attn_b_act(act):
            A, T, V = SB["a"], SB["t"], SB["v"]
            stb = f2["stb"]

            def body(i):
                for t in range(4):
                    act.wait_ge(tile_done, done("b", t, i, 8))
                    if ran(i - 1):
                        act.wait_ge(T.sem, T.at("sc3", i - 1))
                    nc.scalar.activation(f2["q"][:, t, :], ps[:, t, 0:256], ACT.Copy)\
                        .then_inc(A.sem, A.step(f"q{t}"))
                    round_weights(act, "b", t + 2, i, 8)
                for j in range(4):
                    act.wait_ge(V.sem, V.at(f"sn{j}", i))
                    if ran(i if j else i - 1):
                        act.wait_ge(T.sem, T.at(f"wt{j - 1}" if j else "wt3", i if j else i - 1))
                    for k in range(4):
                        o, s = ((f2["p0"][:, k, :], ps[:, 4, 144 * k:144 * k + 144]) if k < 2 else
                                (f2["p1"][:, k - 2, :], ps[:, 3 + k, 0:NT]))
                        nc.scalar.activation(o, s, ACT.Exp, bias=stb[:, B_NB + k:B_NB + k + 1], scale=SCALE_B,
                                                    accum_out=stb[:, B_RS + k:B_RS + k + 1])\
                            .then_inc(A.sem, A.step(f"e{j}_{k}"))
                    nc.scalar.activation(stb[:, B_SN:B_SN + 4], stb[:, B_SN:B_SN + 4], ACT.Exp)\
                        .then_inc(A.sem, A.step(f"es{j}"))
                    act.wait_ge(tile_done, done("b", 4 + j, i, 8))
                    if ran(i - 1):
                        act.wait_ge(V.sem, V.at(f"o{j}", i - 1))
                    nc.scalar.activation(f2["gb"][:, j, :], ps[:, j, 0:256], ACT.Silu)\
                        .then_inc(A.sem, A.step(f"g{j}"))
                    round_weights(act, "b", j + 6, i, 8)
                    act.wait_ge(T.sem, T.at(f"wt{j}", i))
                    nc.scalar.activation(f2["wk0"], ps[:, 7, :], ACT.Copy)\
                        .then_inc(A.sem, A.step(f"wk{j}"))
            repeat(act, GROUPS_B, body)

        def attn_b_dve(dve):
            A, T, V = SB["a"], SB["t"], SB["v"]
            stb, p0, p1 = f2["stb"], f2["p0"], f2["p1"]
            swap = [r ^ 8 if r < 16 else r for r in range(32)]
            cos = c("cos_b")[:, 0:256].unsqueeze(1).to_broadcast([128, 4, 256])
            sin = c("sin_b")[:, 0:256].unsqueeze(1).to_broadcast([128, 4, 256])
            dve.wait_ge(SK["v"].sem, SK["v"].at("vm"))

            def body(i):
                if ran(i - 1):
                    dve.wait_ge(T.sem, T.at("pv3", i - 1))
                nc.vector.tensor_copy(f2["kg"].unsqueeze(1), f2["kd"][:, bass.ds(i, 1), :])\
                    .then_inc(V.sem, V.step("kg"))
                nc.vector.tensor_copy(f2["vg"][:, 0:2, :], f2["vB"][:, 0:2, bass.ds(64 * i, 64)])\
                    .then_inc(V.sem, V.step("vg"))
                nc.vector.tensor_copy(f2["vg"][0:META, 2:3, :], f2["vB"][0:META, 2:3, bass.ds(64 * i, 64)])\
                    .then_inc(V.sem, V.step("vgm"))
                nc.vector.tensor_copy(f2["sk"], P[:, bass.ds(8 * i + P_AT["sinks"][0], 8)])\
                    .then_inc(V.sem, V.step("sk"))
                dve.wait_ge(A.sem, A.at("q3", i))
                nc.vector.tensor_tensor(f2["xc"], f2["q"], cos, ALU.mult)\
                    .then_inc(V.sem, V.step("rcos"))
                nc.vector.stream_shuffle(f2["sh"], f2["q"], swap)\
                    .then_inc(V.sem, V.step("shuf"))
                dve.wait_ge(V.sem, V.at("shuf", i))
                nc.vector.tensor_tensor(f2["sh"], f2["sh"], sin, ALU.mult)\
                    .then_inc(V.sem, V.step("rsin"))
                dve.wait_ge(V.sem, V.at("rsin", i))
                nc.vector.tensor_tensor(f2["q"], f2["xc"], f2["sh"], ALU.add)\
                    .then_inc(V.sem, V.step("radd"))
                for j in range(4):
                    sink = f2["sk"][:, 2 * j:2 * j + 2].unsqueeze(1).to_broadcast([128, 2, 2])

                    def s4(k):
                        return stb[:, k:k + 4].rearrange("p (a b) -> p a b", a=2)
                    dve.wait_ge(T.sem, T.at(f"sc{j}", i))
                    nc.vector.tensor_reduce(stb[:, 0:2], ps[:, 4, 0:288].rearrange("p (a b) -> p a b", a=2),
                                                   AX.X, ALU.max)\
                        .then_inc(V.sem, V.step(f"ma{j}"))
                    nc.vector.tensor_reduce(stb[:, 2:4], ps[:, 5:7, 0:NT], AX.X, ALU.max)\
                        .then_inc(V.sem, V.step(f"mb{j}"))
                    dve.wait_ge(V.sem, V.at(f"mb{j}", i))
                    nc.vector.scalar_tensor_tensor(out=s4(B_SM), in0=s4(B_MX), scalar=SCALE_B, in1=sink,
                                                          op0=ALU.mult, op1=ALU.max)\
                        .then_inc(V.sem, V.step(f"sm{j}"))
                    dve.wait_ge(V.sem, V.at(f"sm{j}", i))
                    nc.vector.tensor_scalar(stb[:, B_NB:B_NB + 4], stb[:, B_SM:B_SM + 4], -1.0, None,
                                                   ALU.mult)\
                        .then_inc(V.sem, V.step(f"nb{j}"))
                    nc.vector.tensor_tensor(s4(B_SN), sink, s4(B_SM), ALU.subtract)\
                        .then_inc(V.sem, V.step(f"sn{j}"))
                    dve.wait_ge(A.sem, A.at(f"es{j}", i))
                    nc.vector.tensor_tensor(stb[:, B_RR:B_RR + 4], stb[:, B_RS:B_RS + 4],
                                                   stb[:, B_SN:B_SN + 4], ALU.add)\
                        .then_inc(V.sem, V.step(f"den{j}"))
                    dve.wait_ge(V.sem, V.at(f"den{j}", i))
                    nc.vector.reciprocal(stb[:, B_RR:B_RR + 4], stb[:, B_RR:B_RR + 4])\
                        .then_inc(V.sem, V.step(f"rr{j}"))
                    dve.wait_ge(V.sem, V.at(f"rr{j}", i))
                    for k in range(4):
                        w_ = p0[:, k, :] if k < 2 else p1[:, k - 2, :]
                        nc.vector.tensor_scalar(w_, w_, stb[:, B_RR + k:B_RR + k + 1], None, ALU.mult)\
                            .then_inc(V.sem, V.step(f"p{j}_{k}"))
                    dve.wait_ge(T.sem, T.at(f"wt{j}", i))
                    nc.vector.tensor_copy(f2["wk1"], ps[:, 4, 0:256])\
                        .then_inc(V.sem, V.step(f"w1{j}"))
                    nc.vector.tensor_copy(f2["wkm"][0:META, :], ps[0:META, 5, :])\
                        .then_inc(V.sem, V.step(f"wm{j}"))
                    dve.wait_ge(T.sem, T.at(f"pv{j}", i))
                    dve.wait_ge(A.sem, A.at(f"g{j}", i))
                    nc.vector.tensor_tensor(og[:, bass.ds(4 * i + j, 1), 0:256], ps[:, 6:7, 0:256],
                                                   f2["gb"][:, j:j + 1, :], ALU.mult)\
                        .then_inc(V.sem, V.step(f"o{j}"))
            repeat(dve, GROUPS_B, body)

        split_bo = Split("split_bo", og, (hh, hl), SEQ)
        b_out = Product("b_out", "b_out", (hh, hl), SEQ, xT, add=True)
        norm_fin = Norm("norm_fin", xT, SEQ, 0, [("fin", xT, None)])
        split_mix = Split("split_mix", og, (hh, hl), SEQ)
        norm_mix = Norm("norm_mix", xT, SEQ, 1, [("mix_pre", og, split_mix)])

        SR = phase("rw_in", v=" ".join(f"t{t}" for t in range(8)))
        SS = phase("rw_small", a="wa g0 g1 tanh sig0 sig1 f", v=" ".join(
            f"d{k} n{k} m{k}" for k in range(3)) + " zeroa zerob zeroc zerov", t="lora")
        fr = carve([("zr", 24, 256), ("lora", 3, 1024), ("aq", 4, 256), ("bx", 4, 128),
                    ("cx", 4, 128), ("vx", 4, 128), ("LT", 4, 128), ("BQ", 4, 128), ("CA", 4, 128),
                    ("CQ", 4, 128), ("X", 4, 128), ("Y", 4, 128), ("bT", 4, 128), ("cT", 4, 128),
                    ("vT", 4, 128), ("lw", 3, 128), ("pj", 10), ("S", 128), ("R", 128), ("U", 128),
                    ("g", 256), ("bon", 256)])
        zs = C[:, C_AT["cos_a"][0]:C_AT["cos_a"][0] + 1024].rearrange("p (a b) -> p a b", a=4)

        def rw_in_pe(pe):
            split_mix.pe(pe)

            def body(i):
                for t in range(8):
                    if ran(i if t >= 4 else i - 1):
                        pe.wait_ge(SR["v"].sem, SR["v"].at(f"t{(t - 4) % 8}", i if t >= 4 else i - 1))
                    tile(pe, "rw", t, i, 8, [(ps[:, t % 4, :], hh, hl, ALL)], SEQ).then_inc(tile_done, 1)
            repeat(pe, 3, body)
            pe.wait_ge(SR["v"].sem, SR["v"].at("t7", 2))
            for t, m in enumerate((128, SB_HEADS, 128, 32)):
                tile(pe, "small", t, 0, 0, [(ps[:, t, :], hh, hl, ALL)], SEQ, m=m).then_inc(tile_done, 1)

        def rw_in_act(act):
            A = SS["a"]
            act.dma_start(fr["lora"].rearrange("p a b -> p (a b)"), lora).then_inc(lora_in, 16)

            def body(i):
                for t in range(8):
                    round_weights(act, "rw", t + 2, i, 8)
            repeat(act, 3, body)
            act.wait_ge(tile_done, done("small", 0))
            nc.scalar.activation(zs[:, 0, :], ps[:, 0, 0:256], ACT.Copy)\
                .then_inc(A.sem, A.step("wa"))
            round_weights(act, "small", 2)
            round_weights(act, "small", 3)
            act.wait_ge(tile_done, done("small", 3))
            nc.scalar.activation(zs[:, 1, :], ps[:, 2, 0:256], ACT.Copy)\
                .then_inc(A.sem, A.step("g0"))
            nc.scalar.activation(zs[0:32, 2, :], ps[0:32, 3, 0:256], ACT.Copy)\
                .then_inc(A.sem, A.step("g1"))
            act.wait_ge(SS["v"].sem, SS["v"].at("m0"))
            nc.scalar.activation(zs[0:64, 0, :], zs[0:64, 0, :], ACT.Tanh)\
                .then_inc(A.sem, A.step("tanh"))
            act.wait_ge(SS["v"].sem, SS["v"].at("m2"))
            nc.scalar.activation(zs[:, 1, :], zs[:, 1, :], ACT.Sigmoid)\
                .then_inc(A.sem, A.step("sig0"))
            nc.scalar.activation(zs[0:32, 2, :], zs[0:32, 2, :], ACT.Sigmoid)\
                .then_inc(A.sem, A.step("sig1"))
            nc.scalar.activation(zs[0:SB_HEADS, 3, :], ps[0:SB_HEADS, 1, 0:256], ACT.Copy)\
                .then_inc(A.sem, A.step("f"))
            round_weights(act, "zp", 0)
            round_weights(act, "zp", 1)

        def rw_in_dve(dve):
            def body(i):
                for t in range(8):
                    dve.wait_ge(tile_done, done("rw", t, i, 8))
                    nc.vector.tensor_copy(fr["zr"][:, bass.ds(8 * i + t, 1), :],
                                                       ps[:, t % 4:t % 4 + 1, 0:256])\
                        .then_inc(SR["v"].sem, SR["v"].step(f"t{t}"))
            repeat(dve, 3, body)
            V = SS["v"]
            tmp = og[:, 0, 0:256]
            for k, (name, j, rows, ready) in enumerate((("mu_wa", 0, 128, "wa"), ("mu_g", 0, 128, "g0"),
                                                        ("mu_g", 1, 32, "g1"))):
                z = zs[0:rows, k, :]
                dve.wait_ge(SS["a"].sem, SS["a"].at(ready))
                if k:
                    dve.wait_ge(V.sem, V.at(f"m{k - 1}"))
                nc.vector.tensor_tensor(tmp[0:rows, 1:256], z[:, 0:255], z[:, 1:256], ALU.subtract)\
                    .then_inc(V.sem, V.step(f"d{k}"))
                nc.vector.tensor_scalar(tmp[0:rows, 0:1], z[:, 0:1], -1.0, None, ALU.mult)\
                    .then_inc(V.sem, V.step(f"n{k}"))
                dve.wait_ge(V.sem, V.at(f"n{k}"))
                nc.vector.scalar_tensor_tensor(out=z, in0=tmp[0:rows, :], scalar=p(name, j, rows), in1=z,
                                                      op0=ALU.mult, op1=ALU.add)\
                    .then_inc(V.sem, V.step(f"m{k}"))
            nc.vector.memset(fr["aq"], 0.0)\
                .then_inc(V.sem, V.step("zeroa"))
            nc.vector.memset(fr["bx"], 0.0)\
                .then_inc(V.sem, V.step("zerob"))
            nc.vector.memset(fr["cx"], 0.0)\
                .then_inc(V.sem, V.step("zeroc"))
            nc.vector.memset(fr["vx"], 0.0)\
                .then_inc(V.sem, V.step("zerov"))

        NCH = SEQ // CHUNK
        lv = LEVELS[1:]
        SW = phase("rwkv",
                   a="w a g sqk nrm ea enc ec bT cT vT " + " ".join(f"t1_{b}" for b in lv)
                     + " " + " ".join(f"U{n}" for n in range(NCH)) + " sqy root",
                   t="lora kk bon grams tr " + " ".join(f"T{b} dY{b}" for b in lv)
                     + " " + " ".join(f"R{n} U{n} y{n}" for n in range(NCH)) + " mean var",
                   v="pj lw " + " ".join(f"d{z} n{z} m{z}" for z in "rkv") + " kk max rec kkn am1 k2 rk rkk bonus ld "
                     "cum cb a0 a1 q0 q1 ka b0 b1 c0 c1 v0 v1 LT BQ CA CQ x0 x1 y0 y1 "
                     "M2 M4 X2 Y2 M8 X4 Y4 M16 X8 Y8 M32 X16 Y16 Y32 "
                     + " ".join(f"R{n} S{n} P{n}" if 0 < n < NCH - 1 else (f"R{n} P{n}" if n == 0 else f"R{n}")
                                for n in range(NCH))
                     + " ys0 ys1 yc gvar grec gn gl gb gy")
        tmp = {n: og[:, k, 0:256] for k, n in enumerate("r k v kk a ec enc t1".split())}
        tmp["g"] = fr["g"]
        Xv = {"M": (fr["bx"], fr["cx"])}

        def rwkv_pe(pe):
            A, T, V = SW["a"], SW["t"], SW["v"]
            aq, bx, cx, vx, S = fr["aq"], fr["bx"], fr["cx"], fr["vx"], fr["S"]
            pe.wait_ge(SS["a"].sem, SS["a"].at("f"))

            def body(i):
                pe.wait_ge(V.sem, V.at("lw", i))
                if ran(i - 1):
                    pe.wait_ge(V.sem, V.at("grec", i - 1))
                lw = fr["lw"]
                mm(ps[:, 0, 0:256], lw[0:64, 0, :], zs[0:64, 0, :])
                mm(ps[:, 1, 0:256], lw[64:128, 0, :], zs[64:128, 0, :])
                mm(ps[:, 2, 0:256], lw[:, 1, :], zs[:, 1, :], stop=False)
                mm(ps[:, 2, 0:256], lw[0:32, 2, :], zs[0:32, 2, :], start=False)\
                    .then_inc(T.sem, T.step("lora"))
                pe.wait_ge(A.sem, A.at("sqk", i))
                mm(ps[:, 3, 0:256], c("hones"), tmp["t1"])\
                    .then_inc(T.sem, T.step("kk"))
                pe.wait_ge(V.sem, V.at("rkk", i))
                mm(ps[:, 4, 0:256], c("hones"), tmp["enc"])\
                    .then_inc(T.sem, T.step("bon"))
                pe.wait_ge(V.sem, V.at("v1", i))
                for n in range(NCH):
                    mm(ps[:, n, 0:256], bx[:, n, :], aq[:, n, :])
                    mm(ps[:, n, 256:512], cx[:, n, :], aq[:, n, :])
                for n in range(NCH):
                    ins = mm(ps[:, 4, 128 * n:128 * n + 128], aq[:, n, 0:128], bx[:, n, :])
                ins\
                    .then_inc(T.sem, T.step("grams"))
                if ran(i - 1):
                    pe.wait_ge(V.sem, V.at("ys1", i - 1))
                for bank, src in ((5, bx), (6, cx), (7, vx)):
                    for n in range(NCH):
                        ins = nc.tensor.transpose(ps[:, bank, 128 * n:128 * n + 128], src[:, n, :], c("ident"))
                ins\
                    .then_inc(T.sem, T.step("tr"))
                X, Y, T1 = fr["X"], fr["Y"], fr["vx"]
                for k, b in enumerate(lv):
                    pe.wait_ge(V.sem, V.at(f"M{b}", i))
                    pe.wait_ge(V.sem, V.at(f"X{lv[k - 1]}" if k else "y1", i))
                    for n in range(NCH):
                        ins = mm(ps[:, 0, 128 * n:128 * n + 128], Xv["M"][k % 2][:, n, :], X[:, n, :])
                    ins\
                        .then_inc(T.sem, T.step(f"T{b}"))
                    pe.wait_ge(A.sem, A.at(f"t1_{b}", i))
                    if k:
                        pe.wait_ge(V.sem, V.at(f"Y{lv[k - 1]}", i))
                    for n in range(NCH):
                        if b != lv[-1]:
                            mm(ps[:, 1, 128 * n:128 * n + 128], Y[:, n, :], T1[:, n, :])
                        ins = mm(ps[:, 2, 128 * n:128 * n + 128], T1[:, n, :], Y[:, n, :])
                    ins\
                        .then_inc(T.sem, T.step(f"dY{b}"))
                pe.wait_ge(V.sem, V.at(f"Y{lv[-1]}", i))
                for n in range(NCH):
                    if n:
                        pe.wait_ge(V.sem, V.at(f"P{n - 1}", i))
                        mm(ps[:, 3, 0:128], aq[:, n, 0:128], S, stop=False)
                    mm(ps[:, 3, 0:128], fr["CA"][:, n, :], fr["vT"][:, n, :], start=(n == 0))\
                        .then_inc(T.sem, T.step(f"R{n}"))
                    pe.wait_ge(V.sem, V.at(f"R{n}", i))
                    mm(ps[:, 4, 0:128], Y[:, n, :], fr["R"])\
                        .then_inc(T.sem, T.step(f"U{n}"))
                    pe.wait_ge(A.sem, A.at(f"U{n}", i))
                    y = ps[:, 5, 128 * n:128 * n + 128]
                    if n:
                        mm(y, S, aq[:, n, 128:256], stop=False)
                    mm(y, fr["U"], fr["BQ"][:, n, :], start=(n == 0), stop=False)
                    ins = mm(y, fr["vT"][:, n, :], fr["CQ"][:, n, :], start=False)
                    if n < NCH - 1:
                        mm(ps[:, 6, 0:128], fr["cT"][:, n, :], fr["vT"][:, n, :], stop=False)
                        ins = mm(ps[:, 6, 0:128], fr["bT"][:, n, :], fr["U"], start=False)
                    ins\
                        .then_inc(T.sem, T.step(f"y{n}"))
                pe.wait_ge(V.sem, V.at("ys1", i))
                mm(ps[:, 0, 0:256], c("hones"), tmp["t1"])\
                    .then_inc(T.sem, T.step("mean"))
                pe.wait_ge(A.sem, A.at("sqy", i))
                mm(ps[:, 1, 0:256], c("hones"), tmp["enc"])\
                    .then_inc(T.sem, T.step("var"))
            repeat(pe, RW_TILES, body)

        def rwkv_act(act):
            A, T, V = SW["a"], SW["t"], SW["v"]
            pj = fr["pj"]
            flat = "p a b -> p (a b)"

            def body(i):
                act.wait_ge(T.sem, T.at("lora", i))
                if ran(i - 1):
                    act.wait_ge(V.sem, V.at("gy", i - 1))
                nc.scalar.activation(tmp["ec"], ps[:, 0, 0:256], ACT.Sigmoid, bias=pj[:, W0:W0 + 1])\
                    .then_inc(A.sem, A.step("w"))
                nc.scalar.activation(tmp["a"], ps[:, 1, 0:256], ACT.Sigmoid, bias=pj[:, A0:A0 + 1])\
                    .then_inc(A.sem, A.step("a"))
                nc.scalar.activation(tmp["g"], ps[:, 2, 0:256], ACT.Copy)\
                    .then_inc(A.sem, A.step("g"))
                act.wait_ge(V.sem, V.at("kk", i))
                nc.scalar.activation(tmp["t1"], tmp["kk"], ACT.Square)\
                    .then_inc(A.sem, A.step("sqk"))
                act.wait_ge(T.sem, T.at("kk", i))
                nc.scalar.activation(tmp["t1"], ps[:, 3, 0:256], ACT.Sqrt)\
                    .then_inc(A.sem, A.step("nrm"))
                act.wait_ge(V.sem, V.at("cb", i))
                nc.scalar.activation(tmp["t1"], tmp["t1"], ACT.Exp)\
                    .then_inc(A.sem, A.step("ea"))
                nc.scalar.activation(tmp["enc"], tmp["ec"], ACT.Exp, scale=-1.0)\
                    .then_inc(A.sem, A.step("enc"))
                act.wait_ge(A.sem, A.at("enc", i))
                nc.scalar.activation(tmp["ec"], tmp["ec"], ACT.Exp)\
                    .then_inc(A.sem, A.step("ec"))
                act.wait_ge(T.sem, T.at("tr", i))
                nc.scalar.activation(fr["bT"].rearrange(flat), ps[:, 5, :], ACT.Copy, scale=-1.0)\
                    .then_inc(A.sem, A.step("bT"))
                nc.scalar.activation(fr["cT"].rearrange(flat), ps[:, 6, :], ACT.Copy)\
                    .then_inc(A.sem, A.step("cT"))
                nc.scalar.activation(fr["vT"].rearrange(flat), ps[:, 7, :], ACT.Copy)\
                    .then_inc(A.sem, A.step("vT"))
                for b in lv:
                    act.wait_ge(T.sem, T.at(f"T{b}", i))
                    nc.scalar.activation(fr["vx"].rearrange(flat), ps[:, 0, :], ACT.Copy)\
                        .then_inc(A.sem, A.step(f"t1_{b}"))
                for n in range(NCH):
                    act.wait_ge(T.sem, T.at(f"U{n}", i))
                    nc.scalar.activation(fr["U"], ps[:, 4, 0:128], ACT.Copy)\
                        .then_inc(A.sem, A.step(f"U{n}"))
                act.wait_ge(V.sem, V.at("yc", i))
                nc.scalar.activation(tmp["enc"], tmp["ec"], ACT.Square)\
                    .then_inc(A.sem, A.step("sqy"))
                act.wait_ge(V.sem, V.at("gvar", i))
                nc.scalar.activation(tmp["t1"], tmp["t1"], ACT.Sqrt)\
                    .then_inc(A.sem, A.step("root"))
            repeat(act, RW_TILES, body)

        def rwkv_dve(dve):
            A, T, V = SW["a"], SW["t"], SW["v"]
            pj = fr["pj"]
            aq, bx, cx, vx = fr["aq"], fr["bx"], fr["cx"], fr["vx"]
            flat = "p a b -> p (a b)"
            r, k, v, kk, a, ec, enc, t1 = (tmp[n] for n in "r k v kk a ec enc t1".split())

            def col(k_):
                return pj[:, k_:k_ + 1]

            def mask(name):
                return c(name).unsqueeze(1).to_broadcast([128, NCH, 128])

            def spread(o, off, x, y, names, op=ALU.mult):
                for h in range(2):
                    r_ = slice(64 * h, 64 * h + 64)
                    dst = o[r_, :, off + 64 * h:off + 64 * h + 64]
                    xv = x[r_].rearrange("p (a b) -> p a b", a=NCH)
                    if y is None:
                        nc.vector.tensor_copy(dst, xv)\
                            .then_inc(V.sem, V.step(names[h]))
                    else:
                        nc.vector.tensor_tensor(dst, xv, y[r_].rearrange("p (a b) -> p a b", a=NCH), op)\
                            .then_inc(V.sem, V.step(names[h]))

            def body(i):
                if ran(i - 1):
                    dve.wait_ge(V.sem, V.at("gy", i - 1))
                dve.wait_ge(lora_in, 16)
                nc.vector.tensor_copy(pj, P[:, bass.ds(10 * i + P_AT["rw"][0], 10)])\
                    .then_inc(V.sem, V.step("pj"))
                nc.vector.tensor_copy(fr["lw"], fr["lora"][:, :, bass.ds(128 * i, 128)])\
                    .then_inc(V.sem, V.step("lw"))
                dve.wait_ge(V.sem, V.at("pj", i))
                for q, (z, o) in enumerate(zip("rkv", (r, k, v))):
                    src = fr["zr"][:, bass.ds(i + 8 * q, 1), :]
                    nc.vector.tensor_tensor(o[:, 1:256].unsqueeze(1), src[:, :, 0:255], src[:, :, 1:256], ALU.subtract)\
                        .then_inc(V.sem, V.step(f"d{z}"))
                    nc.vector.tensor_scalar(o[:, 0:1].unsqueeze(1), src[:, :, 0:1], -1.0, None, ALU.mult)\
                        .then_inc(V.sem, V.step(f"n{z}"))
                    dve.wait_ge(V.sem, V.at(f"n{z}", i))
                    nc.vector.scalar_tensor_tensor(out=o.unsqueeze(1), in0=o.unsqueeze(1), scalar=col(MU_R + q), in1=src,
                                                   op0=ALU.mult, op1=ALU.add)\
                        .then_inc(V.sem, V.step(f"m{z}"))
                dve.wait_ge(V.sem, V.at("mv", i))
                nc.vector.tensor_scalar(kk, k, col(K_K), None, ALU.mult)\
                    .then_inc(V.sem, V.step("kk"))
                dve.wait_ge(A.sem, A.at("nrm", i))
                nc.vector.tensor_scalar(t1, t1, 1e-12, None, ALU.max)\
                    .then_inc(V.sem, V.step("max"))
                dve.wait_ge(V.sem, V.at("max", i))
                nc.vector.reciprocal(t1, t1)\
                    .then_inc(V.sem, V.step("rec"))
                dve.wait_ge(V.sem, V.at("rec", i))
                nc.vector.tensor_tensor(kk, kk, t1, ALU.mult)\
                    .then_inc(V.sem, V.step("kkn"))
                dve.wait_ge(V.sem, V.at("kkn", i))
                nc.vector.tensor_scalar(t1, a, -1.0, col(K_A), ALU.add, ALU.mult)\
                    .then_inc(V.sem, V.step("am1"))
                dve.wait_ge(V.sem, V.at("am1", i))
                nc.vector.scalar_tensor_tensor(out=k, in0=t1, scalar=1.0, in1=k,
                                               op0=ALU.add, op1=ALU.mult)\
                    .then_inc(V.sem, V.step("k2"))
                dve.wait_ge(V.sem, V.at("k2", i))
                nc.vector.tensor_scalar(enc, r, col(R_K), None, ALU.mult)\
                    .then_inc(V.sem, V.step("rk"))
                dve.wait_ge(V.sem, V.at("rk", i))
                nc.vector.tensor_tensor(enc, enc, k, ALU.mult)\
                    .then_inc(V.sem, V.step("rkk"))
                dve.wait_ge(T.sem, T.at("bon", i))
                nc.vector.tensor_tensor(fr["bon"], ps[:, 4, 0:256], v, ALU.mult)\
                    .then_inc(V.sem, V.step("bonus"))
                nc.vector.tensor_scalar(t1, ec, -DECAY, None, ALU.mult)\
                    .then_inc(V.sem, V.step("ld"))
                dve.wait_ge(V.sem, V.at("ld", i))
                nc.vector.tensor_tensor_scan(ec, c("reset"), t1, 0.0, ALU.mult, ALU.add)\
                    .then_inc(V.sem, V.step("cum"))
                dve.wait_ge(V.sem, V.at("cum", i))
                nc.vector.tensor_tensor(t1, ec, t1, ALU.subtract)\
                    .then_inc(V.sem, V.step("cb"))
                dve.wait_ge(A.sem, A.at("ec", i))
                spread(aq, 0, kk, t1, ("a0", "a1"))
                spread(aq, 128, r, ec, ("q0", "q1"))
                dve.wait_ge(V.sem, V.at("a1", i))
                nc.vector.tensor_tensor(kk, kk, a, ALU.mult)\
                    .then_inc(V.sem, V.step("ka"))
                dve.wait_ge(V.sem, V.at("ka", i))
                spread(bx, 0, kk, enc, ("b0", "b1"))
                spread(cx, 0, k, enc, ("c0", "c1"))
                spread(vx, 0, v, None, ("v0", "v1"))
                dve.wait_ge(T.sem, T.at("grams", i))
                nc.vector.tensor_tensor(fr["LT"], ps[:, 0:4, 0:128], mask("strict"), ALU.mult)\
                    .then_inc(V.sem, V.step("LT"))
                nc.vector.scalar_tensor_tensor(out=fr["BQ"], in0=ps[:, 0:4, 128:256], scalar=-1.0, in1=mask("incl"),
                                               op0=ALU.mult, op1=ALU.mult)\
                    .then_inc(V.sem, V.step("BQ"))
                nc.vector.tensor_tensor(fr["CA"], ps[:, 0:4, 256:384], mask("strict"), ALU.mult)\
                    .then_inc(V.sem, V.step("CA"))
                nc.vector.tensor_tensor(fr["CQ"], ps[:, 0:4, 384:512], mask("incl"), ALU.mult)\
                    .then_inc(V.sem, V.step("CQ"))
                nc.vector.tensor_tensor(fr["X"], ps[:, 4, :].rearrange("p (a b) -> p a b", a=NCH), mask("lev1t"), ALU.mult)\
                    .then_inc(V.sem, V.step("x0"))
                dve.wait_ge(V.sem, V.at("x0", i))
                nc.vector.tensor_tensor(fr["X"], mask("ident"), fr["X"], ALU.subtract)\
                    .then_inc(V.sem, V.step("x1"))
                nc.vector.tensor_tensor(fr["Y"], fr["LT"], mask("lev1"), ALU.mult)\
                    .then_inc(V.sem, V.step("y0"))
                dve.wait_ge(V.sem, V.at("y0", i))
                nc.vector.tensor_tensor(fr["Y"], mask("ident"), fr["Y"], ALU.subtract)\
                    .then_inc(V.sem, V.step("y1"))
                dve.wait_ge(T.sem, T.at("tr", i))
                nc.vector.tensor_tensor(bx, fr["LT"], mask(f"lev{lv[0]}"), ALU.mult)\
                    .then_inc(V.sem, V.step(f"M{lv[0]}"))
                nc.vector.tensor_tensor(cx, fr["LT"], mask(f"lev{lv[1]}"), ALU.mult)\
                    .then_inc(V.sem, V.step(f"M{lv[1]}"))
                for step, b in enumerate(lv):
                    dve.wait_ge(T.sem, T.at(f"dY{b}", i))
                    if b != lv[-1]:
                        nc.vector.tensor_tensor(fr["X"].rearrange(flat), fr["X"].rearrange(flat), ps[:, 1, :], ALU.subtract)\
                            .then_inc(V.sem, V.step(f"X{b}"))
                    nc.vector.tensor_tensor(fr["Y"].rearrange(flat), fr["Y"].rearrange(flat), ps[:, 2, :], ALU.subtract)\
                        .then_inc(V.sem, V.step(f"Y{b}"))
                    if step + 2 < len(lv):
                        nc.vector.tensor_tensor(Xv["M"][step % 2], fr["LT"], mask(f"lev{lv[step + 2]}"), ALU.mult)\
                            .then_inc(V.sem, V.step(f"M{lv[step + 2]}"))
                S = fr["S"]
                for n in range(NCH):
                    dve.wait_ge(T.sem, T.at(f"R{n}", i))
                    nc.vector.tensor_copy(fr["R"], ps[:, 3, 0:128])\
                        .then_inc(V.sem, V.step(f"R{n}"))
                    if n == NCH - 1:
                        break
                    dve.wait_ge(T.sem, T.at(f"y{n}", i))
                    end = ec[:, CHUNK * (n + 1) - 1:CHUNK * (n + 1)]
                    if n == 0:
                        nc.vector.tensor_scalar(S, ps[:, 6, 0:128], end, None, ALU.mult)\
                            .then_inc(V.sem, V.step("P0"))
                    else:
                        nc.vector.tensor_tensor(S, S, ps[:, 6, 0:128], ALU.add)\
                            .then_inc(V.sem, V.step(f"S{n}"))
                        dve.wait_ge(V.sem, V.at(f"S{n}", i))
                        nc.vector.tensor_scalar(S, S, end, None, ALU.mult)\
                            .then_inc(V.sem, V.step(f"P{n}"))
                dve.wait_ge(T.sem, T.at(f"y{NCH - 1}", i))
                y = ps[:, 5, :].rearrange("p (a b) -> p a b", a=NCH)
                for h in range(2):
                    r_ = slice(64 * h, 64 * h + 64)
                    nc.vector.tensor_copy(t1[r_].rearrange("p (a b) -> p a b", a=NCH), y[r_, :, r_])\
                        .then_inc(V.sem, V.step(f"ys{h}"))
                dve.wait_ge(T.sem, T.at("mean", i))
                nc.vector.scalar_tensor_tensor(out=ec, in0=ps[:, 0, 0:256], scalar=-1.0 / 64, in1=t1,
                                               op0=ALU.mult, op1=ALU.add)\
                    .then_inc(V.sem, V.step("yc"))
                dve.wait_ge(T.sem, T.at("var", i))
                nc.vector.tensor_scalar(t1, ps[:, 1, 0:256], 1.0 / 64, eps[:, 2:3], ALU.mult, ALU.add)\
                    .then_inc(V.sem, V.step("gvar"))
                dve.wait_ge(A.sem, A.at("root", i))
                nc.vector.reciprocal(t1, t1)\
                    .then_inc(V.sem, V.step("grec"))
                dve.wait_ge(V.sem, V.at("grec", i))
                nc.vector.tensor_tensor(ec, ec, t1, ALU.mult)\
                    .then_inc(V.sem, V.step("gn"))
                dve.wait_ge(V.sem, V.at("gn", i))
                nc.vector.tensor_scalar(ec, ec, col(LN_W), col(LN_B), ALU.mult, ALU.add)\
                    .then_inc(V.sem, V.step("gl"))
                dve.wait_ge(V.sem, V.at("gl", i))
                nc.vector.tensor_tensor(ec, ec, fr["bon"], ALU.add)\
                    .then_inc(V.sem, V.step("gb"))
                dve.wait_ge(V.sem, V.at("gb", i))
                nc.vector.tensor_tensor(og[:, bass.ds(8 + i, 1), 0:256], ec.unsqueeze(1), fr["g"].unsqueeze(1), ALU.mult)\
                    .then_inc(V.sem, V.step("gy"))
            repeat(dve, RW_TILES, body)

        SZ = phase("zp", v=" ".join(f"t{t}" for t in range(8)))
        fz = carve([("z", 24, 256), ("vv", 8, 256), ("p", 4, 384), ("q", 4, 384), ("u", 4, 384),
                    ("fs", 4, 256)])

        def zp_pe(pe):
            pe.wait_ge(SW["v"].sem, SW["v"].at("gy", RW_TILES - 1))

            def body(i):
                for t in range(8):
                    if ran(i if t >= 4 else i - 1):
                        pe.wait_ge(SZ["v"].sem, SZ["v"].at(f"t{(t - 4) % 8}", i if t >= 4 else i - 1))
                    tile(pe, "zp", t, i, 8, [(ps[:, t % 4, :], hh, hl, ALL)], SEQ).then_inc(tile_done, 1)
            repeat(pe, 3, body)

        def zp_act(act):
            def body(i):
                for t in range(8):
                    round_weights(act, "zp", t + 2, i, 8)
            repeat(act, 3, body)

        def zp_dve(dve):
            def body(i):
                for t in range(8):
                    dve.wait_ge(tile_done, done("zp", t, i, 8))
                    nc.vector.tensor_copy(fz["z"][:, bass.ds(8 * i + t, 1), :],
                                                       ps[:, t % 4:t % 4 + 1, 0:256])\
                        .then_inc(SZ["v"].sem, SZ["v"].step(f"t{t}"))
            repeat(dve, 3, body)

        H4 = range(4)
        ST = phase("attn_z",
                   a="va vb abs exp ln relu ew ya fabs fexp fln frelu " + " ".join(f"x{k}" for k in range(8)),
                   t="v0 v1 z logw ya f wt yb",
                   v="sq_a sq_b l m0 m1 fb fl cum ncum mx0 mx1 nb rr " + " ".join(f"n{k}" for k in range(8)) + " wt yb")
        z, u = fz["z"], fz["u"]
        zq_a, zk_a, zv_a, zq_b, zk_b, zv_b = (z[:, 4 * k:4 * k + 4, :] for k in range(6))
        fsm = zs[0:SB_HEADS, 3, :]
        F_MX, F_NB, F_RS, F_RR = 32, 40, 48, 56

        def attn_z_pe(pe):
            A, T, V = ST["a"], ST["t"], ST["v"]
            pe.wait_ge(SZ["v"].sem, SZ["v"].at("t7", 2))
            for k, zv in enumerate((zv_a, zv_b)):
                for h in H4:
                    for tok in range(2):
                        bank, at = 4 * k + h // 2, 256 * (h % 2) + 128 * tok
                        ins = nc.tensor.transpose(ps[:, bank, at:at + 128], zv[:, h, 128 * tok:128 * tok + 128],
                                                  c("ident"))
                ins\
                    .then_inc(T.sem, T.step(f"v{k}"))
            pe.wait_ge(V.sem, V.at("sq_b"))
            pe.wait_ge(A.sem, A.at("va"))
            for h in H4:
                mm(ps[:, h, 0:256], zk_a[:, h, 0:128], zq_a[:, h, :])
                ins = mm(ps[:, h, 256:384], zk_a[:, h, 128:256], zq_a[:, h, 128:256])
            ins\
                .then_inc(T.sem, T.step("z"))
            pe.wait_ge(A.sem, A.at("vb"))
            pe.wait_ge(V.sem, V.at("m1"))
            L = fz["p"]
            for h in H4:
                o = ps[:, 4 + h, :]
                mm(o[:, 0:256], zk_a[:, h, 0:128], zq_a[:, h, :], stop=False)
                mm(o[:, 0:256], c("tri"), L[:, h, 0:256], start=False, stop=False)
                mm(o[:, 128:256], c("ones"), L[:, h, 256:384], start=False, stop=False)
                mm(o[:, 0:128], c("ident"), c("not_after"), start=False)
                mm(o[:, 256:384], zk_a[:, h, 128:256], zq_a[:, h, 128:256], stop=False)
                mm(o[:, 256:384], c("tri"), L[:, h, 256:384], start=False, stop=False)
                ins = mm(o[:, 256:384], c("ident"), c("not_after"), start=False)
            ins\
                .then_inc(T.sem, T.step("logw"))
            pe.wait_ge(A.sem, A.at("ew"))
            W = fz["q"]
            for h in H4:
                o = ps[:, h, 0:256]
                mm(o, fz["vv"][:, h, 0:128], W[:, h, 0:256], stop=False)
                ins = mm(o[:, 128:256], fz["vv"][:, h, 128:256], W[:, h, 256:384], start=False)
            ins\
                .then_inc(T.sem, T.step("ya"))
            pe.wait_ge(V.sem, V.at("ncum"))
            cum, ncum = fz["fs"][0:4, 0, :], fz["fs"][0:4, 1, :]
            for h in H4:
                o = ps[:, 4 + h, :]
                sel = c("sel", 4)[:, 128 * h:128 * h + 128]
                mm(o[:, 0:128], zq_b[:, h, 0:128], zk_b[:, h, 0:128], stop=False)
                mm(o[:, 0:128], sel, ncum[:, 0:128], start=False, stop=False)
                mm(o[:, 0:128], cum[:, 0:128], sel, start=False, stop=False)
                mm(o[:, 0:128], c("ident"), c("future"), start=False)
                mm(o[:, 128:384], zq_b[:, h, 128:256], zk_b[:, h, :], stop=False)
                mm(o[:, 128:384], sel, ncum, start=False, stop=False)
                for k in range(2):
                    mm(o[:, 128 + 128 * k:256 + 128 * k], cum[:, 128:256], sel, start=False, stop=False)
                ins = mm(o[:, 256:384], c("ident"), c("future"), start=False)
            ins\
                .then_inc(T.sem, T.step("f"))
            pe.wait_ge(V.sem, V.at("n7"))
            pe.wait_ge(A.sem, A.at("ya"))
            pr = fz["p"]
            for h in H4:
                nc.tensor.transpose(ps[:, h, 0:128], pr[:, h, 0:128], c("ident"))
                nc.tensor.transpose(ps[:, h, 128:256], pr[:, h, 128:256], c("ident"))
                ins = nc.tensor.transpose(ps[:, h, 256:384], pr[:, h, 256:384], c("ident"))
            ins\
                .then_inc(T.sem, T.step("wt"))
            pe.wait_ge(V.sem, V.at("wt"))
            W = fz["q"]
            for h in H4:
                o = ps[:, 4 + h, 0:256]
                mm(o, fz["vv"][:, 4 + h, 0:128], W[:, h, 0:256], stop=False)
                ins = mm(o[:, 128:256], fz["vv"][:, 4 + h, 128:256], W[:, h, 256:384], start=False)
            ins\
                .then_inc(T.sem, T.step("yb"))

        def attn_z_act(act):
            A, T, V = ST["a"], ST["t"], ST["v"]
            act.wait_ge(T.sem, T.at("v0"))
            vv = fz["vv"]
            nc.scalar.activation(vv[:, 0:4, :], ps[:, 0:2, :].rearrange("p a (b c) -> p (a b) c", b=2),
                                        ACT.Copy)\
                .then_inc(A.sem, A.step("va"))
            act.wait_ge(T.sem, T.at("v1"))
            nc.scalar.activation(vv[:, 4:8, :], ps[:, 4:6, :].rearrange("p a (b c) -> p (a b) c", b=2),
                                        ACT.Copy)\
                .then_inc(A.sem, A.step("vb"))
            zz = ps[:, 0:4, 0:384]
            act.wait_ge(T.sem, T.at("z"))
            nc.scalar.activation(fz["q"], zz, ACT.Abs)\
                .then_inc(A.sem, A.step("abs"))
            act.wait_ge(A.sem, A.at("abs"))
            nc.scalar.activation(fz["q"], fz["q"], ACT.Exp, scale=-1.0)\
                .then_inc(A.sem, A.step("exp"))
            act.wait_ge(A.sem, A.at("exp"))
            nc.scalar.activation(fz["q"], fz["q"], ACT.Ln, bias=eps[:, 3:4])\
                .then_inc(A.sem, A.step("ln"))
            nc.scalar.activation(u, zz, ACT.Relu)\
                .then_inc(A.sem, A.step("relu"))
            act.wait_ge(T.sem, T.at("logw"))
            act.wait_ge(V.sem, V.at("l"))
            nc.scalar.activation(fz["q"], ps[:, 4:8, 0:384], ACT.Exp)\
                .then_inc(A.sem, A.step("ew"))
            act.wait_ge(T.sem, T.at("ya"))
            nc.scalar.activation(og[:, 0:4, 0:256], ps[:, 0:4, 0:256], ACT.Copy)\
                .then_inc(A.sem, A.step("ya"))
            f = fz["fs"]
            act.wait_ge(V.sem, V.at("fb"))
            nc.scalar.activation(f[0:4, 2, :], f[0:4, 0, :], ACT.Abs)\
                .then_inc(A.sem, A.step("fabs"))
            act.wait_ge(A.sem, A.at("fabs"))
            nc.scalar.activation(f[0:4, 2, :], f[0:4, 2, :], ACT.Exp, scale=-1.0)\
                .then_inc(A.sem, A.step("fexp"))
            act.wait_ge(A.sem, A.at("fexp"))
            nc.scalar.activation(f[0:4, 2, :], f[0:4, 2, :], ACT.Ln, bias=eps[0:4, 3:4])\
                .then_inc(A.sem, A.step("fln"))
            nc.scalar.activation(f[0:4, 3, :], f[0:4, 0, :], ACT.Relu, scale=-1.0)\
                .then_inc(A.sem, A.step("frelu"))
            act.wait_ge(V.sem, V.at("nb"))
            for h in H4:
                for k, s_ in enumerate((slice(0, 128), slice(128, 384))):
                    q = 4 * k + h
                    nc.scalar.activation(fz["p"][:, h, s_], ps[:, 4 + h, s_], ACT.Exp,
                                                bias=st[:, F_NB + q:F_NB + q + 1],
                                                accum_out=st[:, F_RS + q:F_RS + q + 1])\
                        .then_inc(A.sem, A.step(f"x{2 * h + k}"))

        def attn_z_dve(dve):
            A, T, V = ST["a"], ST["t"], ST["v"]
            flat = "p a b -> p (a b)"
            L, f = fz["p"], fz["fs"]
            dve.wait_ge(SZ["v"].sem, SZ["v"].at("t7", 2))
            nc.vector.tensor_scalar(zq_a, zq_a, SCALE_Z, None, ALU.mult)\
                .then_inc(V.sem, V.step("sq_a"))
            nc.vector.tensor_scalar(zq_b, zq_b, SCALE_Z, None, ALU.mult)\
                .then_inc(V.sem, V.step("sq_b"))
            dve.wait_ge(A.sem, A.at("relu"))
            nc.vector.scalar_tensor_tensor(out=L.rearrange(flat), in0=fz["q"].rearrange(flat), scalar=-1.0,
                                                  in1=u.rearrange(flat), op0=ALU.mult, op1=ALU.subtract)\
                .then_inc(V.sem, V.step("l"))
            dve.wait_ge(V.sem, V.at("l"))
            after = c("after").unsqueeze(1).to_broadcast([128, 4, 128])
            nc.vector.tensor_tensor(L[:, :, 0:128], L[:, :, 0:128], after, ALU.mult)\
                .then_inc(V.sem, V.step("m0"))
            nc.vector.tensor_tensor(L[:, :, 256:384], L[:, :, 256:384], after, ALU.mult)\
                .then_inc(V.sem, V.step("m1"))
            nc.vector.tensor_scalar(f[0:4, 0, :], fsm, p("bf", 0, 4), None, ALU.add)\
                .then_inc(V.sem, V.step("fb"))
            dve.wait_ge(A.sem, A.at("frelu"))
            nc.vector.scalar_tensor_tensor(out=f[0:4, 1, :], in0=f[0:4, 2, :], scalar=-1.0, in1=f[0:4, 3, :],
                                                  op0=ALU.mult, op1=ALU.subtract)\
                .then_inc(V.sem, V.step("fl"))
            dve.wait_ge(V.sem, V.at("fl"))
            nc.vector.tensor_tensor_scan(f[0:4, 0, :], c("ones", 4)[:, 0:1].to_broadcast([4, 256]),
                                                f[0:4, 1, :], 0.0, ALU.mult, ALU.add)\
                .then_inc(V.sem, V.step("cum"))
            dve.wait_ge(V.sem, V.at("cum"))
            nc.vector.tensor_scalar(f[0:4, 1, :], f[0:4, 0, :], -1.0, None, ALU.mult)\
                .then_inc(V.sem, V.step("ncum"))
            dve.wait_ge(T.sem, T.at("f"))
            nc.vector.tensor_reduce(st[:, F_MX:F_MX + 4], ps[:, 4:8, 0:128], AX.X, ALU.max)\
                .then_inc(V.sem, V.step("mx0"))
            nc.vector.tensor_reduce(st[:, F_MX + 4:F_MX + 8], ps[:, 4:8, 128:384], AX.X, ALU.max)\
                .then_inc(V.sem, V.step("mx1"))
            dve.wait_ge(V.sem, V.at("mx1"))
            nc.vector.tensor_scalar(st[:, F_NB:F_NB + 8], st[:, F_MX:F_MX + 8], -1.0, None, ALU.mult)\
                .then_inc(V.sem, V.step("nb"))
            dve.wait_ge(A.sem, A.at("x7"))
            nc.vector.reciprocal(st[:, F_RR:F_RR + 8], st[:, F_RS:F_RS + 8])\
                .then_inc(V.sem, V.step("rr"))
            dve.wait_ge(V.sem, V.at("rr"))
            for h in H4:
                for k, s_ in enumerate((slice(0, 128), slice(128, 384))):
                    q = 4 * k + h
                    w_ = fz["p"][:, h, s_]
                    nc.vector.tensor_scalar(w_, w_, st[:, F_RR + q:F_RR + q + 1], None, ALU.mult)\
                        .then_inc(V.sem, V.step(f"n{2 * h + k}"))
            dve.wait_ge(T.sem, T.at("wt"))
            nc.vector.tensor_copy(fz["q"], ps[:, 0:4, 0:384])\
                .then_inc(V.sem, V.step("wt"))
            dve.wait_ge(T.sem, T.at("yb"))
            nc.vector.tensor_copy(og[:, 4:8, 0:256], ps[:, 4:8, 0:256])\
                .then_inc(V.sem, V.step("yb"))

        SM = phase("mix", a="sg0 sg1 sg2 sg3 sg4 sg5", v="ma0 mb0 mc0 s0 o0 ma1 mb1 mc1 s1 o1")
        split_y = Split("split_y", og, (gh, gl), SEQ)
        fm = carve([("pair", PAIR), ("sg", 6, 256), ("ta", 2, 256), ("tb", 2, 256), ("tc", 2, 256)])
        BANK = ((2, 3, 0), (1, 2, 3))

        def mix_pe(pe):
            A, V = SM["a"], SM["v"]
            split_y.pe(pe)

            def body(i):
                for t in range(6):
                    if t < 4:
                        if ran(i - 1):
                            pe.wait_ge(V.sem, V.at(("mc0", "ma1", "mb1", "mc1")[t], i - 1))
                    else:
                        pe.wait_ge(A.sem, A.at(f"sg{t - 4}", i))
                    tile(pe, "mix", t, i, 8, [(ps[:, t % 4, :], hh, hl, ALL)], SEQ).then_inc(tile_done, 1)
                for jj in range(2):
                    if jj:
                        pe.wait_ge(V.sem, V.at("mb0", i))
                    else:
                        pe.wait_ge(A.sem, A.at("sg4", i))
                    if jj:
                        pe.wait_ge(A.sem, A.at("sg5", i))
                    tile(pe, "mix", 6 + jj, i, 8,
                         [(ps[:, BANK[jj][k], :], gh, gl, kts)
                          for k, kts in enumerate((range(0, 4), range(4, 8), range(8, 16)))], SEQ)\
                        .then_inc(tile_done, 1)
            repeat(pe, 8, body)

        def mix_act(act):
            def body(i):
                for t in range(6):
                    act.wait_ge(tile_done, done("mix", t, i, 8))
                    if ran(i - 1):
                        act.wait_ge(SM["v"].sem, SM["v"].at("mc1", i - 1))
                    nc.scalar.activation(fm["sg"][:, t, :], ps[:, t % 4, 0:256], ACT.Sigmoid)\
                        .then_inc(SM["a"].sem, SM["a"].step(f"sg{t}"))
                    round_weights(act, "mix", t + 2, i, 8)
                round_weights(act, "mix", 8, i, 8)
                round_weights(act, "mix", 9, i, 8)
            repeat(act, 8, body)

        def mix_dve(dve):
            V = SM["v"]

            def body(i):
                for jj in range(2):
                    dve.wait_ge(tile_done, done("mix", 6 + jj, i, 8))
                    dve.wait_ge(SM["a"].sem, SM["a"].at("sg5", i))
                    for k, n in enumerate("abc"):
                        nc.vector.tensor_tensor(fm["t" + n][:, jj, :], ps[:, BANK[jj][k], 0:256],
                                                       fm["sg"][:, 2 * k + jj, :], ALU.mult)\
                            .then_inc(V.sem, V.step(f"m{n}{jj}"))
                    dve.wait_ge(V.sem, V.at(f"mc{jj}", i))
                    ta = fm["ta"][:, jj:jj + 1, :]
                    nc.vector.tensor_tensor(ta, ta, fm["tb"][:, jj:jj + 1, :], ALU.add)\
                        .then_inc(V.sem, V.step(f"s{jj}"))
                    dve.wait_ge(V.sem, V.at(f"s{jj}", i))
                    nc.vector.tensor_tensor(og[:, bass.ds(2 * i + jj, 1), 0:256], ta,
                                                   fm["tc"][:, jj:jj + 1, :], ALU.add)\
                        .then_inc(V.sem, V.step(f"o{jj}"))
            repeat(dve, 8, body)

        split_m = Split("split_m", og, (hh, hl), SEQ)
        mix_out = Product("mix_out", "mix_out", (hh, hl), SEQ, og, add=False)
        norm_post = Norm("norm_post", og, SEQ, 1, [("mix_post", og, None)], residual=xT)
        split_mlp = Split("split_mlp", og, (hh, hl), SEQ)
        norm_mlp = Norm("norm_mlp", xT, SEQ, 1, [("mlp_pre", og, split_mlp)])

        SU = phase("mlp", a=" ".join(f"relu{t} hi{t}" for t in range(16)),
                   v=" ".join(f"sq{t} lo{t}" for t in range(16)) + " " + " ".join(f"d{t}" for t in range(16)))
        fu = carve([("pair", PAIR), ("r", 4, 256), ("sq", 4, 256)])

        def mlp_pe(pe):
            A, V = SU["a"], SU["v"]
            split_mlp.pe(pe)

            def body(i):
                for t in range(16):
                    if t >= 4:
                        pe.wait_ge(A.sem, A.at(f"relu{t - 4}", i))
                    elif ran(i - 1):
                        pe.wait_ge(V.sem, V.at(f"d{t + 12}", i - 1))
                    tile(pe, "mlp", t, i, 32, [(ps[:, t % 4, :], hh, hl, ALL)], SEQ).then_inc(tile_done, 1)
                pe.wait_ge(A.sem, A.at("hi15", i))
                pe.wait_ge(V.sem, V.at("lo15", i))
                for t in range(16):
                    if t >= 4:
                        pe.wait_ge(V.sem, V.at(f"d{t - 4}", i))
                    tile(pe, "mlp", 16 + t, i, 32, [(ps[:, t % 4, :], gh, gl, ALL)], SEQ).then_inc(tile_done, 1)
            repeat(pe, 4, body)

        def mlp_act(act):
            A, V = SU["a"], SU["v"]

            def body(i):
                if ran(i - 1):
                    round_weights(act, "mlp", 0, i, 32)
                if ran(i - 1):
                    round_weights(act, "mlp", 1, i, 32)
                for t in range(16):
                    act.wait_ge(tile_done, done("mlp", t, i, 32))
                    if t >= 4:
                        act.wait_ge(V.sem, V.at(f"sq{t - 4}", i))
                    elif ran(i - 1):
                        act.wait_ge(V.sem, V.at(f"sq{t + 12}", i - 1))
                    nc.scalar.activation(fu["r"][:, t % 4, :], ps[:, t % 4, 0:256], ACT.Relu)\
                        .then_inc(A.sem, A.step(f"relu{t}"))
                    round_weights(act, "mlp", t + 2, i, 32)
                    act.wait_ge(A.sem, A.at(f"relu{t}", i))
                    nc.scalar.activation(gh[:, t, :], fu["r"][:, t % 4, :], ACT.Square)\
                        .then_inc(A.sem, A.step(f"hi{t}"))
                for t in range(14):
                    round_weights(act, "mlp", t + 18, i, 32)
            repeat(act, 4, body)

        def mlp_dve(dve):
            A, V = SU["a"], SU["v"]

            def body(i):
                for t in range(16):
                    dve.wait_ge(A.sem, A.at(f"relu{t}", i))
                    sq, r_ = fu["sq"][:, t % 4, :], fu["r"][:, t % 4, :]
                    nc.vector.tensor_tensor(sq, r_, r_, ALU.mult)\
                        .then_inc(V.sem, V.step(f"sq{t}"))
                    dve.wait_ge(A.sem, A.at(f"hi{t}", i))
                    dve.wait_ge(V.sem, V.at(f"sq{t}", i))
                    nc.vector.tensor_tensor(gl[:, t, :], sq, gh[:, t, :].bitcast(F32), ALU.subtract)\
                        .then_inc(V.sem, V.step(f"lo{t}"))
                for t in range(16):
                    dve.wait_ge(tile_done, done("mlp", 16 + t, i, 32))
                    if ran(i - 1):
                        nc.vector.tensor_tensor(og[:, t, 0:256], ps[:, t % 4, 0:256], og[:, t, 0:256], ALU.add)\
                            .then_inc(V.sem, V.step(f"d{t}"))
                    else:
                        nc.vector.tensor_copy(og[:, t, 0:256], ps[:, t % 4, 0:256])\
                            .then_inc(V.sem, V.step(f"d{t}"))
            repeat(dve, 4, body)

        norm_out = Norm("norm_out", og, SEQ, 1, [("mlp_post", og, None)], residual=xT)

        block = ctx.enter_context(nc.Block())

        @block.sync
        def _(sp):
            sp.dma_start(xT[:, :, :], x).then_inc(x_in, 16)
            for s in range(4):
                sp.dma_start(raw[:, s, :, :].rearrange("p a b -> p (a b)"), w[:, s, :])\
                    .then_inc(raw_in[s // 2], 16)
            sp.dma_start(C[:, :], consts).then_inc(cp_in, 16)
            sp.dma_start(P[:, :], params).then_inc(cp_in, 16)

            def load(n, slot):
                sp.dma_start(raw[:, slot, :, :].rearrange("p a b -> p (a b)").unsqueeze(1),
                             w[:, bass.ds(n, 1), :]).then_inc(raw_in[slot // 2], 16)
            with sp.Fori(1, N_TILES // 2) as i:
                for s in range(4):
                    sp.wait_ge(lo_done, 4 * i + s - 3)
                    load(4 * i + s, s)
            sp.wait_ge(norm_out.V.sem, norm_out.V.at(norm_out.last))
            sp.dma_start(out, xT[:, :, 0:SEQ]).then_inc(out_in, 16)
            sp.wait_ge(out_in, 16)

        @block.scalar
        def _(act):
            round_weights(act, "a", 0)
            round_weights(act, "a", 1)
            act.wait_ge(x_in, 16)
            norm_a.act(act)
            lam_act(act)
            attn_a_act(act)
            split_ao.act(act, SA["v"], [SA["v"].at(f"og1", h) for h in (1, 3, 5, 7)])
            a_out.act(act)
            act.wait_ge(a_out.V.sem, a_out.V.at("t7", 1))
            norm_b.act(act)
            kv_act(act)
            attn_b_act(act)
            split_bo.act(act, SB["v"], [SB["v"].at("o3", g) for g in range(4)])
            b_out.act(act)
            act.wait_ge(b_out.V.sem, b_out.V.at("t7", 1))
            norm_fin.act(act)
            act.wait_ge(norm_fin.V.sem, norm_fin.V.at(norm_fin.last))
            norm_mix.act(act)
            rw_in_act(act)
            rwkv_act(act)
            zp_act(act)
            attn_z_act(act)
            split_y.act(act, ST["v"], [ST["v"].at("yb")] * 4)
            mix_act(act)
            split_m.act(act, SM["v"], [SM["v"].at("o1", g) for g in (1, 3, 5, 7)])
            mix_out.act(act)
            act.wait_ge(mix_out.V.sem, mix_out.V.at("t7", 1))
            norm_post.act(act)
            act.wait_ge(norm_post.V.sem, norm_post.V.at(norm_post.last))
            norm_mlp.act(act)
            mlp_act(act)
            act.wait_ge(SU["v"].sem, SU["v"].at("d15", 3))
            norm_out.act(act)

        @block.vector
        def _(dve):
            for k, value in enumerate((1e-5, 1e-6, 64e-5, 1.0)):
                nc.vector.memset(eps[:, k:k + 1], value).then_inc(eps_set, 1)
            nc.vector.memset(st[:, :], 1.0).then_inc(eps_set, 1)
            dve.wait_ge(eps_set, 5)
            dve.wait_ge(cp_in, 32)
            norm_a.dve(dve)
            lam_dve(dve)
            attn_a_dve(dve)
            split_ao.dve(dve)
            a_out.dve(dve)
            dve.wait_ge(a_out.V.sem, a_out.V.at("t7", 1))
            norm_b.dve(dve)
            kv_dve(dve)
            attn_b_dve(dve)
            split_bo.dve(dve)
            b_out.dve(dve)
            dve.wait_ge(b_out.V.sem, b_out.V.at("t7", 1))
            norm_fin.dve(dve)
            dve.wait_ge(norm_fin.V.sem, norm_fin.V.at(norm_fin.last))
            norm_mix.dve(dve)
            rw_in_dve(dve)
            rwkv_dve(dve)
            zp_dve(dve)
            attn_z_dve(dve)
            split_y.dve(dve)
            mix_dve(dve)
            split_m.dve(dve)
            mix_out.dve(dve)
            dve.wait_ge(mix_out.V.sem, mix_out.V.at("t7", 1))
            norm_post.dve(dve)
            dve.wait_ge(norm_post.V.sem, norm_post.V.at(norm_post.last))
            norm_mlp.dve(dve)
            mlp_dve(dve)
            dve.wait_ge(SU["v"].sem, SU["v"].at("d15", 3))
            norm_out.dve(dve)

        @block.tensor
        def _(pe):
            pe.wait_ge(cp_in, 32)
            norm_a.pe(pe)
            lam_pe(pe)
            attn_a_pe(pe)
            split_ao.pe(pe)
            a_out.pe(pe)
            norm_b.pe(pe)
            kv_pe(pe)
            attn_b_pe(pe)
            split_bo.pe(pe)
            b_out.pe(pe)
            norm_fin.pe(pe)
            norm_mix.pe(pe)
            rw_in_pe(pe)
            rwkv_pe(pe)
            zp_pe(pe)
            attn_z_pe(pe)
            mix_pe(pe)
            split_m.pe(pe)
            mix_out.pe(pe)
            norm_post.pe(pe)
            norm_mlp.pe(pe)
            mlp_pe(pe)
            norm_out.pe(pe)

        @block.gpsimd
        def _(pool):
            def rest(i, s):
                if s % 2 == 0:
                    pool.wait_ge(hi_done, 2 * i + s // 2 + 1)
                h = slice(8 * (s % 2), 8 * (s % 2) + 8)
                nc.gpsimd.tensor_tensor(wl[:, s // 2, h, :], raw[:, s, :, :],
                                        wh[:, s // 2, h, :].bitcast(F32), ALU.subtract)\
                    .then_inc(lo_done, 1)
            with pool.Fori(0, N_TILES // 2) as i:
                for s in range(4):
                    rest(i, s)


def constants():
    q = np.arange(128)
    same = (q[:, None] // 64) == (q[None, :] // 64)
    col, row = q[None, :], q[:, None]
    t = {
        "ident": np.eye(128), "ones": np.ones((128, 128)), "hones": same, "tri": row >= col,
        "after": col > row, "not_after": np.where(col <= row, NEG, 0), "future": np.where(col > row, NEG, 0),
        "strict": same & (row < col), "incl": same & (row <= col),
    }
    for b in LEVELS:
        t[f"lev{b}"] = (row // (2 * b) == col // (2 * b)) & ((row // b) % 2 == 0) & ((col // b) % 2 == 1)
    t["lev1t"] = t["lev1"].T
    t["reset"] = np.broadcast_to(np.arange(256) % 64 != 0, (128, 256))
    pos = np.concatenate([np.arange(SEQ) + META, np.arange(META)]).astype(np.float32)
    for name, dim in (("a", 32), ("b", 16)):
        inv = np.float32(ROPE_THETA) ** (-np.arange(0, dim, 2, dtype=np.float32) / np.float32(dim))
        ang = (pos[None, :] * inv[:, None]).astype(np.float32)
        cos, sin = np.ones((128, NT)), np.zeros((128, NT))
        for r in range(0, 128, 64 if name == "b" else 128):
            half = dim // 2
            cos[r:r + half] = cos[r + half:r + dim] = np.cos(ang)
            sin[r:r + half], sin[r + half:r + dim] = -np.sin(ang), np.sin(ang)
        t[f"cos_{name}"], t[f"sin_{name}"] = cos, sin
    t["low"] = np.broadcast_to(q < 64, (128, 128))
    t["high"] = np.broadcast_to(q >= 64, (128, 128))
    t["neg"] = np.full((128, 64), NEG)
    t["sel"] = np.repeat(np.eye(128)[:, 0:4], 128, axis=1)
    c = np.zeros((128, C_N), np.float32)
    for name, (a, b) in C_AT.items():
        c[:, a:b] = t[name]
    return c


def lay_out(w):
    tiles = np.zeros((128, N_TILES, TILE), np.float32)
    n = 0

    def put(m):
        nonlocal n
        for k in range(0, m.shape[1], 128):
            cols = m[:, k:k + 128]
            c = cols.shape[1]
            tiles[:, n].reshape(128, 16, 128)[:, :, 0:c] = cols.reshape(16, 128, c).transpose(1, 0, 2)
            n += 1

    a, b, z = w["a_w_in"][0], w["b_w_in"][0], w["w_in_2"][0]
    for h in range(HEADS_A):
        for part in range(4):
            put(a[:, D * part + 256 * h:D * part + 256 * h + 256])
    for g in range(8):
        put(w["a_w_out"][0][:, 256 * g:256 * g + 256])
    for g in range(2):
        put(w["w_kv"][:, 256 * g:256 * g + 256])
    for g in range(GROUPS_B):
        for part in range(2):
            for k in range(2):
                c = D * part + 512 * g + 256 * k
                put(b[:, c:c + 256])
    for g in range(8):
        put(w["b_w_out"][0][:, 256 * g:256 * g + 256])
    for g in range(12):
        put(z[:, IN_R + 256 * g:IN_R + 256 * g + 256])
    wa, gates = IN_R + 3072, IN_R + 3072 + 288
    put(z[:, wa:wa + 128])
    put(z[:, 3072:3076])
    put(z[:, wa + 128:wa + 288])
    lora = np.zeros((128, 3072), np.float32)
    lora[0:64, 0:1024] = w["rwkv_w_up_2"][0]
    lora[64:128, 0:1024] = w["rwkv_a_up_2"][0]
    lora[:, 1024:2048] = w["rwkv_g_up_2"][0][0:128]
    lora[0:32, 2048:3072] = w["rwkv_g_up_2"][0][128:160]
    for g in range(12):
        put(z[:, 256 * g:256 * g + 256])
    for g in range(8):
        for part in range(3):
            c = gates + D * part + 256 * g
            put(z[:, c:c + 256])
        put(np.concatenate([w[f"w_branch_{k}_2"][0][:, 256 * g:256 * g + 256] for k in "abc"]))
    for g in range(8):
        put(w["w_out_2"][0][:, 256 * g:256 * g + 256])
    for b_ in range(4):
        f = slice(2048 * b_, 2048 * b_ + 2048)
        put(w["w_mlp_up_2"][0][:, f])
        put(w["w_mlp_down_2"][0][f, :])
    assert n == N_TILES

    p = np.zeros((128, P_N), np.float32)

    def cols(name, v, k=0):
        v = np.asarray(v).reshape(-1)
        rows = min(128, len(v))
        v = v.reshape(-1, rows).T
        p[0:rows, P_AT[name][0] + k:P_AT[name][0] + k + v.shape[1]] = v

    for name, key in (("a", "a_norm"), ("kv", "kv_norm"), ("b", "b_norm"), ("fin", "final_norm"),
                      ("mix_pre", "norm_mix_pre_2"), ("mix_post", "norm_mix_post_2"),
                      ("mlp_pre", "norm_mlp_pre_2"), ("mlp_post", "norm_mlp_post_2")):
        cols(name, w[key])
    for k, key in enumerate(("q1", "k1", "q2", "k2")):
        cols("lam", w["a_lambda_" + key], k)
    cols("subln", w["a_subln"])
    p[:, P_AT["sinks"][0]:P_AT["sinks"][1]] = w["b_sinks"].reshape(1, -1)
    mu = w["rwkv_mu_2"][0]
    cols("mu_wa", mu[3072:3200])
    cols("mu_g", mu[3200:3328])
    cols("mu_g", mu[3328:3360], 1)
    cols("bf", w["b_forget_2"])
    for j in range(RW_TILES):
        f = slice(128 * j, 128 * j + 128)
        parts = [mu[0:1024], mu[1024:2048], mu[2048:3072]] + [
            w[f"rwkv_{k}_2"].reshape(-1) for k in ("w0", "a0", "k_k", "k_a", "r_k", "ln_w", "ln_b")]
        for k, v in enumerate(parts):
            cols("rw", v[f], 10 * j + k)
    return tiles.reshape(128, 2 * N_TILES, TILE // 2), lora, p


def kernel(**inputs):
    import concourse.bacc as _bacc
    from concourse.bass_utils import run_bass_kernel_spmd as _run

    w = {k: np.asarray(v) for k, v in inputs.items()}
    tiles, lora, p = lay_out(w)
    x = np.concatenate([w["x"][0], w["meta_tokens"]]).T.reshape(KT, 128, NT).transpose(1, 0, 2)
    arrays = {"weights": tiles, "tokens": np.ascontiguousarray(x), "params": p, "consts": constants(),
              "lora": lora}
    nc = _bacc.Bacc("TRN2", target_bir_lowering=False, num_devices=1)
    args = [nc.dram_tensor(n, a.shape, F32, kind="ExternalInput").ap() for n, a in arrays.items()]
    out = nc.dram_tensor("out", [128, KT, SEQ], F32, kind="ExternalOutput").ap()
    build(nc, *args, out)
    r = _run(nc, [arrays], core_ids=[0]).results[0]["out"]
    return np.ascontiguousarray(r.transpose(2, 1, 0)).reshape(1, SEQ, D)
```

```python
from contextlib import ExitStack

import concourse.bass as bass
import numpy as np
from concourse import mybir

ALU = mybir.AluOpType
ACT = mybir.ActivationFunctionType
F32 = mybir.dt.float32
F32R = mybir.dt.float32r
AX = mybir.AxisListType

D = 2048
SEQ = 256
META = 16
NT = SEQ + META
KT = D // 128
CHUNK = 64
TILE = 16 * 128
NEG = -1e30
HEADS_A = 8
GROUPS_B = 4
SB_HEADS = 4
RW_TILES = 8
FF_TILES = 64
ROPE_THETA = 500000.0
SCALE_A = 128 ** -0.5
SCALE_B = 64 ** -0.5
SCALE_Z = 128 ** -0.5
LAMBDA_INIT = 0.8 - 0.6
DECAY = float(np.exp(-0.5))
IN_R = 3076

TILES = [("a", 8 * HEADS_A), ("a_out", 16), ("kv", 4), ("b", 8 * GROUPS_B), ("b_out", 16), ("rw", 3),
         ("small", 4), ("fill", 8 * RW_TILES - 3), ("mix", 48), ("mix_out", 16), ("mlp", 2 * FF_TILES)]
FIRST = {}
for _name, _n in TILES:
    FIRST[_name] = sum(n for _, n in TILES[:len(FIRST)])
N_TILES = sum(n for _, n in TILES)


def columns(sizes):
    at, n = {}, 0
    for name, size in sizes:
        at[name] = (n, n + size)
        n += size
    return at, n


P_AT, P_N = columns([(g, KT) for g in ("a", "kv", "b", "fin", "mix_pre", "mix_post", "mlp_pre", "mlp_post")]
                    + [("lam", 4), ("subln", 2), ("sinks", 32), ("mu_wa", 1), ("mu_g", 2), ("bf", 1),
                       ("rw", 10 * RW_TILES)])
MU_R, MU_K, MU_V, W0, A0, K_K, K_A, R_K, LN_W, LN_B = range(10)
LEVELS = (1, 2, 4, 8, 16, 32)
C_AT, C_N = columns([("ident", 128), ("ones", 128), ("hones", 128), ("tri", 128), ("after", 128),
                     ("not_after", 128), ("future", 128), ("strict", 128), ("incl", 128), ("lev1t", 128)]
                    + [(f"lev{b}", 128) for b in LEVELS]
                    + [("reset", 256), ("cos_a", NT), ("sin_a", NT), ("cos_b", NT), ("sin_b", NT),
                       ("low", 128), ("high", 128), ("neg", 64), ("sel", 4 * 128)])


class Steps:

    def __init__(self, sem, names):
        self.sem, self.per = sem, len(names)
        self.at_ = {n: k + 1 for k, n in enumerate(names)}
        assert len(self.at_) == self.per
        self.now = 0

    def step(self, name):
        self.now += 1
        if self.at_[name] != self.now:
            raise ValueError(f"step {name} out of order, at {self.now}")
        self.now %= self.per
        return 1

    def at(self, name, i=0):
        return self.at_[name] + self.per * i


def ran(i):
    return not isinstance(i, int) or i >= 0


def repeat(eng, n, body):
    body(0)
    if n > 1:
        with eng.Fori(1, n) as i:
            body(i)


def runs(eng, n, body):
    body(0)
    with eng.Fori(1, n - 1) as i:
        body(i)
    body(n - 1)


def build(nc, w, x, params, consts, lora, out):
    with ExitStack() as ctx:
        def sb(name, shape, dtype=F32):
            return ctx.enter_context(nc.sbuf_tensor(name, shape, dtype))

        def sem(name):
            return ctx.enter_context(nc.semaphore(name))

        raw = sb("raw", [128, 4, 8, 128])
        wh, wl = sb("wh", [128, 2, 16, 128], F32R), sb("wl", [128, 2, 16, 128], F32R)
        C = sb("C", [128, C_N])
        P = sb("P", [128, P_N])
        xT = sb("xT", [128, KT, NT])
        hh, hl = sb("hh", [128, KT, NT], F32R), sb("hl", [128, KT, NT], F32R)
        og = sb("og", [128, KT, NT])
        st = sb("st", [128, 64])
        eps = sb("eps", [128, 4])
        ARENA = nc.sbuf_bytes_remaining // 4 - 8
        with nc.sbuf_tensor("arena", [128, ARENA], F32) as arena:
            pass
        gh, gl = sb("gh", [128, KT, SEQ], F32R), sb("gl", [128, KT, SEQ], F32R)
        PAIR = 2 * KT * SEQ
        ps = ctx.enter_context(nc.psum_tensor("ps", [128, 8, 512], F32))

        def c(name, rows=128):
            a, b = C_AT[name]
            return C[0:rows, a:b]

        def p(name, k=0, rows=128):
            return P[0:rows, P_AT[name][0] + k:P_AT[name][0] + k + 1]

        def carve(sizes):
            got, at = {}, 0
            for name, *shape in sizes:
                n = int(np.prod(shape))
                v = arena[:, at:at + n]
                if len(shape) == 2:
                    v = v.rearrange("p (a b) -> p a b", a=shape[0])
                got[name] = v
                at += n
            if at > ARENA:
                raise ValueError(f"arena: {at} of {ARENA}")
            return got

        raw_in = [sem(f"raw_in{s}") for s in range(2)]
        hi_done, lo_done, tile_done = sem("hi_done"), sem("lo_done"), sem("tile_done")
        lora_in = sem("lora_in")
        x_in, cp_in, out_in = sem("x_in"), sem("cp_in"), sem("out_in")
        eps_set = sem("eps_set")

        def phase(name, **steps):
            return {e: Steps(sem(f"{name}_{e}"), s.split()) for e, s in steps.items()}

        def done(phase_name, t, i=0, per=0):
            return FIRST[phase_name] + t + 1 + per * i

        def round_weights(act, phase_name, t, i=0, per=0):
            m = FIRST[phase_name] + t
            if m >= N_TILES:
                return
            act.wait_ge(raw_in[m % 2], 32 * (m // 2 + 1) + 16 * per * i)
            if m >= 2:
                act.wait_ge(tile_done, m - 1 + per * i)
            nc.scalar.activation(wh[:, m % 2, :, :].rearrange("p a b -> p (a b)"),
                                 raw[:, 2 * (m % 2):2 * (m % 2) + 2, :, :].rearrange("p a b c -> p (a b c)"),
                                 ACT.Copy)\
                .then_inc(hi_done, 1)

        def tile(pe, phase_name, t, i, per, parts, n, m=128, ready=None, late=()):
            q = FIRST[phase_name] + t
            slot = q % 2
            pe.wait_ge(hi_done, q + 1 + per * i)
            for acc, rh, rl, kts in parts:
                for kt in kts:
                    if ready is not None and kt % 4 == 0:
                        pe.wait_ge(ready.V.sem, ready.V.at(f"l{kt // 4}"))
                    if kt == 12:
                        for steps, count in late:
                            pe.wait_ge(steps.sem, count)
                    nc.tensor.matmul(acc[0:m, 0:n], wh[:, slot, kt, 0:m], rh[:, kt, 0:n],
                                     start=(kt == kts[0]), stop=False)
                    nc.tensor.matmul(acc[0:m, 0:n], wh[:, slot, kt, 0:m], rl[:, kt, 0:n],
                                     start=False, stop=False)
            for acc, rh, rl, kts in parts:
                for kt in kts:
                    if kt % 8 == 0:
                        pe.wait_ge(lo_done, 2 * q + kt // 8 + 1 + 2 * per * i)
                    ins = nc.tensor.matmul(acc[0:m, 0:n], wl[:, slot, kt, 0:m], rh[:, kt, 0:n],
                                           start=False, stop=(kt == kts[-1]))
            return ins

        ALL = range(KT)

        def first(i, t, split):
            return split if isinstance(i, int) and i == 0 and t == 0 else None

        def mm(o, lhsT, rhs, start=True, stop=True):
            return nc.tensor.matmul(o, lhsT, rhs, start=start, stop=stop)

        class Split:
            def __init__(self, name, src, pair, n):
                self.src, self.pair, self.n = src, pair, n
                s = phase(name, a="h0 h1 h2 h3", v="l0 l1 l2 l3")
                self.A, self.V = s["a"], s["v"]

            def act(self, eng, V, written):
                for k in range(4):
                    f = slice(4 * k, 4 * k + 4)
                    eng.wait_ge(V.sem, V.at(written[k]) if isinstance(written[k], str) else written[k])
                    nc.scalar.activation(self.pair[0][:, f, 0:self.n], self.src[:, f, 0:self.n], ACT.Copy)\
                        .then_inc(self.A.sem, self.A.step(f"h{k}"))

            def dve(self, eng, quarters=range(4)):
                for k in quarters:
                    f = slice(4 * k, 4 * k + 4)
                    eng.wait_ge(self.A.sem, self.A.at(f"h{k}"))
                    nc.vector.tensor_tensor(self.pair[1][:, f, 0:self.n], self.src[:, f, 0:self.n],
                                            self.pair[0][:, f, 0:self.n].bitcast(F32), ALU.subtract)\
                        .then_inc(self.V.sem, self.V.step(f"l{k}"))

        class Norm:

            def __init__(self, name, src, n, eps_col, outs, residual=None, written=None, after=None):
                self.written, self.after = written, after
                self.src, self.n, self.eps_col, self.outs, self.residual = src, n, eps_col, outs, residual
                s = phase(name, a="sq0 sq1 sq2 sq3 root", t="s0 s1 s2 s3",
                          v="var rstd " + " ".join(
                              f"o{k}_{kt}" + (f" r{kt - 4}" if residual is not None and kt >= 4 else "")
                              for k in range(len(outs)) for kt in range(KT))
                          + (" r12 r13 r14 r15" if residual is not None else ""))
                self.A, self.T, self.V = s["a"], s["t"], s["v"]
                a = carve([("low", ARENA - 9 * NT), ("sq", 2, 4 * NT), ("rstd", NT)])
                self.rstd = a["rstd"][:, 0:n]
                self.sq = [a["sq"][:, k, :].rearrange("p (a b) -> p a b", a=4)[:, :, 0:n] for k in range(2)]
                self.last = f"r{KT - 1}" if residual is not None else f"o{len(outs) - 1}_{KT - 1}"

            def act(self, eng):
                for k in range(4):
                    if self.after is not None and k >= 2:
                        round_weights(eng, self.after, k - 2)
                    if self.written is not None:
                        eng.wait_ge(self.written[0].sem, self.written[1][k])
                    if k >= 2:
                        eng.wait_ge(self.T.sem, self.T.at(f"s{k - 2}"))
                    nc.scalar.activation(self.sq[k % 2], self.src[:, 4 * k:4 * k + 4, 0:self.n],
                                                     ACT.Square)\
                        .then_inc(self.A.sem, self.A.step(f"sq{k}"))
                eng.wait_ge(self.V.sem, self.V.at("var"))
                nc.scalar.activation(self.rstd, self.rstd, ACT.Sqrt)\
                    .then_inc(self.A.sem, self.A.step("root"))
                for k, (gain, dst, split) in enumerate(self.outs):
                    if split is not None:
                        split.act(eng, self.V, [f"o{k}_{4 * j + 3}" for j in range(4)])

            def pe(self, eng):
                for k in range(4):
                    eng.wait_ge(self.A.sem, self.A.at(f"sq{k}"))
                    for j in range(4):
                        ins = mm(ps[:, 7, 0:self.n], c("ones"), self.sq[k % 2][:, j, :],
                                 start=(k == 0 and j == 0), stop=(k == 3 and j == 3))
                    ins\
                        .then_inc(self.T.sem, self.T.step(f"s{k}"))

            def dve(self, eng):
                n, V = self.n, self.V
                eng.wait_ge(self.T.sem, self.T.at("s3"))
                nc.vector.tensor_scalar(self.rstd, ps[:, 7, 0:n], 1.0 / D,
                                               eps[:, self.eps_col:self.eps_col + 1], ALU.mult, ALU.add)\
                    .then_inc(V.sem, V.step("var"))
                eng.wait_ge(self.A.sem, self.A.at("root"))
                nc.vector.reciprocal(self.rstd, self.rstd)\
                    .then_inc(V.sem, V.step("rstd"))
                eng.wait_ge(V.sem, V.at("rstd"))
                def residual(kt):
                    eng.wait_ge(V.sem, V.at(f"o0_{kt}"))
                    x = self.residual[:, kt, 0:n]
                    nc.vector.tensor_tensor(x, x, self.outs[0][1][:, kt, 0:n], ALU.add)\
                        .then_inc(V.sem, V.step(f"r{kt}"))

                for k, (gain, dst, split) in enumerate(self.outs):
                    if k:
                        eng.wait_ge(self.outs[k - 1][2].V.sem, self.outs[k - 1][2].V.at("l3"))
                    for kt in range(KT):
                        nc.vector.scalar_tensor_tensor(
                            out=dst[:, kt, 0:n], in0=self.src[:, kt, 0:n], scalar=p(gain, kt), in1=self.rstd,
                            op0=ALU.mult, op1=ALU.mult)\
                            .then_inc(V.sem, V.step(f"o{k}_{kt}"))
                        if self.residual is not None and kt >= 4:
                            residual(kt - 4)
                        if split is not None and kt % 4 == 3 and kt > 3:
                            eng.wait_ge(V.sem, V.at(f"o{k}_{kt - 4}"))
                            split.dve(eng, range(kt // 4 - 1, kt // 4))
                    if split is not None:
                        eng.wait_ge(V.sem, V.at(f"o{k}_{KT - 1}"))
                        split.dve(eng, range(3, 4))
                if self.residual is not None:
                    for kt in range(KT - 4, KT):
                        residual(kt)

        class Product:
            def __init__(self, name, units, rhs, n, dst, add, split):
                self.split = split
                self.units, self.rhs, self.n, self.dst, self.add = units, rhs, n, dst, add
                self.V = phase(name, v=" ".join(f"t{t}" for t in range(8)))["v"]

            def pe(self, eng):
                def body(i):
                    for t in range(8):
                        if ran(i if t >= 4 else i - 1):
                            eng.wait_ge(self.V.sem, self.V.at(f"t{(t - 4) % 8}", i if t >= 4 else i - 1))
                        tile(eng, self.units, t, i, 8, [(ps[:, t % 4, :], *self.rhs, ALL)], self.n,
                             ready=first(i, t, self.split))\
                            .then_inc(tile_done, 1)
                repeat(eng, 2, body)

            def act(self, eng):
                for t in range(2, 16):
                    round_weights(eng, self.units, t)

            def written(self):
                return self.V, [self.V.at(f"t{(4 * k + 3) % 8}", (4 * k + 3) // 8) for k in range(4)]

            def dve(self, eng):
                def body(i):
                    for t in range(8):
                        eng.wait_ge(tile_done, done(self.units, t, i, 8))
                        o = self.dst[:, bass.ds(8 * i + t, 1), 0:self.n]
                        acc = ps[:, t % 4:t % 4 + 1, 0:self.n]
                        if self.add:
                            nc.vector.tensor_tensor(o, acc, o, ALU.add)\
                                .then_inc(self.V.sem, self.V.step(f"t{t}"))
                        else:
                            nc.vector.tensor_copy(o, acc)\
                                .then_inc(self.V.sem, self.V.step(f"t{t}"))
                repeat(eng, 2, body)

        split_a = Split("split_a", og, (hh, hl), NT)
        norm_a = Norm("norm_a", xT, NT, 0, [("a", og, split_a)], after="a")
        SA = phase("attn_a",
                   a="qk0 qk1 qk2 qk3 v0 v1 e0 e1 e2 e3 e4 e5 g0 g1 wT sqo root",
                   t="scores vt wt pv osum",
                   v="rcos shuf rsin radd mx0 mx1 mxm nb v vm rr rl n0 w0 n1 w1 nm wm wTm var rstd o0 o1 og0 og1")
        fa = carve([("qk", 4, NT), ("sh", 4, NT), ("xc", 4, NT), ("vT", 2, NT), ("v", 3, 256), ("ga", 2, NT), ("p0", 2, 144),
                    ("p1", 2, NT), ("pm", 2, META), ("wT", 384), ("wTm", NT), ("sqo", 2, NT), ("rstd", NT),
                    ("o", 2, NT)])
        A_MX, A_NB, A_RS, A_RR = 0, 6, 12, 18
        LAM = 24
        lam_steps = phase("lam", v="prod1 prod2 diff neg", t="sum", a="exp")

        def lam_pe(pe):
            pe.wait_ge(lam_steps["v"].sem, lam_steps["v"].at("prod2"))
            mm(ps[:, 6, 0:2], c("ones"), st[:, LAM + 1:LAM + 3])\
                .then_inc(lam_steps["t"].sem, lam_steps["t"].step("sum"))

        def lam_act(act):
            act.wait_ge(lam_steps["t"].sem, lam_steps["t"].at("sum"))
            nc.scalar.activation(st[:, LAM + 3:LAM + 5], ps[:, 6, 0:2], ACT.Exp)\
                .then_inc(lam_steps["a"].sem, lam_steps["a"].step("exp"))

        def lam_dve(dve):
            V = lam_steps["v"]
            for k in range(2):
                nc.vector.tensor_tensor(st[:, LAM + 1 + k:LAM + 2 + k], p("lam", 2 * k), p("lam", 2 * k + 1),
                                               ALU.mult)\
                    .then_inc(V.sem, V.step(f"prod{k + 1}"))
            dve.wait_ge(lam_steps["a"].sem, lam_steps["a"].at("exp"))
            nc.vector.tensor_tensor(st[:, LAM:LAM + 1], st[:, LAM + 4:LAM + 5], st[:, LAM + 3:LAM + 4],
                                           ALU.subtract)\
                .then_inc(V.sem, V.step("diff"))
            dve.wait_ge(V.sem, V.at("diff"))
            nc.vector.tensor_scalar(st[:, LAM:LAM + 1], st[:, LAM:LAM + 1], -LAMBDA_INIT, None, ALU.add)\
                .then_inc(V.sem, V.step("neg"))

        def attn_a_pe(pe):
            A, T, V = SA["a"], SA["t"], SA["v"]
            qk, v, p0, p1, pm = fa["qk"], fa["v"], fa["p0"], fa["p1"], fa["pm"]

            def body(i):
                for t in range(6):
                    if t == 0:
                        if ran(i - 1):
                            pe.wait_ge(V.sem, V.at("vm", i - 1))
                    elif t == 1:
                        if ran(i - 1):
                            pe.wait_ge(A.sem, A.at("v1", i - 1))
                    elif t < 4:
                        if ran(i - 1):
                            pe.wait_ge(A.sem, A.at(f"g{t - 2}", i - 1))
                    else:
                        pe.wait_ge(A.sem, A.at(f"qk{t - 4}", i))
                    tile(pe, "a", t, i, 8, [(ps[:, t % 4, :], hh, hl, ALL)], NT,
                         ready=first(i, t, split_a)).then_inc(tile_done, 1)
                pe.wait_ge(V.sem, V.at("radd", i))
                if ran(i - 1):
                    pe.wait_ge(A.sem, A.at("wT", i - 1))
                if ran(i - 1):
                    pe.wait_ge(V.sem, V.at("var", i - 1))
                if ran(i - 1):
                    pe.wait_ge(V.sem, V.at("o1", i - 1))
                for a in range(2):
                    k = qk[:, 2 + a, :]
                    q = qk[:, a, :]
                    o = ps[:, 4, 144 * a:144 * a + 144]
                    mm(o[:, 128:144], q[:, 0:128], k[:, 256:NT])
                    mm(o[:, 0:128], q[:, 0:128], k[:, 0:128], stop=False)
                    mm(o[:, 64:128], c("low", 1), c("neg", 1), start=False)
                    o = ps[:, 5 + a, :]
                    mm(o[:, 0:NT], q[:, 128:256], k, stop=False)
                    mm(o[:, 192:256], c("low", 1), c("neg", 1), start=False)
                    ins = mm(ps[0:META, 4, 288 + META * a:288 + META * (a + 1)], q[:, 256:NT], k[:, 256:NT])
                ins\
                    .then_inc(T.sem, T.step("scores"))
                pe.wait_ge(A.sem, A.at("v1", i))
                if ran(i - 1):
                    pe.wait_ge(V.sem, V.at("o1", i - 1))
                for tok in range(2):
                    for d in range(2):
                        nc.tensor.transpose(ps[:, 7, 256 * tok + 128 * d:256 * tok + 128 * d + 128],
                                            fa["vT"][:, d, 128 * tok:128 * tok + 128], c("ident"))
                for d in range(2):
                    ins = nc.tensor.transpose(ps[0:META, 0, 128 * d:128 * d + 128], fa["vT"][:, d, 256:NT], c("ident"))
                ins\
                    .then_inc(T.sem, T.step("vt"))
                for t in (6, 7):
                    pe.wait_ge(A.sem, A.at(f"qk{t - 4}", i))
                    tile(pe, "a", t, i, 8, [(ps[:, t % 4, :], hh, hl, ALL)], NT).then_inc(tile_done, 1)
                pe.wait_ge(V.sem, V.at("wm", i))
                pe.wait_ge(A.sem, A.at("e5", i))
                nc.tensor.transpose(ps[:, 4, 0:128], p0[:, 0, 0:128], c("ident"))
                nc.tensor.transpose(ps[:, 4, 128:256], p1[:, 0, 0:128], c("ident"))
                nc.tensor.transpose(ps[:, 4, 256:384], p1[:, 0, 128:256], c("ident"))
                nc.tensor.transpose(ps[0:META, 5, 0:128], p0[:, 0, 128:144], c("ident"))
                nc.tensor.transpose(ps[0:META, 5, 128:256], p1[:, 0, 256:NT], c("ident"))
                nc.tensor.transpose(ps[0:META, 5, 256:NT], pm[0:META, 0, :], c("ident", META)[:, 0:META])\
                    .then_inc(T.sem, T.step("wt"))
                pe.wait_ge(A.sem, A.at("wT", i))
                pe.wait_ge(V.sem, V.at("wTm", i))
                for d in range(2):
                    o = ps[:, 6 + d, :]
                    f = slice(128 * d, 128 * d + 128)
                    mm(o[:, 0:NT], v[0:META, 2, f], fa["wTm"][0:META, :], stop=False)
                    mm(o[:, 0:256], v[:, 0, f], fa["wT"][:, 0:256], start=False, stop=False)
                    ins = mm(o[:, 128:256], v[:, 1, f], fa["wT"][:, 256:384], start=False)
                ins\
                    .then_inc(T.sem, T.step("pv"))
                pe.wait_ge(A.sem, A.at("sqo", i))
                for d in range(2):
                    ins = mm(ps[:, 5, 0:NT], c("ones"), fa["sqo"][:, d, :], start=(d == 0), stop=(d == 1))
                ins\
                    .then_inc(T.sem, T.step("osum"))
            repeat(pe, HEADS_A, body)

        def attn_a_act(act):
            A, T, V = SA["a"], SA["t"], SA["v"]

            def body(i):
                for t in range(4):
                    act.wait_ge(tile_done, done("a", t, i, 8))
                    if ran(i - 1):
                        act.wait_ge(T.sem, T.at("scores", i - 1))
                    nc.scalar.activation(fa["qk"][:, t, :], ps[:, t, 0:NT], ACT.Copy)\
                        .then_inc(A.sem, A.step(f"qk{t}"))
                    round_weights(act, "a", t + 2, i, 8)
                for d in range(2):
                    act.wait_ge(tile_done, done("a", 4 + d, i, 8))
                    if ran(i - 1):
                        act.wait_ge(T.sem, T.at("vt", i - 1))
                    nc.scalar.activation(fa["vT"][:, d, :], ps[:, d, 0:NT], ACT.Copy)\
                        .then_inc(A.sem, A.step(f"v{d}"))
                    round_weights(act, "a", d + 6, i, 8)
                act.wait_ge(V.sem, V.at("nb", i))
                if ran(i - 1):
                    act.wait_ge(T.sem, T.at("wt", i - 1))

                def e(k, rows, o, s):
                    nc.scalar.activation(o, s, ACT.Exp, bias=st[0:rows, A_NB + k:A_NB + k + 1], scale=SCALE_A,
                                                accum_out=st[0:rows, A_RS + k:A_RS + k + 1])\
                        .then_inc(A.sem, A.step(f"e{k}"))
                for a in range(2):
                    e(a, 128, fa["p0"][:, a, :], ps[:, 4, 144 * a:144 * a + 144])
                for a in range(2):
                    e(2 + a, 128, fa["p1"][:, a, :], ps[:, 5 + a, 0:NT])
                for a in range(2):
                    e(4 + a, META, fa["pm"][0:META, a, :], ps[0:META, 4, 288 + META * a:288 + META * (a + 1)])
                for d in range(2):
                    act.wait_ge(tile_done, done("a", 6 + d, i, 8))
                    if ran(i - 1):
                        act.wait_ge(V.sem, V.at("og1", i - 1))
                    nc.scalar.activation(fa["ga"][:, d, :], ps[:, 2 + d, 0:NT], ACT.Silu)\
                        .then_inc(A.sem, A.step(f"g{d}"))
                    round_weights(act, "a", d + 8, i, 8)
                act.wait_ge(T.sem, T.at("wt", i))
                nc.scalar.activation(fa["wT"], ps[:, 4, 0:384], ACT.Copy)\
                    .then_inc(A.sem, A.step("wT"))
                act.wait_ge(T.sem, T.at("pv", i))
                nc.scalar.activation(fa["sqo"], ps[:, 6:8, 0:NT], ACT.Square)\
                    .then_inc(A.sem, A.step("sqo"))
                act.wait_ge(V.sem, V.at("var", i))
                nc.scalar.activation(fa["rstd"], fa["rstd"], ACT.Sqrt)\
                    .then_inc(A.sem, A.step("root"))
            repeat(act, HEADS_A, body)

        def attn_a_dve(dve):
            A, T, V = SA["a"], SA["t"], SA["v"]
            swap = [(r + 16) % 32 for r in range(32)]
            x, xc, sh = fa["qk"][0:32], fa["xc"][0:32], fa["sh"][0:32]
            cos = c("cos_a", 32).unsqueeze(1).to_broadcast([32, 4, NT])
            sin = c("sin_a", 32).unsqueeze(1).to_broadcast([32, 4, NT])
            p0, p1, pm = fa["p0"], fa["p1"], fa["pm"]

            def body(i):
                dve.wait_ge(A.sem, A.at("qk3", i))
                nc.vector.tensor_tensor(xc, x, cos, ALU.mult)\
                    .then_inc(V.sem, V.step("rcos"))
                nc.vector.stream_shuffle(sh, x, swap)\
                    .then_inc(V.sem, V.step("shuf"))
                dve.wait_ge(V.sem, V.at("shuf", i))
                nc.vector.tensor_tensor(sh, sh, sin, ALU.mult)\
                    .then_inc(V.sem, V.step("rsin"))
                dve.wait_ge(V.sem, V.at("rsin", i))
                nc.vector.tensor_tensor(x, xc, sh, ALU.add)\
                    .then_inc(V.sem, V.step("radd"))
                dve.wait_ge(T.sem, T.at("scores", i))
                nc.vector.tensor_reduce(st[:, 0:2], ps[:, 4, 0:288].rearrange("p (a b) -> p a b", a=2),
                                               AX.X, ALU.max)\
                    .then_inc(V.sem, V.step("mx0"))
                nc.vector.tensor_reduce(st[:, 2:4], ps[:, 5:7, 0:NT], AX.X, ALU.max)\
                    .then_inc(V.sem, V.step("mx1"))
                nc.vector.tensor_reduce(st[0:META, 4:6],
                                               ps[0:META, 4, 288:320].rearrange("p (a b) -> p a b", a=2),
                                               AX.X, ALU.max)\
                    .then_inc(V.sem, V.step("mxm"))
                dve.wait_ge(V.sem, V.at("mxm", i))
                nc.vector.tensor_scalar(st[:, A_NB:A_NB + 6], st[:, A_MX:A_MX + 6], -SCALE_A, None, ALU.mult)\
                    .then_inc(V.sem, V.step("nb"))
                dve.wait_ge(T.sem, T.at("vt", i))
                if ran(i - 1):
                    dve.wait_ge(T.sem, T.at("pv", i - 1))
                nc.vector.tensor_copy(fa["v"][:, 0:2, :], ps[:, 7, :].rearrange("p (a b) -> p a b", a=2))\
                    .then_inc(V.sem, V.step("v"))
                nc.vector.tensor_copy(fa["v"][0:META, 2, :], ps[0:META, 0, 0:256])\
                    .then_inc(V.sem, V.step("vm"))
                dve.wait_ge(A.sem, A.at("e5", i))
                nc.vector.reciprocal(st[:, A_RR:A_RR + 6], st[:, A_RS:A_RS + 6])\
                    .then_inc(V.sem, V.step("rr"))
                dve.wait_ge(V.sem, V.at("rr", i))
                odd = st[:, A_RR:A_RR + 6].rearrange("p (a b) -> p a b", b=2)[:, :, 1]
                nc.vector.tensor_scalar(odd, odd, st[:, LAM:LAM + 1], None, ALU.mult)\
                    .then_inc(V.sem, V.step("rl"))
                dve.wait_ge(V.sem, V.at("rl", i))
                for k, (w_, rows) in enumerate(((p0, 128), (p1, 128), (pm, META))):
                    r = A_RR + 2 * k
                    s = "01m"[k]
                    nc.vector.tensor_scalar(w_[0:rows, 0, :], w_[0:rows, 0, :], st[0:rows, r:r + 1], None,
                                                   ALU.mult)\
                        .then_inc(V.sem, V.step(f"n{s}"))
                    dve.wait_ge(V.sem, V.at(f"n{s}", i))
                    nc.vector.scalar_tensor_tensor(
                        out=w_[0:rows, 0, :], in0=w_[0:rows, 1, :], scalar=st[0:rows, r + 1:r + 2],
                        in1=w_[0:rows, 0, :], op0=ALU.mult, op1=ALU.add)\
                        .then_inc(V.sem, V.step(f"w{s}"))
                dve.wait_ge(T.sem, T.at("wt", i))
                nc.vector.tensor_copy(fa["wTm"][0:META, :], ps[0:META, 5, 0:NT])\
                    .then_inc(V.sem, V.step("wTm"))
                dve.wait_ge(T.sem, T.at("osum", i))
                nc.vector.tensor_scalar(fa["rstd"], ps[:, 5, 0:NT], 1.0 / 256, eps[:, 0:1], ALU.mult, ALU.add)\
                    .then_inc(V.sem, V.step("var"))
                dve.wait_ge(A.sem, A.at("root", i))
                nc.vector.reciprocal(fa["rstd"], fa["rstd"])\
                    .then_inc(V.sem, V.step("rstd"))
                dve.wait_ge(V.sem, V.at("rstd", i))
                for d in range(2):
                    nc.vector.scalar_tensor_tensor(
                        out=fa["o"][:, d, :], in0=ps[:, 6 + d, 0:NT], scalar=p("subln", d), in1=fa["rstd"],
                        op0=ALU.mult, op1=ALU.mult)\
                        .then_inc(V.sem, V.step(f"o{d}"))
                dve.wait_ge(A.sem, A.at("g1", i))
                for d in range(2):
                    dve.wait_ge(V.sem, V.at(f"o{d}", i))
                    nc.vector.scalar_tensor_tensor(
                        out=og[:, bass.ds(2 * i + d, 1), :], in0=fa["o"][:, d:d + 1, :], scalar=1.0 - LAMBDA_INIT,
                        in1=fa["ga"][:, d:d + 1, :], op0=ALU.mult, op1=ALU.mult)\
                        .then_inc(V.sem, V.step(f"og{d}"))
            repeat(dve, HEADS_A, body)

        split_ao = Split("split_ao", og, (hh, hl), NT)
        a_out = Product("a_out", "a_out", (hh, hl), NT, xT, add=True, split=split_ao)

        split_kv = Split("split_kv", og, (hh, hl), NT)
        split_b = Split("split_b", og, (gh, gl), SEQ)
        norm_b = Norm("norm_b", xT, NT, 0, [("kv", og, split_kv), ("b", og, split_b)],
                      written=a_out.written(), after="kv")
        SK = phase("kv", a="c0 c1 c2 c3", t="vt",
                   v="shuf rsin rcos radd zero " + " ".join(f"k{g}_{h}" for g in range(4) for h in range(2)) + " v vm")
        fb = carve([("pair", PAIR), ("kd", 4, 2 * NT), ("vB", 3, 256), ("kv", 4, NT), ("sh", 2, NT)])

        def kv_pe(pe):
            for t in range(4):
                tile(pe, "kv", t, 0, 0, [(ps[:, t, :], hh, hl, ALL)], NT,
                     ready=first(0, t, split_kv)).then_inc(tile_done, 1)
            pe.wait_ge(SK["a"].sem, SK["a"].at("c3"))
            for tok in range(2):
                for k in range(2):
                    nc.tensor.transpose(ps[:, 4, 256 * tok + 128 * k:256 * tok + 128 * k + 128],
                                        fb["kv"][:, 2 + k, 128 * tok:128 * tok + 128], c("ident"))
            for k in range(2):
                ins = nc.tensor.transpose(ps[0:META, 5, 128 * k:128 * k + 128], fb["kv"][:, 2 + k, 256:NT], c("ident"))
            ins\
                .then_inc(SK["t"].sem, SK["t"].step("vt"))

        def kv_act(act):
            for t in range(4):
                act.wait_ge(tile_done, done("kv", t))
                nc.scalar.activation(fb["kv"][:, t, :], ps[:, t, 0:NT], ACT.Copy)\
                    .then_inc(SK["a"].sem, SK["a"].step(f"c{t}"))
                round_weights(act, "kv", t + 2)

        def kv_dve(dve):
            V = SK["v"]
            swap = [r ^ 8 if r < 16 else r for r in range(32)]
            x, sh = fb["kv"][:, 0:2, :], fb["sh"]
            dve.wait_ge(SK["a"].sem, SK["a"].at("c1"))
            nc.vector.stream_shuffle(sh, x, swap)\
                .then_inc(V.sem, V.step("shuf"))
            dve.wait_ge(V.sem, V.at("shuf"))
            nc.vector.tensor_tensor(sh, sh, c("sin_b").unsqueeze(1).to_broadcast([128, 2, NT]), ALU.mult)\
                .then_inc(V.sem, V.step("rsin"))
            nc.vector.tensor_tensor(x, x, c("cos_b").unsqueeze(1).to_broadcast([128, 2, NT]), ALU.mult)\
                .then_inc(V.sem, V.step("rcos"))
            dve.wait_ge(V.sem, V.at("rcos"))
            nc.vector.tensor_tensor(x, x, sh, ALU.add)\
                .then_inc(V.sem, V.step("radd"))
            nc.vector.memset(fb["kd"], 0.0)\
                .then_inc(V.sem, V.step("zero"))
            dve.wait_ge(V.sem, V.at("zero"))
            for g in range(4):
                for h in range(2):
                    nc.vector.tensor_copy(fb["kd"][64 * h:64 * h + 64, g, NT * h:NT * h + NT],
                                                 fb["kv"][64 * (g % 2):64 * (g % 2) + 64, g // 2, :])\
                        .then_inc(V.sem, V.step(f"k{g}_{h}"))
            dve.wait_ge(SK["t"].sem, SK["t"].at("vt"))
            nc.vector.tensor_copy(fb["vB"][:, 0:2, :], ps[:, 4, :].rearrange("p (a b) -> p a b", a=2))\
                .then_inc(V.sem, V.step("v"))
            nc.vector.tensor_copy(fb["vB"][0:META, 2, :], ps[0:META, 5, 0:256])\
                .then_inc(V.sem, V.step("vm"))

        rounds = " ".join(f"R{j}" for j in range(4))
        SQ = phase("b_q", a="q0 q1 q2 q3")["a"]

        def final(i):
            return isinstance(i, int) and i == GROUPS_B - 1

        SB = phase("attn_b",
                   a=" ".join(f"e{j}_0 e{j}_1 e{j}_2 e{j}_3 es{j} g{j} wk{j}" for j in range(4)),
                   t=" ".join(f"sc{j} wt{j} pv{j}" for j in range(4)),
                   v="kg vg vgm sk rcos shuf rsin radd " + " ".join(
                       f"ma{j} mb{j} sm{j} nb{j} sn{j} den{j} rr{j} p{j}_0 p{j}_1 p{j}_2 p{j}_3 w1{j} wm{j} o{j}"
                       for j in range(4)))
        f2 = carve([("pair", PAIR), ("kd", 4, 2 * NT), ("vB", 3, 256), ("q", 4, 256), ("sh", 4, 256), ("xc", 4, 256), ("kg", 2 * NT), ("vg", 3, 64),
                    ("sk", 8), ("p0", 2, 144), ("p1", 2, NT), ("wk0", 512), ("wk1", 256), ("wkm", 512),
                    ("gb", 4, 256), ("stb", 32)])
        B_MX, B_SM, B_NB, B_SN, B_RS, B_RR = 0, 4, 8, 12, 16, 20

        def attn_b_pe(pe):
            A, T, V = SB["a"], SB["t"], SB["v"]
            q, kg, vg, p0, p1 = f2["q"], f2["kg"], f2["vg"], f2["p0"], f2["p1"]
            pe.wait_ge(split_b.V.sem, split_b.V.at("l3"))
            for t in range(4):
                tile(pe, "b", t, 0, 0, [(ps[:, t, :], gh, gl, ALL)], SEQ).then_inc(tile_done, 1)
            pe.wait_ge(SK["v"].sem, SK["v"].at("vm"))

            def body(i):
                pe.wait_ge(V.sem, V.at("radd", i))
                for j in range(4):
                    if j:
                        pe.wait_ge(V.sem, V.at(f"o{j - 1}", i))
                    else:
                        if ran(i - 1):
                            pe.wait_ge(V.sem, V.at("o3", i - 1))
                    for a in range(2):
                        ka = kg[:, NT * a:NT * a + NT]
                        o = ps[:, 4, 144 * a:144 * a + 144]
                        mm(o[:, 128:144], q[:, j, 0:128], ka[:, 256:NT])
                        mm(o[:, 0:128], q[:, j, 0:128], ka[:, 0:128], stop=False)
                        mm(o[:, 64:128], c("low", 1), c("neg", 1), start=False)
                        o = ps[:, 5 + a, :]
                        mm(o[:, 0:NT], q[:, j, 128:256], ka, stop=False)
                        mm(o[:, 192:256], c("low", 1), c("neg", 1), start=False, stop=False)
                        ins = mm(o[:, 0:64], c("high", 1), c("neg", 1), start=False)
                    ins\
                        .then_inc(T.sem, T.step(f"sc{j}"))
                    if j >= 2:
                        pe.wait_ge(A.sem, A.at(f"g{j - 2}", i))
                    elif ran(i - 1):
                        pe.wait_ge(A.sem, A.at(f"g{j + 2}", i - 1))
                    else:
                        pe.wait_ge(SQ.sem, SQ.at(f"q{j}"))
                    if final(i):
                        tile(pe, "b", 4 + 8 * i + j, 0, 0, [(ps[:, j % 2, :], gh, gl, ALL)], SEQ)\
                            .then_inc(tile_done, 1)
                    else:
                        tile(pe, "b", 4 + 2 * j, i, 8, [(ps[:, j % 2, :], gh, gl, ALL)], SEQ)\
                            .then_inc(tile_done, 1)
                    pe.wait_ge(V.sem, V.at(f"p{j}_3", i))
                    if ran(i if j else i - 1):
                        pe.wait_ge(A.sem, A.at(f"wk{j - 1}" if j else "wk3", i if j else i - 1))
                    for a in range(2):
                        nc.tensor.transpose(ps[:, 7, 256 * a:256 * a + 128], p0[:, a, 0:128], c("ident"))
                        nc.tensor.transpose(ps[:, 7, 256 * a + 128:256 * a + 256], p1[:, a, 0:128], c("ident"))
                        nc.tensor.transpose(ps[:, 4, 128 * a:128 * a + 128], p1[:, a, 128:256], c("ident"))
                        nc.tensor.transpose(ps[0:META, 5, 256 * a:256 * a + 128], p0[:, a, 128:144], c("ident"))
                        ins = nc.tensor.transpose(ps[0:META, 5, 256 * a + 128:256 * a + 256], p1[:, a, 256:NT],
                                                  c("ident"))
                    ins\
                        .then_inc(T.sem, T.step(f"wt{j}"))
                    if not final(i):
                        if j >= 2:
                            pe.wait_ge(SQ.sem, SQ.at(f"q{j - 2}", i + 1))
                        else:
                            pe.wait_ge(SQ.sem, SQ.at(f"q{j + 2}", i))
                        tile(pe, "b", 5 + 2 * j, i, 8, [(ps[:, 2 + j % 2, :], gh, gl, ALL)], SEQ)\
                            .then_inc(tile_done, 1)
                    pe.wait_ge(A.sem, A.at(f"wk{j}", i))
                    pe.wait_ge(V.sem, V.at(f"wm{j}", i))
                    for a in range(2):
                        o = ps[64 * a:64 * a + 64, 6, :]
                        mm(o[:, 0:256], vg[0:META, 2, :], f2["wkm"][0:META, 256 * a:256 * a + 256], stop=False)
                        mm(o[:, 0:256], vg[:, 0, :], f2["wk0"][:, 256 * a:256 * a + 256], start=False, stop=False)
                        ins = mm(o[:, 128:256], vg[:, 1, :], f2["wk1"][:, 128 * a:128 * a + 128], start=False)
                    ins\
                        .then_inc(T.sem, T.step(f"pv{j}"))
            runs(pe, GROUPS_B, body)

        def attn_b_act(act):
            A, T, V = SB["a"], SB["t"], SB["v"]
            stb = f2["stb"]

            act.wait_ge(SK["v"].sem, SK["v"].at("vm"))
            for t in range(4):
                act.wait_ge(tile_done, done("b", t))
                nc.scalar.activation(f2["q"][:, t, :], ps[:, t, 0:256], ACT.Copy)\
                    .then_inc(SQ.sem, SQ.step(f"q{t}"))
                round_weights(act, "b", t + 2)

            def body(i):
                for j in range(4):
                    act.wait_ge(V.sem, V.at(f"sn{j}", i))
                    if ran(i if j else i - 1):
                        act.wait_ge(T.sem, T.at(f"wt{j - 1}" if j else "wt3", i if j else i - 1))
                    for k in range(4):
                        o, s = ((f2["p0"][:, k, :], ps[:, 4, 144 * k:144 * k + 144]) if k < 2 else
                                (f2["p1"][:, k - 2, :], ps[:, 3 + k, 0:NT]))
                        nc.scalar.activation(o, s, ACT.Exp, bias=stb[:, B_NB + k:B_NB + k + 1], scale=SCALE_B,
                                                    accum_out=stb[:, B_RS + k:B_RS + k + 1])\
                            .then_inc(A.sem, A.step(f"e{j}_{k}"))
                    nc.scalar.activation(stb[:, B_SN:B_SN + 4], stb[:, B_SN:B_SN + 4], ACT.Exp)\
                        .then_inc(A.sem, A.step(f"es{j}"))
                    if final(i):
                        act.wait_ge(tile_done, done("b", 4 + 8 * i + j))
                    else:
                        act.wait_ge(tile_done, done("b", 4 + 2 * j, i, 8))
                    if ran(i - 1):
                        act.wait_ge(V.sem, V.at(f"o{j}", i - 1))
                    nc.scalar.activation(f2["gb"][:, j, :], ps[:, j % 2, 0:256], ACT.Silu)\
                        .then_inc(A.sem, A.step(f"g{j}"))
                    if final(i):
                        round_weights(act, "b", 6 + 8 * i + j)
                    else:
                        round_weights(act, "b", 6 + 2 * j, i, 8)
                    act.wait_ge(T.sem, T.at(f"wt{j}", i))
                    nc.scalar.activation(f2["wk0"], ps[:, 7, :], ACT.Copy)\
                        .then_inc(A.sem, A.step(f"wk{j}"))
                    if not final(i):
                        act.wait_ge(tile_done, done("b", 5 + 2 * j, i, 8))
                        nc.scalar.activation(f2["q"][:, j, :], ps[:, 2 + j % 2, 0:256], ACT.Copy)\
                            .then_inc(SQ.sem, SQ.step(f"q{j}"))
                        round_weights(act, "b", 7 + 2 * j, i, 8)
            runs(act, GROUPS_B, body)

        def attn_b_dve(dve):
            A, T, V = SB["a"], SB["t"], SB["v"]
            stb, p0, p1 = f2["stb"], f2["p0"], f2["p1"]
            swap = [r ^ 8 if r < 16 else r for r in range(32)]
            cos = c("cos_b")[:, 0:256].unsqueeze(1).to_broadcast([128, 4, 256])
            sin = c("sin_b")[:, 0:256].unsqueeze(1).to_broadcast([128, 4, 256])
            dve.wait_ge(SK["v"].sem, SK["v"].at("vm"))

            def body(i):
                if ran(i - 1):
                    dve.wait_ge(T.sem, T.at("pv3", i - 1))
                nc.vector.tensor_copy(f2["kg"].unsqueeze(1), f2["kd"][:, bass.ds(i, 1), :])\
                    .then_inc(V.sem, V.step("kg"))
                nc.vector.tensor_copy(f2["vg"][:, 0:2, :], f2["vB"][:, 0:2, bass.ds(64 * i, 64)])\
                    .then_inc(V.sem, V.step("vg"))
                nc.vector.tensor_copy(f2["vg"][0:META, 2:3, :], f2["vB"][0:META, 2:3, bass.ds(64 * i, 64)])\
                    .then_inc(V.sem, V.step("vgm"))
                nc.vector.tensor_copy(f2["sk"], P[:, bass.ds(8 * i + P_AT["sinks"][0], 8)])\
                    .then_inc(V.sem, V.step("sk"))
                dve.wait_ge(SQ.sem, SQ.at("q3", i))
                nc.vector.tensor_tensor(f2["xc"], f2["q"], cos, ALU.mult)\
                    .then_inc(V.sem, V.step("rcos"))
                nc.vector.stream_shuffle(f2["sh"], f2["q"], swap)\
                    .then_inc(V.sem, V.step("shuf"))
                dve.wait_ge(V.sem, V.at("shuf", i))
                nc.vector.tensor_tensor(f2["sh"], f2["sh"], sin, ALU.mult)\
                    .then_inc(V.sem, V.step("rsin"))
                dve.wait_ge(V.sem, V.at("rsin", i))
                nc.vector.tensor_tensor(f2["q"], f2["xc"], f2["sh"], ALU.add)\
                    .then_inc(V.sem, V.step("radd"))
                for j in range(4):
                    sink = f2["sk"][:, 2 * j:2 * j + 2].unsqueeze(1).to_broadcast([128, 2, 2])

                    def s4(k):
                        return stb[:, k:k + 4].rearrange("p (a b) -> p a b", a=2)
                    dve.wait_ge(T.sem, T.at(f"sc{j}", i))
                    nc.vector.tensor_reduce(stb[:, 0:2], ps[:, 4, 0:288].rearrange("p (a b) -> p a b", a=2),
                                                   AX.X, ALU.max)\
                        .then_inc(V.sem, V.step(f"ma{j}"))
                    nc.vector.tensor_reduce(stb[:, 2:4], ps[:, 5:7, 0:NT], AX.X, ALU.max)\
                        .then_inc(V.sem, V.step(f"mb{j}"))
                    dve.wait_ge(V.sem, V.at(f"mb{j}", i))
                    nc.vector.scalar_tensor_tensor(out=s4(B_SM), in0=s4(B_MX), scalar=SCALE_B, in1=sink,
                                                          op0=ALU.mult, op1=ALU.max)\
                        .then_inc(V.sem, V.step(f"sm{j}"))
                    dve.wait_ge(V.sem, V.at(f"sm{j}", i))
                    nc.vector.tensor_scalar(stb[:, B_NB:B_NB + 4], stb[:, B_SM:B_SM + 4], -1.0, None,
                                                   ALU.mult)\
                        .then_inc(V.sem, V.step(f"nb{j}"))
                    nc.vector.tensor_tensor(s4(B_SN), sink, s4(B_SM), ALU.subtract)\
                        .then_inc(V.sem, V.step(f"sn{j}"))
                    dve.wait_ge(A.sem, A.at(f"es{j}", i))
                    nc.vector.tensor_tensor(stb[:, B_RR:B_RR + 4], stb[:, B_RS:B_RS + 4],
                                                   stb[:, B_SN:B_SN + 4], ALU.add)\
                        .then_inc(V.sem, V.step(f"den{j}"))
                    dve.wait_ge(V.sem, V.at(f"den{j}", i))
                    nc.vector.reciprocal(stb[:, B_RR:B_RR + 4], stb[:, B_RR:B_RR + 4])\
                        .then_inc(V.sem, V.step(f"rr{j}"))
                    dve.wait_ge(V.sem, V.at(f"rr{j}", i))
                    for k in range(4):
                        w_ = p0[:, k, :] if k < 2 else p1[:, k - 2, :]
                        nc.vector.tensor_scalar(w_, w_, stb[:, B_RR + k:B_RR + k + 1], None, ALU.mult)\
                            .then_inc(V.sem, V.step(f"p{j}_{k}"))
                    dve.wait_ge(T.sem, T.at(f"wt{j}", i))
                    nc.vector.tensor_copy(f2["wk1"], ps[:, 4, 0:256])\
                        .then_inc(V.sem, V.step(f"w1{j}"))
                    nc.vector.tensor_copy(f2["wkm"][0:META, :], ps[0:META, 5, :])\
                        .then_inc(V.sem, V.step(f"wm{j}"))
                    dve.wait_ge(T.sem, T.at(f"pv{j}", i))
                    dve.wait_ge(A.sem, A.at(f"g{j}", i))
                    nc.vector.tensor_tensor(og[:, bass.ds(4 * i + j, 1), 0:256], ps[:, 6:7, 0:256],
                                                   f2["gb"][:, j:j + 1, :], ALU.mult)\
                        .then_inc(V.sem, V.step(f"o{j}"))
            runs(dve, GROUPS_B, body)

        split_bo = Split("split_bo", og, (hh, hl), SEQ)
        b_out = Product("b_out", "b_out", (hh, hl), SEQ, xT, add=True, split=split_bo)
        norm_fin = Norm("norm_fin", xT, SEQ, 0, [("fin", xT, None)], written=b_out.written(), after="rw")
        split_mix = Split("split_mix", og, (hh, hl), SEQ)
        norm_mix = Norm("norm_mix", xT, SEQ, 1, [("mix_pre", og, split_mix)],
                        written=(norm_fin.V, [norm_fin.V.at(f"o0_{4 * k + 3}") for k in range(4)]))

        SR = phase("rw_in", a="r k v")
        SS = phase("rw_small", a="wa g0 g1 tanh sig0 sig1 f", v=" ".join(
            f"d{k} n{k} m{k}" for k in range(3)) + " zeroa zerob zeroc zerov", t="lora")
        fr = carve([("z", 24, 256), ("aq", 4, 256), ("bx", 4, 128),
                    ("cx", 4, 128), ("vx", 4, 128), ("LT", 4, 128), ("BQ", 4, 128), ("CA", 4, 128),
                    ("CQ", 4, 128), ("X", 4, 128), ("Y", 4, 128), ("bT", 4, 128), ("cT", 4, 128),
                    ("vT", 4, 128), ("lw", 3, 128), ("pj", 10), ("S", 128), ("RU", 256),
                    ("g", 256), ("bon", 256)])
        fr["R"], fr["U"] = fr["RU"][:, 0:128], fr["RU"][:, 128:256]
        ga = arena[:, ARENA - KT * SEQ:ARENA].rearrange("p (a b) -> p a b", a=KT)
        if 24 * 256 + 1024 + 12 * 512 + 384 + 10 + 896 > ARENA - KT * SEQ:
            raise ValueError("the gates overlap the recurrence's storage")
        tmp = {n: og[:, k, 0:256] for k, n in enumerate("r k v kk a ec enc t1".split())}
        tmp["g"] = fr["g"]
        raw_rkv = {"r": tmp["kk"], "k": tmp["a"], "v": fr["RU"]}
        zs = C[:, C_AT["cos_a"][0]:C_AT["cos_a"][0] + 1024].rearrange("p (a b) -> p a b", a=4)

        def rw_in_pe(pe):
            for t in range(3):
                tile(pe, "rw", t, 0, 0, [(ps[:, t, :], hh, hl, ALL)], SEQ,
                     ready=first(0, t, split_mix)).then_inc(tile_done, 1)
            for t, m in enumerate((128, SB_HEADS, 128, 32)):
                tile(pe, "small", t, 0, 0, [(ps[:, 3 + t, :], hh, hl, ALL)], SEQ, m=m).then_inc(tile_done, 1)

        def rw_in_act(act):
            A = SS["a"]
            act.wait_ge(norm_mix.V.sem, norm_mix.V.at(norm_mix.last))
            act.dma_start(fr["lw"].rearrange("p a b -> p (a b)").unsqueeze(1), lora[:, 0:1, :]).then_inc(lora_in, 16)
            for t, n in enumerate("rkv"):
                act.wait_ge(tile_done, done("rw", t))
                nc.scalar.activation(raw_rkv[n], ps[:, t, 0:256], ACT.Copy)\
                    .then_inc(SR["a"].sem, SR["a"].step(n))
                round_weights(act, "rw", t + 2)
            act.wait_ge(tile_done, done("small", 0))
            nc.scalar.activation(zs[:, 0, :], ps[:, 3, 0:256], ACT.Copy)\
                .then_inc(A.sem, A.step("wa"))
            round_weights(act, "small", 2)
            round_weights(act, "small", 3)
            act.wait_ge(tile_done, done("small", 3))
            nc.scalar.activation(zs[:, 1, :], ps[:, 5, 0:256], ACT.Copy)\
                .then_inc(A.sem, A.step("g0"))
            nc.scalar.activation(zs[0:32, 2, :], ps[0:32, 6, 0:256], ACT.Copy)\
                .then_inc(A.sem, A.step("g1"))
            act.wait_ge(SS["v"].sem, SS["v"].at("m0"))
            nc.scalar.activation(zs[0:64, 0, :], zs[0:64, 0, :], ACT.Tanh)\
                .then_inc(A.sem, A.step("tanh"))
            act.wait_ge(SS["v"].sem, SS["v"].at("m2"))
            nc.scalar.activation(zs[:, 1, :], zs[:, 1, :], ACT.Sigmoid)\
                .then_inc(A.sem, A.step("sig0"))
            nc.scalar.activation(zs[0:32, 2, :], zs[0:32, 2, :], ACT.Sigmoid)\
                .then_inc(A.sem, A.step("sig1"))
            nc.scalar.activation(zs[0:SB_HEADS, 3, :], ps[0:SB_HEADS, 4, 0:256], ACT.Copy)\
                .then_inc(A.sem, A.step("f"))
            round_weights(act, "fill", 0)
            round_weights(act, "fill", 1)

        def rw_in_dve(dve):
            V = SS["v"]
            tmp = og[:, 0, 0:256]
            dve.wait_ge(split_mix.V.sem, split_mix.V.at("l3"))
            for k, (name, j, rows, ready) in enumerate((("mu_wa", 0, 128, "wa"), ("mu_g", 0, 128, "g0"),
                                                        ("mu_g", 1, 32, "g1"))):
                z = zs[0:rows, k, :]
                dve.wait_ge(SS["a"].sem, SS["a"].at(ready))
                if k:
                    dve.wait_ge(V.sem, V.at(f"m{k - 1}"))
                nc.vector.tensor_tensor(tmp[0:rows, 1:256], z[:, 0:255], z[:, 1:256], ALU.subtract)\
                    .then_inc(V.sem, V.step(f"d{k}"))
                nc.vector.tensor_scalar(tmp[0:rows, 0:1], z[:, 0:1], -1.0, None, ALU.mult)\
                    .then_inc(V.sem, V.step(f"n{k}"))
                dve.wait_ge(V.sem, V.at(f"n{k}"))
                nc.vector.scalar_tensor_tensor(out=z, in0=tmp[0:rows, :], scalar=p(name, j, rows), in1=z,
                                                      op0=ALU.mult, op1=ALU.add)\
                    .then_inc(V.sem, V.step(f"m{k}"))
            nc.vector.memset(fr["aq"], 0.0)\
                .then_inc(V.sem, V.step("zeroa"))
            nc.vector.memset(fr["bx"], 0.0)\
                .then_inc(V.sem, V.step("zerob"))
            nc.vector.memset(fr["cx"], 0.0)\
                .then_inc(V.sem, V.step("zeroc"))
            nc.vector.memset(fr["vx"], 0.0)\
                .then_inc(V.sem, V.step("zerov"))

        NCH = SEQ // CHUNK
        lv = LEVELS[1:]
        SW = phase("rwkv",
                   a="w a g sqk nrm ea enc ec bT cT vT " + " ".join(f"t1_{b}" for b in lv)
                     + " " + " ".join(f"U{n}" for n in range(NCH)) + " sqy root",
                   t="lora kk bon grams tr " + " ".join(f"T{b} dY{b}" for b in lv)
                     + " " + " ".join(f"R{n} U{n} y{n}" for n in range(NCH)) + " mean var",
                   v="pj " + " ".join(f"d{z} n{z} m{z}" for z in "rkv") + " kk max rec kkn am1 k2 rk rkk bonus ld "
                     "cum cb a0 a1 q0 q1 ka b0 b1 c0 c1 v0 v1 LT BQ CA CQ x0 x1 y0 y1 "
                     "M2 M4 X2 Y2 M8 X4 Y4 M16 X8 Y8 M32 X16 Y16 Y32 "
                     + " ".join(f"R{n} S{n} P{n}" if 0 < n < NCH - 1 else (f"R{n} P{n}" if n == 0 else f"R{n}")
                                for n in range(NCH))
                     + " ys0 ys1 yc gvar grec gn gl gb gy")
        Xv = {"M": (fr["bx"], fr["cx"])}

        SF = phase("fill", a=" ".join(f"f{t}" for t in range(8)))

        def fills(i):
            return 5 if isinstance(i, int) and i == RW_TILES - 1 else 8

        def fill(pe, i, parts):
            for part in parts:
                t, k = part // 6, part % 6
                if t >= fills(i):
                    return
                q = FIRST["fill"] + t
                acc = ps[:, 6 + t % 2, 0:SEQ]
                if k == 0:
                    pe.wait_ge(hi_done, q + 1 + 8 * i)
                    if ran(i if t >= 2 else i - 1):
                        pe.wait_ge(SF["a"].sem, SF["a"].at(f"f{(t - 2) % 8}", i if t >= 2 else i - 1))
                if k < 4:
                    for kt in range(4 * k, 4 * k + 4):
                        mm(acc, wh[:, q % 2, kt, :], hh[:, kt, 0:SEQ], start=(kt == 0), stop=False)
                        mm(acc, wh[:, q % 2, kt, :], hl[:, kt, 0:SEQ], start=False, stop=False)
                else:
                    pe.wait_ge(lo_done, 2 * q + k - 3 + 16 * i)
                    for kt in range(8 * (k - 4), 8 * (k - 4) + 8):
                        ins = mm(acc, wl[:, q % 2, kt, :], hh[:, kt, 0:SEQ], start=False, stop=(kt == 15))
                    if k == 5:
                        ins.then_inc(tile_done, 1)

        def take(act, i, t):
            if t >= fills(i):
                return
            acc = ps[:, 6 + t % 2, 0:SEQ]
            if t < 5:
                round_weights(act, "fill", t + 2, i, 8)
                dst = fr["z"][:, bass.ds(i + 8 * t, 1), :] if t < 3 else ga[:, bass.ds(2 * i + t - 3, 1), :]
                nc.scalar.activation(dst, acc.unsqueeze(1), ACT.Copy)\
                    .then_inc(SF["a"].sem, SF["a"].step(f"f{t}"))
            else:
                act.wait_ge(tile_done, done("fill", t, i, 8))
                if t == 5:
                    act.wait_ge(SW["v"].sem, SW["v"].at("b1", i))
                if t == 7:
                    act.wait_ge(SW["t"].sem, SW["t"].at(f"y{NCH - 1}", i))
                nc.scalar.activation(raw_rkv["rkv"[t - 5]], acc, ACT.Copy)\
                    .then_inc(SF["a"].sem, SF["a"].step(f"f{t}"))
                round_weights(act, "fill", t + 2, i, 8)

        def rwkv_pe(pe):
            A, T, V = SW["a"], SW["t"], SW["v"]
            aq, bx, cx, vx, S = fr["aq"], fr["bx"], fr["cx"], fr["vx"], fr["S"]
            pe.wait_ge(SS["a"].sem, SS["a"].at("f"))

            def body(i):
                fill(pe, i, range(0, 5))
                pe.wait_ge(lora_in, 16 * i + 16)
                if ran(i - 1):
                    pe.wait_ge(V.sem, V.at("grec", i - 1))
                lw = fr["lw"]
                mm(ps[:, 0, 0:256], lw[0:64, 0, :], zs[0:64, 0, :])
                mm(ps[:, 1, 0:256], lw[64:128, 0, :], zs[64:128, 0, :])
                mm(ps[:, 2, 0:256], lw[:, 1, :], zs[:, 1, :], stop=False)
                mm(ps[:, 2, 0:256], lw[0:32, 2, :], zs[0:32, 2, :], start=False)\
                    .then_inc(T.sem, T.step("lora"))
                fill(pe, i, range(5, 7))
                pe.wait_ge(A.sem, A.at("sqk", i))
                mm(ps[:, 3, 0:256], c("hones"), tmp["t1"])\
                    .then_inc(T.sem, T.step("kk"))
                fill(pe, i, range(7, 12))
                pe.wait_ge(V.sem, V.at("rkk", i))
                mm(ps[:, 4, 0:256], c("hones"), tmp["enc"])\
                    .then_inc(T.sem, T.step("bon"))
                fill(pe, i, range(12, 19))
                pe.wait_ge(V.sem, V.at("v1", i))
                for n in range(NCH):
                    mm(ps[:, n, 0:256], bx[:, n, :], aq[:, n, :])
                    mm(ps[:, n, 256:512], cx[:, n, :], aq[:, n, :])
                for n in range(NCH):
                    ins = mm(ps[:, 4, 128 * n:128 * n + 128], aq[:, n, 0:128], bx[:, n, :])
                ins\
                    .then_inc(T.sem, T.step("grams"))
                if ran(i - 1):
                    pe.wait_ge(V.sem, V.at("ys1", i - 1))
                for n in range(NCH):
                    nc.tensor.transpose(ps[:, 5, 128 * n:128 * n + 128], bx[:, n, :], c("ident"))
                fill(pe, i, range(19, 21))
                pe.wait_ge(V.sem, V.at("CQ", i))
                for bank, src in ((0, cx), (1, vx)):
                    for n in range(NCH):
                        ins = nc.tensor.transpose(ps[:, bank, 128 * n:128 * n + 128], src[:, n, :], c("ident"))
                ins\
                    .then_inc(T.sem, T.step("tr"))
                fill(pe, i, range(21, 24))
                X, Y, T1 = fr["X"], fr["Y"], fr["vx"]
                for k, b in enumerate(lv):
                    pe.wait_ge(V.sem, V.at(f"M{b}", i))
                    pe.wait_ge(V.sem, V.at(f"X{lv[k - 1]}" if k else "y1", i))
                    for n in range(NCH):
                        ins = mm(ps[:, 2, 128 * n:128 * n + 128], Xv["M"][k % 2][:, n, :], X[:, n, :])
                    ins\
                        .then_inc(T.sem, T.step(f"T{b}"))
                    fill(pe, i, range(24 + 2 * k, 25 + 2 * k))
                    pe.wait_ge(A.sem, A.at(f"t1_{b}", i))
                    if k:
                        pe.wait_ge(V.sem, V.at(f"Y{lv[k - 1]}", i))
                    for n in range(NCH):
                        if b != lv[-1]:
                            mm(ps[:, 3, 128 * n:128 * n + 128], Y[:, n, :], T1[:, n, :])
                        ins = mm(ps[:, 4, 128 * n:128 * n + 128], T1[:, n, :], Y[:, n, :])
                    ins\
                        .then_inc(T.sem, T.step(f"dY{b}"))
                    fill(pe, i, range(25 + 2 * k, 26 + 2 * k))
                pe.wait_ge(V.sem, V.at(f"Y{lv[-1]}", i))
                for n in range(NCH):
                    if n:
                        pe.wait_ge(V.sem, V.at(f"P{n - 1}", i))
                        mm(ps[:, 3, 0:128], aq[:, n, 0:128], S, stop=False)
                    mm(ps[:, 3, 0:128], fr["CA"][:, n, :], fr["vT"][:, n, :], start=(n == 0))\
                        .then_inc(T.sem, T.step(f"R{n}"))
                    fill(pe, i, range(34 + 3 * n, 35 + 3 * n))
                    pe.wait_ge(V.sem, V.at(f"R{n}", i))
                    mm(ps[:, 4, 0:128], Y[:, n, :], fr["R"])\
                        .then_inc(T.sem, T.step(f"U{n}"))
                    fill(pe, i, range(35 + 3 * n, 36 + 3 * n))
                    pe.wait_ge(A.sem, A.at(f"U{n}", i))
                    y = ps[:, 5, 128 * n:128 * n + 128]
                    if n:
                        mm(y, S, aq[:, n, 128:256], stop=False)
                    mm(y, fr["U"], fr["BQ"][:, n, :], start=(n == 0), stop=False)
                    ins = mm(y, fr["vT"][:, n, :], fr["CQ"][:, n, :], start=False)
                    if n < NCH - 1:
                        mm(ps[:, 2, 0:128], fr["cT"][:, n, :], fr["vT"][:, n, :], stop=False)
                        ins = mm(ps[:, 2, 0:128], fr["bT"][:, n, :], fr["U"], start=False)
                    ins\
                        .then_inc(T.sem, T.step(f"y{n}"))
                    if n < NCH - 1:
                        fill(pe, i, range(36 + 3 * n, 37 + 3 * n))
                pe.wait_ge(V.sem, V.at("ys1", i))
                mm(ps[:, 0, 0:256], c("hones"), tmp["t1"])\
                    .then_inc(T.sem, T.step("mean"))
                fill(pe, i, range(45, 46))
                pe.wait_ge(A.sem, A.at("sqy", i))
                mm(ps[:, 1, 0:256], c("hones"), tmp["enc"])\
                    .then_inc(T.sem, T.step("var"))
                fill(pe, i, range(46, 48))
            runs(pe, RW_TILES, body)

        def rwkv_act(act):
            A, T, V = SW["a"], SW["t"], SW["v"]
            pj = fr["pj"]
            flat = "p a b -> p (a b)"

            def body(i):
                act.wait_ge(T.sem, T.at("lora", i))
                act.wait_ge(V.sem, V.at("mv", i))
                if ran(i - 1):
                    act.wait_ge(V.sem, V.at("gy", i - 1))
                nc.scalar.activation(tmp["ec"], ps[:, 0, 0:256], ACT.Sigmoid, bias=pj[:, W0:W0 + 1])\
                    .then_inc(A.sem, A.step("w"))
                nc.scalar.activation(tmp["a"], ps[:, 1, 0:256], ACT.Sigmoid, bias=pj[:, A0:A0 + 1])\
                    .then_inc(A.sem, A.step("a"))
                nc.scalar.activation(tmp["g"], ps[:, 2, 0:256], ACT.Copy)\
                    .then_inc(A.sem, A.step("g"))
                if not isinstance(i, int) or i < RW_TILES - 1:
                    act.dma_start(fr["lw"].rearrange("p a b -> p (a b)").unsqueeze(1),
                                  lora[:, bass.ds(i + 1, 1), :]).then_inc(lora_in, 16)
                act.wait_ge(V.sem, V.at("kk", i))
                nc.scalar.activation(tmp["t1"], tmp["kk"], ACT.Square)\
                    .then_inc(A.sem, A.step("sqk"))
                take(act, i, 0)
                act.wait_ge(T.sem, T.at("kk", i))
                nc.scalar.activation(tmp["t1"], ps[:, 3, 0:256], ACT.Sqrt)\
                    .then_inc(A.sem, A.step("nrm"))
                take(act, i, 1)
                act.wait_ge(V.sem, V.at("cb", i))
                nc.scalar.activation(tmp["t1"], tmp["t1"], ACT.Exp)\
                    .then_inc(A.sem, A.step("ea"))
                nc.scalar.activation(tmp["enc"], tmp["ec"], ACT.Exp, scale=-1.0)\
                    .then_inc(A.sem, A.step("enc"))
                act.wait_ge(A.sem, A.at("enc", i))
                nc.scalar.activation(tmp["ec"], tmp["ec"], ACT.Exp)\
                    .then_inc(A.sem, A.step("ec"))
                take(act, i, 2)
                act.wait_ge(T.sem, T.at("tr", i))
                nc.scalar.activation(fr["bT"].rearrange(flat), ps[:, 5, :], ACT.Copy, scale=-1.0)\
                    .then_inc(A.sem, A.step("bT"))
                nc.scalar.activation(fr["cT"].rearrange(flat), ps[:, 0, :], ACT.Copy)\
                    .then_inc(A.sem, A.step("cT"))
                nc.scalar.activation(fr["vT"].rearrange(flat), ps[:, 1, :], ACT.Copy)\
                    .then_inc(A.sem, A.step("vT"))
                take(act, i, 3)
                for b in lv:
                    act.wait_ge(T.sem, T.at(f"T{b}", i))
                    nc.scalar.activation(fr["vx"].rearrange(flat), ps[:, 2, :], ACT.Copy)\
                        .then_inc(A.sem, A.step(f"t1_{b}"))
                    if b == lv[3]:
                        take(act, i, 4)
                for n in range(NCH):
                    act.wait_ge(T.sem, T.at(f"U{n}", i))
                    nc.scalar.activation(fr["U"], ps[:, 4, 0:128], ACT.Copy)\
                        .then_inc(A.sem, A.step(f"U{n}"))
                    if n == 0:
                        take(act, i, 5)
                    if n == 2:
                        take(act, i, 6)
                act.wait_ge(V.sem, V.at("yc", i))
                nc.scalar.activation(tmp["enc"], tmp["ec"], ACT.Square)\
                    .then_inc(A.sem, A.step("sqy"))
                act.wait_ge(V.sem, V.at("gvar", i))
                nc.scalar.activation(tmp["t1"], tmp["t1"], ACT.Sqrt)\
                    .then_inc(A.sem, A.step("root"))
                take(act, i, 7)
            runs(act, RW_TILES, body)

        def rwkv_dve(dve):
            A, T, V = SW["a"], SW["t"], SW["v"]
            pj = fr["pj"]
            aq, bx, cx, vx = fr["aq"], fr["bx"], fr["cx"], fr["vx"]
            flat = "p a b -> p (a b)"
            r, k, v, kk, a, ec, enc, t1 = (tmp[n] for n in "r k v kk a ec enc t1".split())

            def col(k_):
                return pj[:, k_:k_ + 1]

            def mask(name):
                return c(name).unsqueeze(1).to_broadcast([128, NCH, 128])

            def spread(o, off, x, y, names, op=ALU.mult):
                for h in range(2):
                    r_ = slice(64 * h, 64 * h + 64)
                    dst = o[r_, :, off + 64 * h:off + 64 * h + 64]
                    xv = x[r_].rearrange("p (a b) -> p a b", a=NCH)
                    if y is None:
                        nc.vector.tensor_copy(dst, xv)\
                            .then_inc(V.sem, V.step(names[h]))
                    else:
                        nc.vector.tensor_tensor(dst, xv, y[r_].rearrange("p (a b) -> p a b", a=NCH), op)\
                            .then_inc(V.sem, V.step(names[h]))

            def body(i):
                if ran(i - 1):
                    dve.wait_ge(V.sem, V.at("gy", i - 1))
                nc.vector.tensor_copy(pj, P[:, bass.ds(10 * i + P_AT["rw"][0], 10)])\
                    .then_inc(V.sem, V.step("pj"))
                dve.wait_ge(V.sem, V.at("pj", i))
                if ran(i - 1):
                    dve.wait_ge(SF["a"].sem, SF["a"].at("f7", i - 1))
                else:
                    dve.wait_ge(SR["a"].sem, SR["a"].at("v"))
                for q, (z, o) in enumerate(zip("rkv", (r, k, v))):
                    src = raw_rkv[z]
                    nc.vector.tensor_tensor(o[:, 1:256], src[:, 0:255], src[:, 1:256], ALU.subtract)\
                        .then_inc(V.sem, V.step(f"d{z}"))
                    nc.vector.tensor_scalar(o[:, 0:1], src[:, 0:1], -1.0, None, ALU.mult)\
                        .then_inc(V.sem, V.step(f"n{z}"))
                    dve.wait_ge(V.sem, V.at(f"n{z}", i))
                    nc.vector.scalar_tensor_tensor(out=o, in0=o, scalar=col(MU_R + q), in1=src,
                                                   op0=ALU.mult, op1=ALU.add)\
                        .then_inc(V.sem, V.step(f"m{z}"))
                dve.wait_ge(V.sem, V.at("mv", i))
                nc.vector.tensor_scalar(kk, k, col(K_K), None, ALU.mult)\
                    .then_inc(V.sem, V.step("kk"))
                dve.wait_ge(A.sem, A.at("nrm", i))
                nc.vector.tensor_scalar(t1, t1, 1e-12, None, ALU.max)\
                    .then_inc(V.sem, V.step("max"))
                dve.wait_ge(V.sem, V.at("max", i))
                nc.vector.reciprocal(t1, t1)\
                    .then_inc(V.sem, V.step("rec"))
                dve.wait_ge(V.sem, V.at("rec", i))
                nc.vector.tensor_tensor(kk, kk, t1, ALU.mult)\
                    .then_inc(V.sem, V.step("kkn"))
                dve.wait_ge(V.sem, V.at("kkn", i))
                nc.vector.tensor_scalar(t1, a, -1.0, col(K_A), ALU.add, ALU.mult)\
                    .then_inc(V.sem, V.step("am1"))
                dve.wait_ge(V.sem, V.at("am1", i))
                nc.vector.scalar_tensor_tensor(out=k, in0=t1, scalar=1.0, in1=k,
                                               op0=ALU.add, op1=ALU.mult)\
                    .then_inc(V.sem, V.step("k2"))
                dve.wait_ge(V.sem, V.at("k2", i))
                nc.vector.tensor_scalar(enc, r, col(R_K), None, ALU.mult)\
                    .then_inc(V.sem, V.step("rk"))
                dve.wait_ge(V.sem, V.at("rk", i))
                nc.vector.tensor_tensor(enc, enc, k, ALU.mult)\
                    .then_inc(V.sem, V.step("rkk"))
                dve.wait_ge(T.sem, T.at("bon", i))
                nc.vector.tensor_tensor(fr["bon"], ps[:, 4, 0:256], v, ALU.mult)\
                    .then_inc(V.sem, V.step("bonus"))
                nc.vector.tensor_scalar(t1, ec, -DECAY, None, ALU.mult)\
                    .then_inc(V.sem, V.step("ld"))
                dve.wait_ge(V.sem, V.at("ld", i))
                nc.vector.tensor_tensor_scan(ec, c("reset"), t1, 0.0, ALU.mult, ALU.add)\
                    .then_inc(V.sem, V.step("cum"))
                dve.wait_ge(V.sem, V.at("cum", i))
                nc.vector.tensor_tensor(t1, ec, t1, ALU.subtract)\
                    .then_inc(V.sem, V.step("cb"))
                dve.wait_ge(A.sem, A.at("ec", i))
                spread(aq, 0, kk, t1, ("a0", "a1"))
                spread(aq, 128, r, ec, ("q0", "q1"))
                dve.wait_ge(V.sem, V.at("a1", i))
                nc.vector.tensor_tensor(kk, kk, a, ALU.mult)\
                    .then_inc(V.sem, V.step("ka"))
                dve.wait_ge(V.sem, V.at("ka", i))
                spread(bx, 0, kk, enc, ("b0", "b1"))
                spread(cx, 0, k, enc, ("c0", "c1"))
                spread(vx, 0, v, None, ("v0", "v1"))
                dve.wait_ge(T.sem, T.at("grams", i))
                nc.vector.tensor_tensor(fr["LT"], ps[:, 0:4, 0:128], mask("strict"), ALU.mult)\
                    .then_inc(V.sem, V.step("LT"))
                nc.vector.scalar_tensor_tensor(out=fr["BQ"], in0=ps[:, 0:4, 128:256], scalar=-1.0, in1=mask("incl"),
                                               op0=ALU.mult, op1=ALU.mult)\
                    .then_inc(V.sem, V.step("BQ"))
                nc.vector.tensor_tensor(fr["CA"], ps[:, 0:4, 256:384], mask("strict"), ALU.mult)\
                    .then_inc(V.sem, V.step("CA"))
                nc.vector.tensor_tensor(fr["CQ"], ps[:, 0:4, 384:512], mask("incl"), ALU.mult)\
                    .then_inc(V.sem, V.step("CQ"))
                nc.vector.tensor_tensor(fr["X"], ps[:, 4, :].rearrange("p (a b) -> p a b", a=NCH), mask("lev1t"), ALU.mult)\
                    .then_inc(V.sem, V.step("x0"))
                dve.wait_ge(V.sem, V.at("x0", i))
                nc.vector.tensor_tensor(fr["X"], mask("ident"), fr["X"], ALU.subtract)\
                    .then_inc(V.sem, V.step("x1"))
                nc.vector.tensor_tensor(fr["Y"], fr["LT"], mask("lev1"), ALU.mult)\
                    .then_inc(V.sem, V.step("y0"))
                dve.wait_ge(V.sem, V.at("y0", i))
                nc.vector.tensor_tensor(fr["Y"], mask("ident"), fr["Y"], ALU.subtract)\
                    .then_inc(V.sem, V.step("y1"))
                dve.wait_ge(T.sem, T.at("tr", i))
                nc.vector.tensor_tensor(bx, fr["LT"], mask(f"lev{lv[0]}"), ALU.mult)\
                    .then_inc(V.sem, V.step(f"M{lv[0]}"))
                nc.vector.tensor_tensor(cx, fr["LT"], mask(f"lev{lv[1]}"), ALU.mult)\
                    .then_inc(V.sem, V.step(f"M{lv[1]}"))
                for step, b in enumerate(lv):
                    dve.wait_ge(T.sem, T.at(f"dY{b}", i))
                    if b != lv[-1]:
                        nc.vector.tensor_tensor(fr["X"].rearrange(flat), fr["X"].rearrange(flat), ps[:, 3, :], ALU.subtract)\
                            .then_inc(V.sem, V.step(f"X{b}"))
                    nc.vector.tensor_tensor(fr["Y"].rearrange(flat), fr["Y"].rearrange(flat), ps[:, 4, :], ALU.subtract)\
                        .then_inc(V.sem, V.step(f"Y{b}"))
                    if step + 2 < len(lv):
                        nc.vector.tensor_tensor(Xv["M"][step % 2], fr["LT"], mask(f"lev{lv[step + 2]}"), ALU.mult)\
                            .then_inc(V.sem, V.step(f"M{lv[step + 2]}"))
                S = fr["S"]
                for n in range(NCH):
                    dve.wait_ge(T.sem, T.at(f"R{n}", i))
                    nc.vector.tensor_copy(fr["R"], ps[:, 3, 0:128])\
                        .then_inc(V.sem, V.step(f"R{n}"))
                    if n == NCH - 1:
                        break
                    dve.wait_ge(T.sem, T.at(f"y{n}", i))
                    end = ec[:, CHUNK * (n + 1) - 1:CHUNK * (n + 1)]
                    if n == 0:
                        nc.vector.tensor_scalar(S, ps[:, 2, 0:128], end, None, ALU.mult)\
                            .then_inc(V.sem, V.step("P0"))
                    else:
                        nc.vector.tensor_tensor(S, S, ps[:, 2, 0:128], ALU.add)\
                            .then_inc(V.sem, V.step(f"S{n}"))
                        dve.wait_ge(V.sem, V.at(f"S{n}", i))
                        nc.vector.tensor_scalar(S, S, end, None, ALU.mult)\
                            .then_inc(V.sem, V.step(f"P{n}"))
                dve.wait_ge(T.sem, T.at(f"y{NCH - 1}", i))
                y = ps[:, 5, :].rearrange("p (a b) -> p a b", a=NCH)
                for h in range(2):
                    r_ = slice(64 * h, 64 * h + 64)
                    nc.vector.tensor_copy(t1[r_].rearrange("p (a b) -> p a b", a=NCH), y[r_, :, r_])\
                        .then_inc(V.sem, V.step(f"ys{h}"))
                dve.wait_ge(T.sem, T.at("mean", i))
                nc.vector.scalar_tensor_tensor(out=ec, in0=ps[:, 0, 0:256], scalar=-1.0 / 64, in1=t1,
                                               op0=ALU.mult, op1=ALU.add)\
                    .then_inc(V.sem, V.step("yc"))
                dve.wait_ge(T.sem, T.at("var", i))
                nc.vector.tensor_scalar(t1, ps[:, 1, 0:256], 1.0 / 64, eps[:, 2:3], ALU.mult, ALU.add)\
                    .then_inc(V.sem, V.step("gvar"))
                dve.wait_ge(A.sem, A.at("root", i))
                nc.vector.reciprocal(t1, t1)\
                    .then_inc(V.sem, V.step("grec"))
                dve.wait_ge(V.sem, V.at("grec", i))
                nc.vector.tensor_tensor(ec, ec, t1, ALU.mult)\
                    .then_inc(V.sem, V.step("gn"))
                dve.wait_ge(V.sem, V.at("gn", i))
                nc.vector.tensor_scalar(ec, ec, col(LN_W), col(LN_B), ALU.mult, ALU.add)\
                    .then_inc(V.sem, V.step("gl"))
                dve.wait_ge(V.sem, V.at("gl", i))
                nc.vector.tensor_tensor(ec, ec, fr["bon"], ALU.add)\
                    .then_inc(V.sem, V.step("gb"))
                dve.wait_ge(V.sem, V.at("gb", i))
                nc.vector.tensor_tensor(og[:, bass.ds(8 + i, 1), 0:256], ec.unsqueeze(1), fr["g"].unsqueeze(1), ALU.mult)\
                    .then_inc(V.sem, V.step("gy"))
            runs(dve, RW_TILES, body)

        fz = carve([("z", 24, 256), ("vv", 8, 256), ("p", 4, 384), ("q", 4, 384), ("u", 4, 384),
                    ("fs", 4, 256)])

        H4 = range(4)
        ST = phase("attn_z",
                   a="va vb abs exp ln relu ew ya fabs fexp fln frelu " + " ".join(f"x{k}" for k in range(8)),
                   t="v0 v1 z logw ya f wt yb",
                   v="sq_a sq_b l m0 m1 fb fl cum ncum mx0 mx1 nb rr " + " ".join(f"n{k}" for k in range(8)) + " wt yb")
        z, u = fz["z"], fz["u"]
        zq_a, zk_a, zv_a, zq_b, zk_b, zv_b = (z[:, 4 * k:4 * k + 4, :] for k in range(6))
        fsm = zs[0:SB_HEADS, 3, :]
        F_MX, F_NB, F_RS, F_RR = 32, 40, 48, 56

        def attn_z_pe(pe):
            A, T, V = ST["a"], ST["t"], ST["v"]
            pe.wait_ge(SF["a"].sem, SF["a"].at("f4", RW_TILES - 1))
            pe.wait_ge(SW["v"].sem, SW["v"].at("gy", RW_TILES - 1))
            for k, zv in enumerate((zv_a, zv_b)):
                for h in H4:
                    for tok in range(2):
                        bank, at = 4 * k + h // 2, 256 * (h % 2) + 128 * tok
                        ins = nc.tensor.transpose(ps[:, bank, at:at + 128], zv[:, h, 128 * tok:128 * tok + 128],
                                                  c("ident"))
                ins\
                    .then_inc(T.sem, T.step(f"v{k}"))
            pe.wait_ge(V.sem, V.at("sq_b"))
            pe.wait_ge(A.sem, A.at("va"))
            for h in H4:
                mm(ps[:, h, 0:256], zk_a[:, h, 0:128], zq_a[:, h, :])
                ins = mm(ps[:, h, 256:384], zk_a[:, h, 128:256], zq_a[:, h, 128:256])
            ins\
                .then_inc(T.sem, T.step("z"))
            pe.wait_ge(A.sem, A.at("vb"))
            pe.wait_ge(V.sem, V.at("m1"))
            L = fz["p"]
            for h in H4:
                o = ps[:, 4 + h, :]
                mm(o[:, 0:256], zk_a[:, h, 0:128], zq_a[:, h, :], stop=False)
                mm(o[:, 0:256], c("tri"), L[:, h, 0:256], start=False, stop=False)
                mm(o[:, 128:256], c("ones"), L[:, h, 256:384], start=False, stop=False)
                mm(o[:, 0:128], c("ident"), c("not_after"), start=False)
                mm(o[:, 256:384], zk_a[:, h, 128:256], zq_a[:, h, 128:256], stop=False)
                mm(o[:, 256:384], c("tri"), L[:, h, 256:384], start=False, stop=False)
                ins = mm(o[:, 256:384], c("ident"), c("not_after"), start=False)
            ins\
                .then_inc(T.sem, T.step("logw"))
            pe.wait_ge(A.sem, A.at("ew"))
            W = fz["q"]
            for h in H4:
                o = ps[:, h, 0:256]
                mm(o, fz["vv"][:, h, 0:128], W[:, h, 0:256], stop=False)
                ins = mm(o[:, 128:256], fz["vv"][:, h, 128:256], W[:, h, 256:384], start=False)
            ins\
                .then_inc(T.sem, T.step("ya"))
            pe.wait_ge(V.sem, V.at("ncum"))
            cum, ncum = fz["fs"][0:4, 0, :], fz["fs"][0:4, 1, :]
            for h in H4:
                o = ps[:, 4 + h, :]
                sel = c("sel", 4)[:, 128 * h:128 * h + 128]
                mm(o[:, 0:128], zq_b[:, h, 0:128], zk_b[:, h, 0:128], stop=False)
                mm(o[:, 0:128], sel, ncum[:, 0:128], start=False, stop=False)
                mm(o[:, 0:128], cum[:, 0:128], sel, start=False, stop=False)
                mm(o[:, 0:128], c("ident"), c("future"), start=False)
                mm(o[:, 128:384], zq_b[:, h, 128:256], zk_b[:, h, :], stop=False)
                mm(o[:, 128:384], sel, ncum, start=False, stop=False)
                for k in range(2):
                    mm(o[:, 128 + 128 * k:256 + 128 * k], cum[:, 128:256], sel, start=False, stop=False)
                ins = mm(o[:, 256:384], c("ident"), c("future"), start=False)
            ins\
                .then_inc(T.sem, T.step("f"))
            pe.wait_ge(V.sem, V.at("n7"))
            pe.wait_ge(A.sem, A.at("ya"))
            pr = fz["p"]
            for h in H4:
                nc.tensor.transpose(ps[:, h, 0:128], pr[:, h, 0:128], c("ident"))
                nc.tensor.transpose(ps[:, h, 128:256], pr[:, h, 128:256], c("ident"))
                ins = nc.tensor.transpose(ps[:, h, 256:384], pr[:, h, 256:384], c("ident"))
            ins\
                .then_inc(T.sem, T.step("wt"))
            pe.wait_ge(V.sem, V.at("wt"))
            W = fz["q"]
            for h in H4:
                o = ps[:, 4 + h, 0:256]
                mm(o, fz["vv"][:, 4 + h, 0:128], W[:, h, 0:256], stop=False)
                ins = mm(o[:, 128:256], fz["vv"][:, 4 + h, 128:256], W[:, h, 256:384], start=False)
            ins\
                .then_inc(T.sem, T.step("yb"))

        def attn_z_act(act):
            A, T, V = ST["a"], ST["t"], ST["v"]
            act.wait_ge(T.sem, T.at("v0"))
            vv = fz["vv"]
            nc.scalar.activation(vv[:, 0:4, :], ps[:, 0:2, :].rearrange("p a (b c) -> p (a b) c", b=2),
                                        ACT.Copy)\
                .then_inc(A.sem, A.step("va"))
            act.wait_ge(T.sem, T.at("v1"))
            nc.scalar.activation(vv[:, 4:8, :], ps[:, 4:6, :].rearrange("p a (b c) -> p (a b) c", b=2),
                                        ACT.Copy)\
                .then_inc(A.sem, A.step("vb"))
            zz = ps[:, 0:4, 0:384]
            act.wait_ge(T.sem, T.at("z"))
            nc.scalar.activation(fz["q"], zz, ACT.Abs)\
                .then_inc(A.sem, A.step("abs"))
            act.wait_ge(A.sem, A.at("abs"))
            nc.scalar.activation(fz["q"], fz["q"], ACT.Exp, scale=-1.0)\
                .then_inc(A.sem, A.step("exp"))
            act.wait_ge(A.sem, A.at("exp"))
            nc.scalar.activation(fz["q"], fz["q"], ACT.Ln, bias=eps[:, 3:4])\
                .then_inc(A.sem, A.step("ln"))
            nc.scalar.activation(u, zz, ACT.Relu)\
                .then_inc(A.sem, A.step("relu"))
            act.wait_ge(T.sem, T.at("logw"))
            act.wait_ge(V.sem, V.at("l"))
            nc.scalar.activation(fz["q"], ps[:, 4:8, 0:384], ACT.Exp)\
                .then_inc(A.sem, A.step("ew"))
            act.wait_ge(T.sem, T.at("ya"))
            nc.scalar.activation(og[:, 0:4, 0:256], ps[:, 0:4, 0:256], ACT.Copy)\
                .then_inc(A.sem, A.step("ya"))
            f = fz["fs"]
            act.wait_ge(V.sem, V.at("fb"))
            nc.scalar.activation(f[0:4, 2, :], f[0:4, 0, :], ACT.Abs)\
                .then_inc(A.sem, A.step("fabs"))
            act.wait_ge(A.sem, A.at("fabs"))
            nc.scalar.activation(f[0:4, 2, :], f[0:4, 2, :], ACT.Exp, scale=-1.0)\
                .then_inc(A.sem, A.step("fexp"))
            act.wait_ge(A.sem, A.at("fexp"))
            nc.scalar.activation(f[0:4, 2, :], f[0:4, 2, :], ACT.Ln, bias=eps[0:4, 3:4])\
                .then_inc(A.sem, A.step("fln"))
            nc.scalar.activation(f[0:4, 3, :], f[0:4, 0, :], ACT.Relu, scale=-1.0)\
                .then_inc(A.sem, A.step("frelu"))
            act.wait_ge(V.sem, V.at("nb"))
            for h in H4:
                for k, s_ in enumerate((slice(0, 128), slice(128, 384))):
                    q = 4 * k + h
                    nc.scalar.activation(fz["p"][:, h, s_], ps[:, 4 + h, s_], ACT.Exp,
                                                bias=st[:, F_NB + q:F_NB + q + 1],
                                                accum_out=st[:, F_RS + q:F_RS + q + 1])\
                        .then_inc(A.sem, A.step(f"x{2 * h + k}"))

        def attn_z_dve(dve):
            A, T, V = ST["a"], ST["t"], ST["v"]
            flat = "p a b -> p (a b)"
            L, f = fz["p"], fz["fs"]
            dve.wait_ge(SF["a"].sem, SF["a"].at("f4", RW_TILES - 1))
            nc.vector.tensor_scalar(zq_a, zq_a, SCALE_Z, None, ALU.mult)\
                .then_inc(V.sem, V.step("sq_a"))
            nc.vector.tensor_scalar(zq_b, zq_b, SCALE_Z, None, ALU.mult)\
                .then_inc(V.sem, V.step("sq_b"))
            dve.wait_ge(A.sem, A.at("relu"))
            nc.vector.scalar_tensor_tensor(out=L.rearrange(flat), in0=fz["q"].rearrange(flat), scalar=-1.0,
                                                  in1=u.rearrange(flat), op0=ALU.mult, op1=ALU.subtract)\
                .then_inc(V.sem, V.step("l"))
            dve.wait_ge(V.sem, V.at("l"))
            after = c("after").unsqueeze(1).to_broadcast([128, 4, 128])
            nc.vector.tensor_tensor(L[:, :, 0:128], L[:, :, 0:128], after, ALU.mult)\
                .then_inc(V.sem, V.step("m0"))
            nc.vector.tensor_tensor(L[:, :, 256:384], L[:, :, 256:384], after, ALU.mult)\
                .then_inc(V.sem, V.step("m1"))
            nc.vector.tensor_scalar(f[0:4, 0, :], fsm, p("bf", 0, 4), None, ALU.add)\
                .then_inc(V.sem, V.step("fb"))
            dve.wait_ge(A.sem, A.at("frelu"))
            nc.vector.scalar_tensor_tensor(out=f[0:4, 1, :], in0=f[0:4, 2, :], scalar=-1.0, in1=f[0:4, 3, :],
                                                  op0=ALU.mult, op1=ALU.subtract)\
                .then_inc(V.sem, V.step("fl"))
            dve.wait_ge(V.sem, V.at("fl"))
            nc.vector.tensor_tensor_scan(f[0:4, 0, :], c("ones", 4)[:, 0:1].to_broadcast([4, 256]),
                                                f[0:4, 1, :], 0.0, ALU.mult, ALU.add)\
                .then_inc(V.sem, V.step("cum"))
            dve.wait_ge(V.sem, V.at("cum"))
            nc.vector.tensor_scalar(f[0:4, 1, :], f[0:4, 0, :], -1.0, None, ALU.mult)\
                .then_inc(V.sem, V.step("ncum"))
            dve.wait_ge(T.sem, T.at("f"))
            nc.vector.tensor_reduce(st[:, F_MX:F_MX + 4], ps[:, 4:8, 0:128], AX.X, ALU.max)\
                .then_inc(V.sem, V.step("mx0"))
            nc.vector.tensor_reduce(st[:, F_MX + 4:F_MX + 8], ps[:, 4:8, 128:384], AX.X, ALU.max)\
                .then_inc(V.sem, V.step("mx1"))
            dve.wait_ge(V.sem, V.at("mx1"))
            nc.vector.tensor_scalar(st[:, F_NB:F_NB + 8], st[:, F_MX:F_MX + 8], -1.0, None, ALU.mult)\
                .then_inc(V.sem, V.step("nb"))
            dve.wait_ge(A.sem, A.at("x7"))
            nc.vector.reciprocal(st[:, F_RR:F_RR + 8], st[:, F_RS:F_RS + 8])\
                .then_inc(V.sem, V.step("rr"))
            dve.wait_ge(V.sem, V.at("rr"))
            for h in H4:
                for k, s_ in enumerate((slice(0, 128), slice(128, 384))):
                    q = 4 * k + h
                    w_ = fz["p"][:, h, s_]
                    nc.vector.tensor_scalar(w_, w_, st[:, F_RR + q:F_RR + q + 1], None, ALU.mult)\
                        .then_inc(V.sem, V.step(f"n{2 * h + k}"))
            dve.wait_ge(T.sem, T.at("wt"))
            nc.vector.tensor_copy(fz["q"], ps[:, 0:4, 0:384])\
                .then_inc(V.sem, V.step("wt"))
            dve.wait_ge(T.sem, T.at("yb"))
            nc.vector.tensor_copy(og[:, 4:8, 0:256], ps[:, 4:8, 0:256])\
                .then_inc(V.sem, V.step("yb"))

        SG = phase("gate_a", a="s0 s1 s2 s3")
        SM = phase("mix", a="sg0 sg1 sg2 sg3", v="ma0 mb0 mc0 s0 o0 ma1 mb1 mc1 s1 o1")
        split_y = Split("split_y", og, (gh, gl), SEQ)
        fm = carve([("pair", PAIR), ("sg", 4, 256), ("ta", 2, 256), ("tb", 2, 256), ("tc", 2, 256)])
        GATE_BANK = (2, 3, 0, 1)
        BANK = ((4, 5, 6), (7, 0, 1))

        def mix_pe(pe):
            A, V = SM["a"], SM["v"]
            pe.wait_ge(split_y.V.sem, split_y.V.at("l3"))

            def body(i):
                for t in range(4):
                    if t < 2:
                        if ran(i - 1):
                            pe.wait_ge(A.sem, A.at(f"sg{t}", i - 1))
                    else:
                        if ran(i - 1):
                            pe.wait_ge(V.sem, V.at(("mb1", "mc1")[t - 2], i - 1))
                    tile(pe, "mix", t, i, 6, [(ps[:, GATE_BANK[t], :], hh, hl, ALL)], SEQ).then_inc(tile_done, 1)
                for jj in range(2):
                    if jj:
                        pe.wait_ge(A.sem, A.at("sg3", i))
                    if ran(i - 1):
                        pe.wait_ge(V.sem, V.at(f"ma1" if jj else "mc0", i - 1))
                    tile(pe, "mix", 4 + jj, i, 6,
                         [(ps[:, BANK[jj][k], :], gh, gl, kts)
                          for k, kts in enumerate((range(0, 4), range(4, 8), range(8, 16)))], SEQ)\
                        .then_inc(tile_done, 1)
            repeat(pe, 8, body)

        def mix_act(act):
            act.wait_ge(SF["a"].sem, SF["a"].at("f4", RW_TILES - 1))
            for k in range(4):
                g_ = ga[:, 4 * k:4 * k + 4, :]
                nc.scalar.activation(g_, g_, ACT.Sigmoid)\
                    .then_inc(SG["a"].sem, SG["a"].step(f"s{k}"))

            def body(i):
                for t in range(4):
                    act.wait_ge(tile_done, done("mix", t, i, 6))
                    if ran(i - 1):
                        act.wait_ge(SM["v"].sem, SM["v"].at("mc1", i - 1))
                    nc.scalar.activation(fm["sg"][:, t, :], ps[:, GATE_BANK[t], 0:256], ACT.Sigmoid)\
                        .then_inc(SM["a"].sem, SM["a"].step(f"sg{t}"))
                    round_weights(act, "mix", t + 2, i, 6)
                round_weights(act, "mix", 6, i, 6)
                round_weights(act, "mix", 7, i, 6)
            repeat(act, 8, body)

        def mix_dve(dve):
            V = SM["v"]
            dve.wait_ge(SG["a"].sem, SG["a"].at("s3"))

            def body(i):
                for jj in range(2):
                    dve.wait_ge(tile_done, done("mix", 4 + jj, i, 6))
                    dve.wait_ge(SM["a"].sem, SM["a"].at("sg3", i))
                    for k, n in enumerate("abc"):
                        gate = ga[:, bass.ds(2 * i + jj, 1), :] if k == 0 else \
                            fm["sg"][:, 2 * (k - 1) + jj:2 * (k - 1) + jj + 1, :]
                        nc.vector.tensor_tensor(fm["t" + n][:, jj:jj + 1, :],
                                                ps[:, BANK[jj][k]:BANK[jj][k] + 1, 0:256], gate, ALU.mult)\
                            .then_inc(V.sem, V.step(f"m{n}{jj}"))
                    dve.wait_ge(V.sem, V.at(f"mc{jj}", i))
                    ta = fm["ta"][:, jj:jj + 1, :]
                    nc.vector.tensor_tensor(ta, ta, fm["tb"][:, jj:jj + 1, :], ALU.add)\
                        .then_inc(V.sem, V.step(f"s{jj}"))
                    dve.wait_ge(V.sem, V.at(f"s{jj}", i))
                    nc.vector.tensor_tensor(og[:, bass.ds(2 * i + jj, 1), 0:256], ta,
                                                   fm["tc"][:, jj:jj + 1, :], ALU.add)\
                        .then_inc(V.sem, V.step(f"o{jj}"))
            repeat(dve, 8, body)

        split_m = Split("split_m", og, (hh, hl), SEQ)
        mix_out = Product("mix_out", "mix_out", (hh, hl), SEQ, og, add=False, split=split_m)
        norm_post = Norm("norm_post", og, SEQ, 1, [("mix_post", og, None)], residual=xT,
                         written=mix_out.written(), after="mlp")
        split_mlp = Split("split_mlp", og, (hh, hl), SEQ)
        norm_mlp = Norm("norm_mlp", xT, SEQ, 1, [("mlp_pre", og, split_mlp)],
                        written=(norm_post.V, [norm_post.V.at(f"r{4 * k + 3}") for k in range(4)]))

        SU = phase("mlp", a=" ".join(f"relu{t} hi{t}" for t in range(16)),
                   v=" ".join(f"sq{t} lo{t}" for t in range(16)) + " " + " ".join(f"d{t}" for t in range(16)))
        fu = carve([("pair", PAIR), ("r", 4, 256), ("sq", 4, 256)])

        def mlp_pe(pe):
            A, V = SU["a"], SU["v"]

            def body(i):
                for t in range(16):
                    if t >= 4:
                        pe.wait_ge(A.sem, A.at(f"relu{t - 4}", i))
                    elif ran(i - 1):
                        pe.wait_ge(V.sem, V.at(f"d{t + 12}", i - 1))
                    tile(pe, "mlp", t, i, 32, [(ps[:, t % 4, :], hh, hl, ALL)], SEQ,
                         ready=first(i, t, split_mlp)).then_inc(tile_done, 1)
                pe.wait_ge(A.sem, A.at("hi11", i))
                pe.wait_ge(V.sem, V.at("lo11", i))
                for t in range(16):
                    if t >= 4:
                        pe.wait_ge(V.sem, V.at(f"d{t - 4}", i))
                    tile(pe, "mlp", 16 + t, i, 32, [(ps[:, t % 4, :], gh, gl, ALL)], SEQ,
                         late=() if t else ((A, A.at("hi15", i)), (V, V.at("lo15", i)))).then_inc(tile_done, 1)
            repeat(pe, 4, body)

        def mlp_act(act):
            A, V = SU["a"], SU["v"]

            def body(i):
                if ran(i - 1):
                    round_weights(act, "mlp", 0, i, 32)
                if ran(i - 1):
                    round_weights(act, "mlp", 1, i, 32)
                for t in range(16):
                    act.wait_ge(tile_done, done("mlp", t, i, 32))
                    if t >= 4:
                        act.wait_ge(V.sem, V.at(f"sq{t - 4}", i))
                    elif ran(i - 1):
                        act.wait_ge(V.sem, V.at(f"sq{t + 12}", i - 1))
                    nc.scalar.activation(fu["r"][:, t % 4, :], ps[:, t % 4, 0:256], ACT.Relu)\
                        .then_inc(A.sem, A.step(f"relu{t}"))
                    act.wait_ge(A.sem, A.at(f"relu{t}", i))
                    nc.scalar.activation(gh[:, t, :], fu["r"][:, t % 4, :], ACT.Square)\
                        .then_inc(A.sem, A.step(f"hi{t}"))
                    round_weights(act, "mlp", t + 2, i, 32)
                for t in range(14):
                    round_weights(act, "mlp", t + 18, i, 32)
            repeat(act, 4, body)

        def mlp_dve(dve):
            A, V = SU["a"], SU["v"]

            def body(i):
                for t in range(16):
                    dve.wait_ge(A.sem, A.at(f"relu{t}", i))
                    sq, r_ = fu["sq"][:, t % 4, :], fu["r"][:, t % 4, :]
                    nc.vector.tensor_tensor(sq, r_, r_, ALU.mult)\
                        .then_inc(V.sem, V.step(f"sq{t}"))
                    dve.wait_ge(A.sem, A.at(f"hi{t}", i))
                    dve.wait_ge(V.sem, V.at(f"sq{t}", i))
                    nc.vector.tensor_tensor(gl[:, t, :], sq, gh[:, t, :].bitcast(F32), ALU.subtract)\
                        .then_inc(V.sem, V.step(f"lo{t}"))
                for t in range(16):
                    dve.wait_ge(tile_done, done("mlp", 16 + t, i, 32))
                    if ran(i - 1):
                        nc.vector.tensor_tensor(og[:, t, 0:256], ps[:, t % 4, 0:256], og[:, t, 0:256], ALU.add)\
                            .then_inc(V.sem, V.step(f"d{t}"))
                    else:
                        nc.vector.tensor_copy(og[:, t, 0:256], ps[:, t % 4, 0:256])\
                            .then_inc(V.sem, V.step(f"d{t}"))
            repeat(dve, 4, body)

        norm_out = Norm("norm_out", og, SEQ, 1, [("mlp_post", og, None)], residual=xT,
                        written=(SU["v"], [SU["v"].at(f"d{4 * k + 3}", 3) for k in range(4)]))

        block = ctx.enter_context(nc.Block())

        @block.sync
        def _(sp):
            sp.dma_start(xT[:, :, :], x).then_inc(x_in, 16)
            sp.dma_start(C[:, :], consts).then_inc(cp_in, 16)
            sp.dma_start(P[:, :], params).then_inc(cp_in, 16)
            for s in range(4):
                sp.dma_start(raw[:, s, :, :].rearrange("p a b -> p (a b)"), w[:, s, :])\
                    .then_inc(raw_in[s // 2], 16)

            def load(n, slot):
                sp.dma_start(raw[:, slot, :, :].rearrange("p a b -> p (a b)").unsqueeze(1),
                             w[:, bass.ds(n, 1), :]).then_inc(raw_in[slot // 2], 16)
            with sp.Fori(1, N_TILES // 2) as i:
                for s in range(4):
                    sp.wait_ge(lo_done, 4 * i + s - 3)
                    load(4 * i + s, s)
            sp.wait_ge(norm_out.V.sem, norm_out.V.at(norm_out.last))
            sp.dma_start(out, xT[:, :, 0:SEQ]).then_inc(out_in, 16)
            sp.wait_ge(out_in, 16)

        @block.scalar
        def _(act):
            lam_act(act)
            act.wait_ge(x_in, 16)
            norm_a.act(act)
            attn_a_act(act)
            split_ao.act(act, SA["v"], [SA["v"].at(f"og1", h) for h in (1, 3, 5, 7)])
            a_out.act(act)
            norm_b.act(act)
            kv_act(act)
            attn_b_act(act)
            split_bo.act(act, SB["v"], [SB["v"].at("o3", g) for g in range(4)])
            b_out.act(act)
            norm_fin.act(act)
            norm_mix.act(act)
            rw_in_act(act)
            rwkv_act(act)
            attn_z_act(act)
            split_y.act(act, ST["v"], [ST["v"].at("yb")] * 4)
            mix_act(act)
            split_m.act(act, SM["v"], [SM["v"].at("o1", g) for g in (1, 3, 5, 7)])
            mix_out.act(act)
            norm_post.act(act)
            norm_mlp.act(act)
            mlp_act(act)
            norm_out.act(act)

        @block.vector
        def _(dve):
            for k, value in enumerate((1e-5, 1e-6, 64e-5, 1.0)):
                nc.vector.memset(eps[:, k:k + 1], value).then_inc(eps_set, 1)
            nc.vector.memset(st[:, :], 1.0).then_inc(eps_set, 1)
            dve.wait_ge(eps_set, 5)
            dve.wait_ge(cp_in, 32)
            lam_dve(dve)
            norm_a.dve(dve)
            attn_a_dve(dve)
            split_ao.dve(dve)
            a_out.dve(dve)
            dve.wait_ge(a_out.V.sem, a_out.V.at("t7", 1))
            norm_b.dve(dve)
            kv_dve(dve)
            attn_b_dve(dve)
            split_bo.dve(dve)
            b_out.dve(dve)
            dve.wait_ge(b_out.V.sem, b_out.V.at("t7", 1))
            norm_fin.dve(dve)
            dve.wait_ge(norm_fin.V.sem, norm_fin.V.at(norm_fin.last))
            norm_mix.dve(dve)
            rw_in_dve(dve)
            rwkv_dve(dve)
            attn_z_dve(dve)
            split_y.dve(dve)
            mix_dve(dve)
            split_m.dve(dve)
            mix_out.dve(dve)
            dve.wait_ge(mix_out.V.sem, mix_out.V.at("t7", 1))
            norm_post.dve(dve)
            dve.wait_ge(norm_post.V.sem, norm_post.V.at(norm_post.last))
            norm_mlp.dve(dve)
            mlp_dve(dve)
            dve.wait_ge(SU["v"].sem, SU["v"].at("d15", 3))
            norm_out.dve(dve)

        @block.tensor
        def _(pe):
            pe.wait_ge(cp_in, 32)
            lam_pe(pe)
            norm_a.pe(pe)
            attn_a_pe(pe)
            a_out.pe(pe)
            norm_b.pe(pe)
            kv_pe(pe)
            attn_b_pe(pe)
            b_out.pe(pe)
            norm_fin.pe(pe)
            norm_mix.pe(pe)
            rw_in_pe(pe)
            rwkv_pe(pe)
            attn_z_pe(pe)
            mix_pe(pe)
            mix_out.pe(pe)
            norm_post.pe(pe)
            norm_mlp.pe(pe)
            mlp_pe(pe)
            norm_out.pe(pe)

        @block.gpsimd
        def _(pool):
            def rest(i, s):
                if s % 2 == 0:
                    pool.wait_ge(hi_done, 2 * i + s // 2 + 1)
                h = slice(8 * (s % 2), 8 * (s % 2) + 8)
                nc.gpsimd.tensor_tensor(wl[:, s // 2, h, :], raw[:, s, :, :],
                                        wh[:, s // 2, h, :].bitcast(F32), ALU.subtract)\
                    .then_inc(lo_done, 1)
            with pool.Fori(0, N_TILES // 2) as i:
                for s in range(4):
                    rest(i, s)


def constants():
    q = np.arange(128)
    same = (q[:, None] // 64) == (q[None, :] // 64)
    col, row = q[None, :], q[:, None]
    t = {
        "ident": np.eye(128), "ones": np.ones((128, 128)), "hones": same, "tri": row >= col,
        "after": col > row, "not_after": np.where(col <= row, NEG, 0), "future": np.where(col > row, NEG, 0),
        "strict": same & (row < col), "incl": same & (row <= col),
    }
    for b in LEVELS:
        t[f"lev{b}"] = (row // (2 * b) == col // (2 * b)) & ((row // b) % 2 == 0) & ((col // b) % 2 == 1)
    t["lev1t"] = t["lev1"].T
    t["reset"] = np.broadcast_to(np.arange(256) % 64 != 0, (128, 256))
    pos = np.concatenate([np.arange(SEQ) + META, np.arange(META)]).astype(np.float32)
    for name, dim in (("a", 32), ("b", 16)):
        inv = np.float32(ROPE_THETA) ** (-np.arange(0, dim, 2, dtype=np.float32) / np.float32(dim))
        ang = (pos[None, :] * inv[:, None]).astype(np.float32)
        cos, sin = np.ones((128, NT)), np.zeros((128, NT))
        for r in range(0, 128, 64 if name == "b" else 128):
            half = dim // 2
            cos[r:r + half] = cos[r + half:r + dim] = np.cos(ang)
            sin[r:r + half], sin[r + half:r + dim] = -np.sin(ang), np.sin(ang)
        t[f"cos_{name}"], t[f"sin_{name}"] = cos, sin
    t["low"] = np.broadcast_to(q < 64, (128, 128))
    t["high"] = np.broadcast_to(q >= 64, (128, 128))
    t["neg"] = np.full((128, 64), NEG)
    t["sel"] = np.repeat(np.eye(128)[:, 0:4], 128, axis=1)
    c = np.zeros((128, C_N), np.float32)
    for name, (a, b) in C_AT.items():
        c[:, a:b] = t[name]
    return c


def lay_out(w):
    tiles = np.zeros((128, N_TILES, TILE), np.float32)
    n = 0

    def put(m):
        nonlocal n
        for k in range(0, m.shape[1], 128):
            cols = m[:, k:k + 128]
            c = cols.shape[1]
            tiles[:, n].reshape(128, 16, 128)[:, :, 0:c] = cols.reshape(16, 128, c).transpose(1, 0, 2)
            n += 1

    a, b, z = w["a_w_in"][0], w["b_w_in"][0], w["w_in_2"][0]
    for h in range(HEADS_A):
        for part in range(4):
            put(a[:, D * part + 256 * h:D * part + 256 * h + 256])
    for g in range(8):
        put(w["a_w_out"][0][:, 256 * g:256 * g + 256])
    for g in range(2):
        put(w["w_kv"][:, 256 * g:256 * g + 256])
    put(b[:, 0:512])
    for g in range(GROUPS_B):
        for j in range(4):
            c = 512 * g + 128 * j
            put(b[:, D + c:D + c + 128])
            if g < GROUPS_B - 1:
                put(b[:, c + 512:c + 640])
    for g in range(8):
        put(w["b_w_out"][0][:, 256 * g:256 * g + 256])
    wa, gates = IN_R + 3072, IN_R + 3072 + 288

    def put_rkv(j):
        for q in range(3):
            c = IN_R + 1024 * q + 128 * j
            put(z[:, c:c + 128])
    put_rkv(0)
    put(z[:, wa:wa + 128])
    put(z[:, 3072:3076])
    put(z[:, wa + 128:wa + 288])
    for j in range(RW_TILES):
        for q in range(3):
            c = 128 * (j + 8 * q)
            put(z[:, c:c + 128])
        put(z[:, gates + 256 * j:gates + 256 * j + 256])
        if j < RW_TILES - 1:
            put_rkv(j + 1)
    lora = np.zeros((128, 3072), np.float32)
    lora[0:64, 0:1024] = w["rwkv_w_up_2"][0]
    lora[64:128, 0:1024] = w["rwkv_a_up_2"][0]
    lora[:, 1024:2048] = w["rwkv_g_up_2"][0][0:128]
    lora[0:32, 2048:3072] = w["rwkv_g_up_2"][0][128:160]
    for g in range(8):
        for part in (1, 2):
            c = gates + D * part + 256 * g
            put(z[:, c:c + 256])
        put(np.concatenate([w[f"w_branch_{k}_2"][0][:, 256 * g:256 * g + 256] for k in "abc"]))
    for g in range(8):
        put(w["w_out_2"][0][:, 256 * g:256 * g + 256])
    for b_ in range(4):
        f = slice(2048 * b_, 2048 * b_ + 2048)
        put(w["w_mlp_up_2"][0][:, f])
        put(w["w_mlp_down_2"][0][f, :])
    assert n == N_TILES, (n, N_TILES)

    p = np.zeros((128, P_N), np.float32)

    def cols(name, v, k=0):
        v = np.asarray(v).reshape(-1)
        rows = min(128, len(v))
        v = v.reshape(-1, rows).T
        p[0:rows, P_AT[name][0] + k:P_AT[name][0] + k + v.shape[1]] = v

    for name, key in (("a", "a_norm"), ("kv", "kv_norm"), ("b", "b_norm"), ("fin", "final_norm"),
                      ("mix_pre", "norm_mix_pre_2"), ("mix_post", "norm_mix_post_2"),
                      ("mlp_pre", "norm_mlp_pre_2"), ("mlp_post", "norm_mlp_post_2")):
        cols(name, w[key])
    for k, key in enumerate(("q1", "k1", "q2", "k2")):
        cols("lam", w["a_lambda_" + key], k)
    cols("subln", w["a_subln"])
    p[:, P_AT["sinks"][0]:P_AT["sinks"][1]] = w["b_sinks"].reshape(1, -1)
    mu = w["rwkv_mu_2"][0]
    cols("mu_wa", mu[3072:3200])
    cols("mu_g", mu[3200:3328])
    cols("mu_g", mu[3328:3360], 1)
    cols("bf", w["b_forget_2"])
    for j in range(RW_TILES):
        f = slice(128 * j, 128 * j + 128)
        parts = [mu[0:1024], mu[1024:2048], mu[2048:3072]] + [
            w[f"rwkv_{k}_2"].reshape(-1) for k in ("w0", "a0", "k_k", "k_a", "r_k", "ln_w", "ln_b")]
        for k, v in enumerate(parts):
            cols("rw", v[f], 10 * j + k)
    lora = np.ascontiguousarray(lora.reshape(128, 3, RW_TILES, 128).transpose(0, 2, 1, 3)).reshape(128, RW_TILES, 384)
    return tiles.reshape(128, 2 * N_TILES, TILE // 2), lora, p


def kernel(**inputs):
    import concourse.bacc as _bacc
    from concourse.bass_utils import run_bass_kernel_spmd as _run

    w = {k: np.asarray(v) for k, v in inputs.items()}
    tiles, lora, p = lay_out(w)
    x = np.concatenate([w["x"][0], w["meta_tokens"]]).T.reshape(KT, 128, NT).transpose(1, 0, 2)
    arrays = {"weights": tiles, "tokens": np.ascontiguousarray(x), "params": p, "consts": constants(),
              "lora": lora}
    nc = _bacc.Bacc("TRN2", target_bir_lowering=False, num_devices=1)
    args = [nc.dram_tensor(n, a.shape, F32, kind="ExternalInput").ap() for n, a in arrays.items()]
    out = nc.dram_tensor("out", [128, KT, SEQ], F32, kind="ExternalOutput").ap()
    build(nc, *args, out)
    r = _run(nc, [arrays], core_ids=[0]).results[0]["out"]
    return np.ascontiguousarray(r.transpose(2, 1, 0)).reshape(1, SEQ, D)
```
